# Optimizing a Trainium2 kernel written in Bass

```python
import jax, jax.numpy as jnp
from jax import lax
import numpy as np

D_MODEL = 1024
BATCH = 1
SEQ = 512
DEPTH = 2

CTX_LEN = 256
GRID_W = 64

FOURIER_WIDTH = D_MODEL // 4
N_FOURIER_HEADS = 4
FOURIER_HEAD_DIM = FOURIER_WIDTH // N_FOURIER_HEADS

V_HEAD_DIM = 64
QK_NOPE_DIM = 64
QK_ROPE_DIM = 32
QK_HEAD_DIM = QK_NOPE_DIM + QK_ROPE_DIM
N_MLA_HEADS = (D_MODEL - FOURIER_WIDTH) // V_HEAD_DIM
MLA_WIDTH = N_MLA_HEADS * V_HEAD_DIM
Q_LORA_RANK = 384
KV_LORA_RANK = 128

MIX_WIDTH = FOURIER_WIDTH + MLA_WIDTH
IN_PROJ_WIDTH = FOURIER_WIDTH + Q_LORA_RANK + KV_LORA_RANK + QK_ROPE_DIM

D_FF = 2816
CONV_WIDTH = 3

ROPE_THETA = 10000.0
NORM_EPS = 1e-6
Q_BLOCK = 128
SOFTMAX_SCALE = QK_HEAD_DIM ** -0.5
N_MOD = 6


def rms_norm(x, g):
    xf = x.astype(jnp.float32)
    y = xf * lax.rsqrt(jnp.mean(xf * xf, axis=-1, keepdims=True) + NORM_EPS)
    return (y * g.astype(jnp.float32)).astype(x.dtype)

def modulate(h, shift, scale):
    return h * (1 + scale) + shift

def axial_rope_tables(rows, dtype):
    row_ids = jnp.broadcast_to(jnp.arange(rows)[:, None], (rows, GRID_W)).reshape(-1).astype(jnp.float32)
    col_ids = jnp.broadcast_to(jnp.arange(GRID_W)[None, :], (rows, GRID_W)).reshape(-1).astype(jnp.float32)
    n_freq = QK_ROPE_DIM // 4
    inv_freq = ROPE_THETA ** (-jnp.arange(n_freq, dtype=jnp.float32) / n_freq)
    ang = jnp.concatenate([row_ids[:, None] * inv_freq, col_ids[:, None] * inv_freq], axis=-1)
    return jnp.cos(ang).astype(dtype), jnp.sin(ang).astype(dtype)

def apply_rope(x, cos, sin):
    x1, x2 = jnp.split(x, 2, axis=-1)
    return jnp.concatenate([x1 * cos - x2 * sin, x2 * cos + x1 * sin], axis=-1)

def fourier_mix(u, w_f, b_f):
    b, n, _ = u.shape
    uh = u.reshape(b, n, N_FOURIER_HEADS, FOURIER_HEAD_DIM).astype(jnp.float32)
    f = jnp.fft.fft2(uh, axes=(1, 3), norm="ortho").real
    f = f.reshape(b, n, FOURIER_WIDTH).astype(u.dtype)
    return f @ w_f + b_f

def mla_q(c_q, g_q, w_q_b, cos, sin):
    b, n, _ = c_q.shape
    q = (rms_norm(c_q, g_q) @ w_q_b).reshape(b, n, N_MLA_HEADS, QK_HEAD_DIM)
    q_nope, q_rope = q[..., :QK_NOPE_DIM], q[..., QK_NOPE_DIM:]
    if cos is not None:
        q_rope = apply_rope(q_rope, cos[:, None, :], sin[:, None, :])
    return q_nope, q_rope

def mla_kv(c_kv, k_rope, g_kv, w_kv_b, cos, sin):
    b, n, _ = c_kv.shape
    kv = (rms_norm(c_kv, g_kv) @ w_kv_b).reshape(b, n, N_MLA_HEADS, QK_NOPE_DIM + V_HEAD_DIM)
    k_nope, v = kv[..., :QK_NOPE_DIM], kv[..., QK_NOPE_DIM:]
    if cos is not None:
        k_rope = apply_rope(k_rope, cos, sin)
    return k_nope, k_rope, v

def mla_attend(q_nope, q_rope, k_nope, k_rope, v):
    s = jnp.einsum('bqhd,bkhd->bhqk', q_nope, k_nope) + jnp.einsum('bqhr,bkr->bhqk', q_rope, k_rope)
    p = jax.nn.softmax(s.astype(jnp.float32) * SOFTMAX_SCALE, axis=-1).astype(v.dtype)
    return jnp.einsum('bhqk,bkhd->bqhd', p, v)

def blocked_attention(q_nope, q_rope, k_nope, k_rope, v):
    b, n, h, _ = q_nope.shape
    nb = n // Q_BLOCK
    qn = q_nope.reshape(b, nb, Q_BLOCK, h, QK_NOPE_DIM).transpose(1, 0, 2, 3, 4)
    qr = q_rope.reshape(b, nb, Q_BLOCK, h, QK_ROPE_DIM).transpose(1, 0, 2, 3, 4)
    out = lax.map(lambda blk: mla_attend(blk[0], blk[1], k_nope, k_rope, v), (qn, qr))
    return out.transpose(1, 0, 2, 3, 4).reshape(b, n, h * V_HEAD_DIM)

def split_in_proj(p):
    f_in = p[..., :FOURIER_WIDTH]
    c_q = p[..., FOURIER_WIDTH:FOURIER_WIDTH + Q_LORA_RANK]
    c_kv = p[..., FOURIER_WIDTH + Q_LORA_RANK:FOURIER_WIDTH + Q_LORA_RANK + KV_LORA_RANK]
    k_rope = p[..., FOURIER_WIDTH + Q_LORA_RANK + KV_LORA_RANK:]
    return f_in, c_q, c_kv, k_rope

def conv_ffn(h, w_up, w_dw, b_dw, w_down):
    u = h @ w_up
    u = lax.conv_general_dilated(u, w_dw[:, None, :], window_strides=(1,),
                                 padding=((CONV_WIDTH // 2, CONV_WIDTH // 2),),
                                 dimension_numbers=('NWC', 'WIO', 'NWC'),
                                 feature_group_count=2 * D_FF) + b_dw
    gate, val = jnp.split(u, 2, axis=-1)
    return (jax.nn.silu(gate) * val) @ w_down

def first_inputs(seed: int = 0) -> dict:
    key = jax.random.key(seed)
    ks = jax.random.split(key, 24)
    f32 = jnp.float32

    def nrm(k, shape, scale):
        return jax.random.normal(k, shape, f32) * scale

    def gain(k, shape):
        return 1.0 + 0.02 * jax.random.normal(k, shape, f32)

    L, D = DEPTH, D_MODEL
    return {
        "x": jax.random.normal(ks[0], (BATCH, SEQ, D), f32),
        "c": jax.random.normal(ks[1], (BATCH, D), f32),
        "ctx": jax.random.normal(ks[2], (BATCH, CTX_LEN, D), f32),
        "c_ctx": jax.random.normal(ks[3], (D,), f32),
        "w_ada": nrm(ks[4], (L, D, N_MOD * D), 0.5 * D ** -0.5),
        "b_ada": nrm(ks[5], (L, N_MOD * D), 0.02),
        "g_mix": gain(ks[6], (L, D)),
        "w_in": nrm(ks[7], (L, D, IN_PROJ_WIDTH), D ** -0.5),
        "w_fourier": nrm(ks[8], (L, FOURIER_WIDTH, FOURIER_WIDTH), FOURIER_WIDTH ** -0.5),
        "b_fourier": nrm(ks[9], (L, FOURIER_WIDTH), 0.02),
        "g_q_a": gain(ks[10], (L, Q_LORA_RANK)),
        "w_q_b": nrm(ks[11], (L, Q_LORA_RANK, N_MLA_HEADS * QK_HEAD_DIM), Q_LORA_RANK ** -0.5),
        "g_kv_a": gain(ks[12], (L, KV_LORA_RANK)),
        "w_kv_b": nrm(ks[13], (L, KV_LORA_RANK, N_MLA_HEADS * (QK_NOPE_DIM + V_HEAD_DIM)), KV_LORA_RANK ** -0.5),
        "w_out": nrm(ks[14], (L, MIX_WIDTH, D), MIX_WIDTH ** -0.5),
        "g_ffn": gain(ks[15], (L, D)),
        "w_up": nrm(ks[16], (L, D, 2 * D_FF), D ** -0.5),
        "w_dw": nrm(ks[17], (L, CONV_WIDTH, 2 * D_FF), CONV_WIDTH ** -0.5),
        "b_dw": nrm(ks[18], (L, 2 * D_FF), 0.02),
        "w_down": nrm(ks[19], (L, D_FF, D), D_FF ** -0.5),
        "g_final": gain(ks[20], (D,)),
    }

def first_block(x, c, ctx, c_ctx, w_ada, b_ada, g_mix, w_in, w_fourier, b_fourier,
              g_q_a, w_q_b, g_kv_a, w_kv_b, w_out, g_ffn, w_up, w_dw, b_dw, w_down, g_final):
    b, n_lat, _ = x.shape
    ROWS = n_lat // GRID_W
    cos, sin = axial_rope_tables(ROWS, x.dtype)
    silu_c = jax.nn.silu(c)
    silu_cc = jax.nn.silu(c_ctx)

    for l in range(DEPTH):
        last = l == DEPTH - 1
        mod_lat = (silu_c @ w_ada[l] + b_ada[l])[:, None, :]
        mod_ctx = silu_cc @ w_ada[l] + b_ada[l]
        sh1, sc1, gt1, sh2, sc2, gt2 = jnp.split(mod_lat, N_MOD, axis=-1)
        csh1, csc1, cgt1, csh2, csc2, cgt2 = jnp.split(mod_ctx, N_MOD, axis=-1)

        h = modulate(rms_norm(x, g_mix[l]), sh1, sc1)
        hc = modulate(rms_norm(ctx, g_mix[l]), csh1, csc1)
        f_in, c_q, c_kv, k_rope_raw = split_in_proj(h @ w_in[l])
        f_in_c, c_q_c, c_kv_c, k_rope_raw_c = split_in_proj(hc @ w_in[l])

        kn_c, kr_c, v_c = mla_kv(c_kv_c, k_rope_raw_c, g_kv_a[l], w_kv_b[l], None, None)
        kn_l, kr_l, v_l = mla_kv(c_kv, k_rope_raw, g_kv_a[l], w_kv_b[l], cos, sin)
        qn_l, qr_l = mla_q(c_q, g_q_a[l], w_q_b[l], cos, sin)

        k_nope_all = jnp.concatenate([kn_l, kn_c], axis=1)
        k_rope_all = jnp.concatenate([kr_l, kr_c], axis=1)
        v_all = jnp.concatenate([v_l, v_c], axis=1)
        att_l = blocked_attention(qn_l, qr_l, k_nope_all, k_rope_all, v_all)
        four_l = fourier_mix(f_in, w_fourier[l], b_fourier[l])
        mix_l = jnp.concatenate([four_l, att_l], axis=-1) @ w_out[l]
        x = x + gt1 * mix_l

        x = x + gt2 * conv_ffn(modulate(rms_norm(x, g_ffn[l]), sh2, sc2),
                               w_up[l], w_dw[l], b_dw[l], w_down[l])

        if not last:
            qn_c, qr_c = mla_q(c_q_c, g_q_a[l], w_q_b[l], None, None)
            att_c = mla_attend(qn_c, qr_c, kn_c, kr_c, v_c).reshape(b, -1, MLA_WIDTH)
            four_c = fourier_mix(f_in_c, w_fourier[l], b_fourier[l])
            mix_c = jnp.concatenate([four_c, att_c], axis=-1) @ w_out[l]
            ctx = ctx + cgt1 * mix_c
            ctx = ctx + cgt2 * conv_ffn(modulate(rms_norm(ctx, g_ffn[l]), csh2, csc2),
                                        w_up[l], w_dw[l], b_dw[l], w_down[l])

    return rms_norm(x, g_final)


A_HEADS = 4
A_DK = 128
A_DV = 128
CONV_K = 4
B_HEADS = 4
B_DK = 128
B_DV = 128
CHUNK = 64
C_HEADS = 16
C_KV_HEADS = 4
C_GROUP = C_HEADS // C_KV_HEADS
C_HD = 64
WINDOW = 128
D_FF_2 = 4 * D_MODEL
PLE_DIM = 256
EPS = 1e-6
N_EVEN = (DEPTH + 1) // 2
N_ODD = DEPTH // 2

A_QK = A_HEADS * A_DK
A_V = A_HEADS * A_DV
B_QK = B_HEADS * B_DK
B_V = B_HEADS * B_DV
A_CONV_CH = 2 * A_QK + A_V
A_COLS = 2 * A_QK + A_V + 2 * A_HEADS + A_V
B_COLS = 2 * B_QK + B_V + 2 * B_HEADS + B_V
IN_COLS = A_COLS + B_COLS
MIX_AB = A_V + B_V
C_Q = C_HEADS * C_HD
C_KV = C_KV_HEADS * C_HD
C_COLS = C_Q + 2 * C_KV


F32 = jnp.float32

def rmsnorm(x, g):
    xf = x.astype(F32)
    y = xf * lax.rsqrt(jnp.mean(xf * xf, -1, keepdims=True) + EPS)
    return (y * g.astype(F32)).astype(x.dtype)

def l2norm(x):
    return x * lax.rsqrt(jnp.sum(x * x, -1, keepdims=True) + EPS)

def causal_conv(x, w):
    k_taps = w.shape[0]
    s = x.shape[1]
    xp = jnp.pad(x, ((0, 0), (k_taps - 1, 0), (0, 0)))
    return sum(xp[:, k:k + s] * w[k] for k in range(k_taps))

def to_chunks(x):
    b, s, h = x.shape[:3]
    x = x.reshape((b, s // CHUNK, CHUNK, h) + x.shape[3:])
    return jnp.moveaxis(x, (1, 3), (0, 2))

def from_chunks(x):
    x = jnp.moveaxis(x, (0, 2), (1, 3))
    b, n, c, h, d = x.shape
    return x.reshape(b, n * c, h, d)

def gated_delta_rule(q, k, v, g, beta):
    b, s, h, dk = q.shape
    dv = v.shape[-1]
    qc, kc, vc = to_chunks(q), to_chunks(k), to_chunks(v)
    gcum = jnp.cumsum(to_chunks(g), -1)
    bc = to_chunks(beta)
    causal = jnp.tril(jnp.ones((CHUNK, CHUNK), bool))
    strict = jnp.tril(jnp.ones((CHUNK, CHUNK), bool), -1)
    diff = gcum[..., :, None] - gcum[..., None, :]
    decay = jnp.where(causal, jnp.exp(jnp.where(causal, diff, 0.0)), 0.0)
    kb = kc * bc[..., None]
    vb = vc * bc[..., None]
    lmat = jnp.where(strict, jnp.einsum('nbhcd,nbhed->nbhce', kb, kc) * decay, 0.0)
    eye = jnp.eye(CHUNK, dtype=lmat.dtype)
    rhs = jnp.concatenate([vb, kb * jnp.exp(gcum)[..., None]], -1)
    uw = lax.linalg.triangular_solve(lmat + eye, rhs, left_side=True, lower=True,
                                     unit_diagonal=True)
    u, w = uw[..., :dv], uw[..., dv:]
    attn_intra = jnp.einsum('nbhcd,nbhed->nbhce', qc, kc) * decay
    q_dec = qc * jnp.exp(gcum)[..., None]
    g_last = gcum[..., -1]
    k_dec = kc * jnp.exp(g_last[..., None] - gcum)[..., None]

    def step(state, xs):
        u_, w_, a_, qd, kd, gl = xs
        v_new = u_ - jnp.einsum('bhcd,bhde->bhce', w_, state)
        o = (jnp.einsum('bhcd,bhde->bhce', qd, state)
             + jnp.einsum('bhcs,bhse->bhce', a_, v_new))
        state = (state * jnp.exp(gl)[..., None, None]
                 + jnp.einsum('bhcd,bhce->bhde', kd, v_new))
        return state, o

    s0 = jnp.zeros((b, h, dk, dv), F32)
    _, o = lax.scan(step, s0, (u, w, attn_intra, q_dec, k_dec, g_last))
    return from_chunks(o)

def mlstm_chunkwise(q, k, v, i_log, f_log):
    b, s, h, dk = q.shape
    dv = v.shape[-1]
    qc, kc, vc = to_chunks(q), to_chunks(k), to_chunks(v)
    ic = to_chunks(i_log)
    bcum = jnp.cumsum(to_chunks(f_log), -1)
    causal = jnp.tril(jnp.ones((CHUNK, CHUNK), bool))
    dmat = bcum[..., :, None] - bcum[..., None, :] + ic[..., None, :]
    dmat = jnp.where(causal, dmat, -jnp.inf)
    m_intra = jnp.max(dmat, -1)
    b_last = bcum[..., -1]
    w_state = b_last[..., None] - bcum + ic
    qk = jnp.einsum('nbhtd,nbhsd->nbhts', qc, kc)

    def step(carry, xs):
        c_st, n_st, m = carry
        q_, k_, v_, qk_, d_, mi, bc_, ws, bl = xs
        a = bc_ + m[..., None]
        mt = jnp.maximum(a, mi)
        inter = jnp.exp(a - mt)
        pmat = qk_ * jnp.exp(d_ - mt[..., None])
        num = (inter[..., None] * jnp.einsum('bhcd,bhde->bhce', q_, c_st)
               + jnp.einsum('bhts,bhse->bhte', pmat, v_))
        den = inter * jnp.einsum('bhcd,bhd->bhc', q_, n_st) + jnp.sum(pmat, -1)
        hout = num / jnp.maximum(jnp.abs(den), jnp.exp(-mt))[..., None]
        m_new = jnp.maximum(bl + m, jnp.max(ws, -1))
        sc = jnp.exp(bl + m - m_new)
        kw = k_ * jnp.exp(ws - m_new[..., None])[..., None]
        c_st = sc[..., None, None] * c_st + jnp.einsum('bhcd,bhce->bhde', kw, v_)
        n_st = sc[..., None] * n_st + jnp.sum(kw, -2)
        return (c_st, n_st, m_new), hout

    carry0 = (jnp.zeros((b, h, dk, dv), F32), jnp.zeros((b, h, dk), F32), jnp.zeros((b, h), F32))
    _, o = lax.scan(step, carry0, (qc, kc, vc, qk, dmat, m_intra, bcum, w_state, b_last))
    return from_chunks(o)

def mixer_ab(hn, w_in, conv_w, a_log, dt_bias, norm_a, i_bias, f_bias, norm_b, w_out):
    b, s, _ = hn.shape
    proj = hn @ w_in
    pa, pb = proj[..., :A_COLS], proj[..., A_COLS:]
    qkv = jax.nn.silu(causal_conv(pa[..., :A_CONV_CH], conv_w)).astype(F32)
    qa = l2norm(qkv[..., :A_QK].reshape(b, s, A_HEADS, A_DK)) * (A_DK ** -0.5)
    ka = l2norm(qkv[..., A_QK:2 * A_QK].reshape(b, s, A_HEADS, A_DK))
    va = qkv[..., 2 * A_QK:].reshape(b, s, A_HEADS, A_DV)
    off = A_CONV_CH
    beta = jax.nn.sigmoid(pa[..., off:off + A_HEADS].astype(F32))
    alpha_pre = pa[..., off + A_HEADS:off + 2 * A_HEADS].astype(F32) + dt_bias.astype(F32)
    g = -jnp.exp(a_log.astype(F32)) * jax.nn.softplus(alpha_pre)
    z = pa[..., off + 2 * A_HEADS:].astype(F32).reshape(b, s, A_HEADS, A_DV)
    oa = gated_delta_rule(qa, ka, va, g, beta)
    oa = rmsnorm(oa, norm_a) * jax.nn.silu(z)
    pbf = pb.astype(F32)
    qb = pbf[..., :B_QK].reshape(b, s, B_HEADS, B_DK) * (B_DK ** -0.5)
    kb = pbf[..., B_QK:2 * B_QK].reshape(b, s, B_HEADS, B_DK)
    vb = pbf[..., 2 * B_QK:2 * B_QK + B_V].reshape(b, s, B_HEADS, B_DV)
    off = 2 * B_QK + B_V
    i_log = pbf[..., off:off + B_HEADS] + i_bias.astype(F32)
    f_log = jax.nn.log_sigmoid(pbf[..., off + B_HEADS:off + 2 * B_HEADS] + f_bias.astype(F32))
    o_gate = jax.nn.sigmoid(pbf[..., off + 2 * B_HEADS:]).reshape(b, s, B_HEADS, B_DV)
    ob = mlstm_chunkwise(qb, kb, vb, i_log, f_log)
    ob = rmsnorm(ob, norm_b) * o_gate
    mixed = jnp.concatenate([oa.reshape(b, s, A_V), ob.reshape(b, s, B_V)], -1)
    return mixed.astype(hn.dtype) @ w_out

def rope(x, pos):
    half = x.shape[-1] // 2
    inv = ROPE_THETA ** (-jnp.arange(half, dtype=F32) / half)
    ang = pos.astype(F32)[..., None] * inv
    cos = jnp.cos(ang)[:, :, None, :]
    sin = jnp.sin(ang)[:, :, None, :]
    x1, x2 = x[..., :half], x[..., half:]
    return jnp.concatenate([x1 * cos - x2 * sin, x2 * cos + x1 * sin], -1)

def mixer_c(hn, pos, w_qkv, b_qkv, sinks, w_o, b_o):
    b, s, _ = hn.shape
    nb = s // WINDOW
    proj = (hn @ w_qkv + b_qkv).astype(F32)
    q = rope(proj[..., :C_Q].reshape(b, s, C_HEADS, C_HD), pos)
    q = q.reshape(b, nb, WINDOW, C_KV_HEADS, C_GROUP, C_HD)
    q = jnp.moveaxis(q, 1, 0)
    k = rope(proj[..., C_Q:C_Q + C_KV].reshape(b, s, C_KV_HEADS, C_HD), pos)
    v = proj[..., C_Q + C_KV:].reshape(b, s, C_KV_HEADS, C_HD)
    kp = jnp.pad(k, ((0, 0), (WINDOW, 0), (0, 0), (0, 0)))
    vp = jnp.pad(v, ((0, 0), (WINDOW, 0), (0, 0), (0, 0)))
    t_idx = jnp.arange(WINDOW)[:, None]
    s_idx = jnp.arange(2 * WINDOW)[None, :]
    band = (s_idx > t_idx) & (s_idx <= t_idx + WINDOW)
    sink = sinks.astype(F32).reshape(C_KV_HEADS, C_GROUP)[None, :, :, None]
    scale = C_HD ** -0.5

    def block(args):
        j, qj = args
        kj = lax.dynamic_slice_in_dim(kp, j * WINDOW, 2 * WINDOW, axis=1)
        vj = lax.dynamic_slice_in_dim(vp, j * WINDOW, 2 * WINDOW, axis=1)
        valid = band & (j * WINDOW - WINDOW + s_idx >= 0)
        sc = jnp.einsum('btkgd,bskd->bkgts', qj, kj) * scale
        sc = jnp.where(valid, sc, -jnp.inf)
        m = jnp.maximum(jnp.max(sc, -1), sink)
        pr = jnp.exp(sc - m[..., None])
        den = jnp.sum(pr, -1) + jnp.exp(sink - m)
        pr = pr / den[..., None]
        return jnp.einsum('bkgts,bskd->btkgd', pr, vj)

    o = lax.map(block, (jnp.arange(nb), q))
    o = jnp.moveaxis(o, 0, 1).reshape(b, s, C_Q)
    return o.astype(hn.dtype) @ w_o + b_o

def second_inputs(seed: int = 0) -> dict:
    key = jax.random.key(seed)
    ks = jax.random.split(key, 24)
    nrm = jax.random.normal
    x = nrm(ks[0], (BATCH, SEQ, D_MODEL), F32)
    p = nrm(ks[1], (DEPTH, BATCH, SEQ, PLE_DIM), F32)
    positions = jnp.broadcast_to(jnp.arange(SEQ, dtype=jnp.int32), (BATCH, SEQ))
    norm_gains = 1.0 + 0.05 * nrm(ks[2], (DEPTH, 4, D_MODEL), F32)
    w_in_ab = nrm(ks[3], (N_EVEN, D_MODEL, IN_COLS), F32) * D_MODEL ** -0.5
    conv_a = nrm(ks[4], (N_EVEN, CONV_K, A_CONV_CH), F32) * CONV_K ** -0.5
    a_log = jnp.log(jax.random.uniform(ks[5], (N_EVEN, A_HEADS), F32, 1.0, 16.0))
    dt = jnp.exp(jax.random.uniform(ks[6], (N_EVEN, A_HEADS), F32, np.log(1e-3), np.log(1e-1)))
    dt_bias = dt + jnp.log(-jnp.expm1(-dt))
    norm_a = 1.0 + 0.05 * nrm(ks[7], (N_EVEN, A_DV), F32)
    i_bias_b = 0.1 * nrm(ks[8], (N_EVEN, B_HEADS), F32)
    f_bias_b = 3.0 + 0.5 * nrm(ks[9], (N_EVEN, B_HEADS), F32)
    norm_b = 1.0 + 0.05 * nrm(ks[10], (N_EVEN, B_HEADS, B_DV), F32)
    w_out_ab = nrm(ks[11], (N_EVEN, MIX_AB, D_MODEL), F32) * MIX_AB ** -0.5
    w_qkv_c = nrm(ks[12], (N_ODD, D_MODEL, C_COLS), F32) * D_MODEL ** -0.5
    b_qkv_c = 0.02 * nrm(ks[13], (N_ODD, C_COLS), F32)
    sinks_c = nrm(ks[14], (N_ODD, C_HEADS), F32)
    w_o_c = nrm(ks[15], (N_ODD, C_Q, D_MODEL), F32) * C_Q ** -0.5
    b_o_c = 0.02 * nrm(ks[16], (N_ODD, D_MODEL), F32)
    w_up = nrm(ks[17], (DEPTH, D_MODEL, D_FF_2), F32) * D_MODEL ** -0.5
    w_down = nrm(ks[18], (DEPTH, D_FF_2, D_MODEL), F32) * D_FF_2 ** -0.5
    w_ple = nrm(ks[19], (DEPTH, PLE_DIM, D_MODEL), F32) * PLE_DIM ** -0.5
    w_ple_gate = nrm(ks[20], (DEPTH, D_MODEL, D_MODEL), F32) * D_MODEL ** -0.5
    return {"x": x, "p": p, "positions": positions, "norm_gains": norm_gains,
            "w_in_ab": w_in_ab, "conv_a": conv_a, "a_log": a_log, "dt_bias": dt_bias,
            "norm_a": norm_a, "i_bias_b": i_bias_b, "f_bias_b": f_bias_b, "norm_b": norm_b,
            "w_out_ab": w_out_ab, "w_qkv_c": w_qkv_c, "b_qkv_c": b_qkv_c, "sinks_c": sinks_c,
            "w_o_c": w_o_c, "b_o_c": b_o_c, "w_up": w_up, "w_down": w_down,
            "w_ple": w_ple, "w_ple_gate": w_ple_gate}

def second_block(x, p, positions, norm_gains, w_in_ab, conv_a, a_log, dt_bias, norm_a,
              i_bias_b, f_bias_b, norm_b, w_out_ab, w_qkv_c, b_qkv_c, sinks_c, w_o_c, b_o_c,
              w_up, w_down, w_ple, w_ple_gate):
    h = x
    for layer in range(DEPTH):
        gains = norm_gains[layer]
        hn = rmsnorm(h, gains[0])
        if layer % 2 == 0:
            e = layer // 2
            mix = mixer_ab(hn, w_in_ab[e], conv_a[e], a_log[e], dt_bias[e], norm_a[e],
                           i_bias_b[e], f_bias_b[e], norm_b[e], w_out_ab[e])
        else:
            o = layer // 2
            mix = mixer_c(hn, positions, w_qkv_c[o], b_qkv_c[o], sinks_c[o], w_o_c[o], b_o_c[o])
        h = h + rmsnorm(mix, gains[1])
        hn = rmsnorm(h, gains[2])
        ff = jnp.square(jax.nn.relu(hn @ w_up[layer])) @ w_down[layer]
        h = h + rmsnorm(ff, gains[3])
        gate = jax.nn.sigmoid(h @ w_ple_gate[layer])
        h = h + gate * (p[layer] @ w_ple[layer])
    return h


def setup_inputs(seed=0):
    out = dict(first_inputs(seed))
    for name, value in second_inputs(seed + 1).items():
        if name != "x":
            out[name + "_2"] = value
    return out


def reference(
    x, c, ctx, c_ctx, w_ada, b_ada, g_mix, w_in, w_fourier, b_fourier, g_q_a, w_q_b, g_kv_a,
    w_kv_b, w_out, g_ffn, w_up, w_dw, b_dw, w_down, g_final, p_2, positions_2, norm_gains_2,
    w_in_ab_2, conv_a_2, a_log_2, dt_bias_2, norm_a_2, i_bias_b_2, f_bias_b_2, norm_b_2,
    w_out_ab_2, w_qkv_c_2, b_qkv_c_2, sinks_c_2, w_o_c_2, b_o_c_2, w_up_2, w_down_2, w_ple_2,
    w_ple_gate_2,
):
    x = first_block(
        x, c, ctx, c_ctx, w_ada, b_ada, g_mix, w_in, w_fourier, b_fourier, g_q_a, w_q_b, g_kv_a,
        w_kv_b, w_out, g_ffn, w_up, w_dw, b_dw, w_down, g_final,
    )
    return second_block(
        x, p_2, positions_2, norm_gains_2, w_in_ab_2, conv_a_2, a_log_2, dt_bias_2, norm_a_2,
        i_bias_b_2, f_bias_b_2, norm_b_2, w_out_ab_2, w_qkv_c_2, b_qkv_c_2, sinks_c_2, w_o_c_2,
        b_o_c_2, w_up_2, w_down_2, w_ple_2, w_ple_gate_2,
    )


_drawn_inputs = setup_inputs


def setup_inputs(seed=0):
    import zlib

    import numpy as np

    out = dict(_drawn_inputs(seed))
    spreads = {}
    factors = {'g_mix': 8.0,
     'b_fourier': 6.483,
     'g_q_a': 8.0,
     'g_kv_a': 8.0,
     'g_ffn': 4.046,
     'b_dw': 4.325,
     'i_bias_b_2': 200.0,
     'sinks_c_2': 2.7}
    for name, (base, spread) in spreads.items():
        noise = np.random.default_rng([zlib.crc32(name.encode()), seed]).standard_normal(out[name].shape)
        drawn = base * np.exp(spread * noise) if base else spread * noise
        out[name] = __import__('jax').numpy.asarray(drawn.astype(out[name].dtype))
    for name, factor in factors.items():
        out[name] = (out[name] * factor).astype(out[name].dtype)
    return out
```

```python
from contextlib import ExitStack, contextmanager

import numpy as np

import concourse.bass as bass
from concourse import mybir
from concourse.alu_op_type import AluOpType as ALU

ACT = mybir.ActivationFunctionType
F32 = mybir.dt.float32
I32 = mybir.dt.int32
AX = mybir.AxisListType.X
ds = bass.ds

P = 128
D = 1024
KT = D // P
NL, NC = 512, 256
W = NL + NC
EPS = 1e-6
DEPTH = 2
NMOD = 6
NHEAD, DV1, DNOPE, DROPE = 12, 64, 64, 32
QRANK, KVRANK, FW = 384, 128, 256
SCALE1 = float((DNOPE + DROPE) ** -0.5)
DFF = 2816
FT1 = DFF // P
NH2 = 4
CHUNK = 64
NCH = NL // CHUNK
DFF2 = 4096
HD2 = 64
NQH, NKVH = 16, 4
WIN = 128
PLE = 256
SCALE2 = float(P ** -0.5)
SLOTS = 4
UB = 8


def vector_columns():
    at, n = {}, 0
    for name, cols in (
        [("c", 2 * KT)]
        + [(f"{v}{l}", m) for l in range(DEPTH) for v, m in (
            ("g_mix", KT), ("g_ffn", KT), ("b_ada", NMOD * KT), ("b_four", 2), ("g_q", 3), ("g_kv", 1),
            ("dw0_", 2 * FT1), ("dw1_", 2 * FT1), ("dw2_", 2 * FT1), ("b_dw", 2 * FT1))]
        + [("g_final", KT)]
        + [(f"gain{l}{i}", KT) for l in range(2) for i in range(4)]
        + [("conv0", 12), ("conv1", 12), ("conv2", 12), ("conv3", 12)]
        + [("norm_a", 1), ("norm_b", NH2), ("b_qkv", 10), ("b_o", KT), ("sink", NQH), ("inv_freq", 1)]
        + [("rowb", 4), ("sign", 1)]
    ):
        at[name] = n
        n += cols
    return at, n


COL, NV = vector_columns()


def shape_constants():
    parts = {}
    parts["ident"] = np.eye(P)
    n_freq = DROPE // 4
    inv = 10000.0 ** (-np.arange(n_freq, dtype=np.float32) / np.float32(n_freq))
    inv = inv.astype(np.float32)
    rows = np.repeat(np.arange(NL // 64), 64).astype(np.float32)
    cols = np.tile(np.arange(64), NL // 64).astype(np.float32)
    ang = np.concatenate([rows[:, None] * inv, cols[:, None] * inv], -1).astype(np.float32).T
    parts["cos1"] = np.tile(np.cos(ang), (8, 1))
    parts["sin1"] = np.tile(np.concatenate([-np.sin(ang), np.sin(ang)]), (4, 1))
    swap = np.zeros((P, P))
    for i in range(P):
        swap[i ^ 16, i] = 1.0
    parts["swap16"] = swap
    k = np.arange(64)
    w64 = 2 * np.pi * np.outer(k, k) % (2 * np.pi * 64) / 64
    cb = np.zeros((P, 2 * P))
    for g in range(2):
        cb[64 * g:64 * g + 64, 64 * g:64 * g + 64] = np.cos(w64) / 8
        cb[64 * g:64 * g + 64, P + 64 * g:P + 64 * g + 64] = np.sin(w64) / 8
    parts["cb"] = cb
    for name, n in (("dft", NL), ("dftc", NC)):
        i = np.arange(n)
        w = 2 * np.pi * (np.outer(i, i) % n) / n
        for s, m in (("c", np.cos(w) / np.sqrt(n)), ("s", -np.sin(w) / np.sqrt(n))):
            parts[name + s] = m.reshape(n // P, P, n).transpose(1, 0, 2).reshape(P, -1)
    e, c = np.arange(P)[:, None], np.arange(P)[None, :]
    same = e // CHUNK == c // CHUNK
    parts["causal"] = (same & (e <= c)) * 1.0
    for lv in range(6):
        b = 1 << lv
        parts[f"lv{lv}"] = ((e // (2 * b) == c // (2 * b)) & (c % (2 * b) >= b) & (e % (2 * b) < b)) * 1.0
    sel = np.zeros((P, NH2 * P))
    for h in range(NH2):
        sel[h, h * P:(h + 1) * P] = 1.0
    parts["sel"] = sel
    start = np.zeros((P, NL))
    start[:, ::CHUNK] = 1.0
    parts["keep"] = 1.0 - start
    parts["drop"] = start * -1e30
    sw = np.zeros((P, P))
    for i in range(P):
        sw[i ^ 32, i] = 1.0
    parts["swap32"] = sw
    q, s = np.arange(WIN)[:, None], np.arange(2 * WIN)[None, :]
    band = (s > q) & (s <= q + WIN)
    m = np.zeros((WIN, NL // WIN, 2 * WIN))
    for j in range(NL // WIN):
        m[:, j] = np.where(band & (j * WIN - WIN + s >= 0), 0.0, -1e30)
    parts["window"] = m.reshape(WIN, -1)
    at, n = {}, 0
    for name, a in parts.items():
        at[name] = (n, a.shape[1])
        n += a.shape[1]
    return at, np.concatenate([np.asarray(a, np.float32) for a in parts.values()], 1)


CAT, CONST = shape_constants()
INV32 = (10000.0 ** (-np.arange(32, dtype=np.float32) / np.float32(32))).astype(np.float32)


def stages():
    out = []
    for l in range(DEPTH):
        out.append((f"ada{l}", 48))
    for l in range(DEPTH):
        out += [(f"in{l}", 8), (f"out{l}", 8), (f"up{l}", 2 * FT1), (f"down{l}", 24)]
    out += [("projA", 16), ("projB", 16), ("outAB", 8), ("up2_0", 32), ("down2_0", 32), ("gate2_0", 8)]
    out += [("qkv", 12), ("outC", 8), ("up2_1", 32), ("down2_1", 32), ("gate2_1", 8)]
    return out


def units(w, order=None):
    w = np.asarray(w)
    if order is not None:
        w = np.concatenate([w[:, a:b] for a, b in order], 1)
    kp, mp = -w.shape[0] % (UB * P), -w.shape[1] % P
    if kp or mp:
        full = np.zeros((w.shape[0] + kp, w.shape[1] + mp), w.dtype)
        full[:w.shape[0], :w.shape[1]] = w
        w = full
    u, m = w.shape[0] // (UB * P), w.shape[1] // P
    return w.reshape(u, UB, P, m, P).transpose(3, 0, 2, 1, 4).reshape(m * u, P, UB * P)


def tiles(a):
    a = np.asarray(a)
    return a.reshape(a.shape[0] // P, P, -1).transpose(1, 0, 2).reshape(P, -1)


class Core:

    def __init__(self, nc, stack, total_units):
        self.nc = nc
        self.total = total_units
        sb = lambda name, n, p=P, dt=F32: stack.enter_context(nc.sbuf_tensor(name, [p, n], dt))
        self.X = sb("X", KT * W)
        self.H = sb("H", KT * W)
        self.RING = sb("RING", SLOTS * UB * P)
        self.VEC = sb("VEC", NV)
        self.MOD = sb("MOD", DEPTH * NMOD * KT * 2)
        self.ONES = sb("ONES", P)
        self.ID = sb("ID", P)
        self.RS = sb("RS", W)
        self.MS = sb("MS", W)
        self.SQ = sb("SQ", 2 * W)
        self.AV = sb("AV", 2 * KT)
        self.ARENA = sb("ARENA", 31800)
        self.PS = stack.enter_context(nc.psum_tensor("PS", [P, 8 * 512], F32))
        sem = lambda name: stack.enter_context(nc.semaphore(name))
        self.filled = [sem(f"ring_filled{i}") for i in range(SLOTS)]
        self.units_done = sem("units_done")
        self.small = sem("small_loaded")
        self.small_n = 0
        self.at = 0
        self.pool = [stack.enter_context(nc.semaphore(f"phase{i}")) for i in range(40)]

    def bank(self, b, n=512, lo=0, p0=0, p1=P):
        return self.PS[p0:p1, 512 * b + lo:512 * b + lo + n]

    def x(self, k, lo=0, n=NL):
        return self.X[:, ds(k * W + lo, n)] if not isinstance(k, int) else self.X[:, k * W + lo:k * W + lo + n]

    def h(self, k, lo=0, n=NL):
        return self.H[:, ds(k * W + lo, n)] if not isinstance(k, int) else self.H[:, k * W + lo:k * W + lo + n]

    def vec(self, name, j=0, n=1):
        a = COL[name] + j
        return self.VEC[:, a:a + n] if isinstance(j, int) else self.VEC[:, ds(a, n)]

    def a(self, lo, n, p0=0, p1=P):
        return self.ARENA[p0:p1, lo:lo + n] if isinstance(lo, int) else self.ARENA[p0:p1, ds(lo, n)]

    def block(self, slot, k):
        o = (slot * UB + k) * P
        return self.RING[:, o:o + P]


@contextmanager
def phase(c, *names, **groups):
    wanted = [(name, None) for name in names] + list(groups.items())
    found, at = {}, 0
    for name, n in wanted:
        found[name] = c.pool[at] if n is None else c.pool[at:at + n]
        at += n or 1
    with c.nc.Block() as block:
        yield found, block
    c.nc.all_engine_barrier(sems_to_clear=range(c.pool[0].num, c.pool[-1].num + 1))


class Chain:

    def __init__(self, eng, sem):
        self.eng, self.sem, self.n = eng, sem, 0

    def __call__(self, ins):
        self.n += 1
        ins.then_inc(self.sem, 1)
        self.eng.wait_ge(self.sem, self.n)


def loop(eng, n, body, peel=0):
    rolled = n - peel if n - peel >= 3 else 0
    if rolled:
        with eng.Fori(0, rolled) as i:
            body(i)
    for i in range(rolled, n):
        body(i)


def prefetch(c, sp, stream, n):
    base = c.at

    def turn(i, count=4):
        for s in range(count):
            sp.wait_ge(c.units_done, base + 4 * i + s + 1)
            sp.dma_start(c.RING[:, s * UB * P:(s + 1) * UB * P],
                         stream[ds(base + 4 * i + s + SLOTS, 1)].rearrange("a p n -> p (a n)")
                         if not isinstance(i, int) else stream[base + 4 * i + s + SLOTS])\
                .then_inc(c.filled[s], 16)
    turns = min(n, c.total - SLOTS - base) // 4
    if turns > 0:
        loop(sp, turns, turn)


def start(c, args):
    with phase(c, "dma", "ones") as (s, block):

        @block.sync
        def _(sp):
            sp.dma_start(c.VEC[:], args["vecs"]).then_inc(s["dma"], 16)
            for i in range(SLOTS):
                sp.dma_start(c.RING[:, i * UB * P:(i + 1) * UB * P], args["stream"][i]).then_inc(c.filled[i], 16)
            sp.dma_start(c.ID[:], args["consts"][:, CAT["ident"][0]:CAT["ident"][0] + P]).then_inc(s["dma"], 16)
            sp.dma_start(c.X[:], args["x_in"]).then_inc(s["dma"], 16)
            sp.wait_ge(s["dma"], 48)

        @block.vector
        def _(dve):
            dve.memset(c.ONES[:], 1.0).then_inc(s["ones"], 1)
            dve.wait_ge(s["ones"], 1)


def ada(c, args):
    n = NMOD * KT
    SC = c.a(0, 2 * KT)
    with phase(c, "silu", "sums", "free") as (s, block):

        @block.sync
        def _(sp):
            prefetch(c, sp, args["stream"], DEPTH * n)

        @block.scalar
        def _(act):
            act.activation(SC, c.vec("c", 0, 2 * KT), ACT.Silu).then_inc(s["silu"], 1)

        @block.tensor
        def _(pe):
            pe.wait_ge(s["silu"], 1)
            for l in range(DEPTH):
                def turn(i):
                    for m in range(4):
                        u = l * n + 4 * i
                        pe.wait_ge(c.filled[m], 16 * (c.at // 4 + l * n // 4 + i + 1))
                        o = 512 * l + 2 * (4 * i + m)
                        for k in range(KT):
                            out = c.PS[:, ds(o, 2)] if not isinstance(i, int) else c.PS[:, o:o + 2]
                            mm = pe.matmul(out, c.block(m, k), SC[:, 2 * k:2 * k + 2], start=(k == 0), stop=(k == KT - 1))
                        mm.then_inc(c.units_done, 1)
                loop(pe, n // 4, turn)

        @block.vector
        def _(dve):
            for l in range(DEPTH):
                dve.wait_ge(c.units_done, c.at + (l + 1) * n)
                b = c.vec(f"b_ada{l}", 0, n).rearrange("p (m a) -> p m a", a=1).broadcast_to([P, n, 2])
                dve.tensor_tensor(c.MOD[:, l * 2 * n:(l + 1) * 2 * n].rearrange("p (m a) -> p m a", a=2),
                                  c.PS[:, 512 * l:512 * l + 2 * n].rearrange("p (m a) -> p m a", a=2),
                                  b, ALU.add).then_inc(s["sums"], 1)
            dve.wait_ge(s["sums"], DEPTH)
    c.at += DEPTH * n


def mod(c, l, part, k, cond):
    o = l * 2 * NMOD * KT
    j = o + 2 * (part * KT + k) + cond
    return c.MOD[:, j:j + 1] if isinstance(k, int) else c.MOD[:, ds(j, 1)]


def norm(c, src, out, nk, size, n, gain, shift=None, scale_prep=None, post=None):
    parts = [(0, 0, min(n, NL))] + ([(1, NL, n - NL)] if n > NL else [])
    with phase(c, "squared", "summed", "mean", "root", "scaled", "own", "prep") as (s, block):

        @block.scalar
        def _(act):
            for k in range(nk):
                if k >= 2:
                    act.wait_ge(s["summed"], k - 1)
                act.activation(c.SQ[:, (k % 2) * W:(k % 2) * W + n], src(k, 0, n), ACT.Square).then_inc(s["squared"], 1)
            act.wait_ge(s["mean"], 1)
            act.activation(c.RS[:, 0:n], c.MS[:, 0:n], ACT.Sqrt).then_inc(s["root"], 1)
            if shift is not None:
                for k in range(nk):
                    act.wait_ge(s["scaled"], (k + 1) * len(parts))
                    for q, lo, m in parts:
                        o = out(k, lo, m)
                        act.activation(o, o, ACT.Identity, bias=shift(k, q))

        @block.tensor
        def _(pe):
            for k in range(nk):
                pe.wait_ge(s["squared"], k + 1)
                for q, lo, m in parts:
                    mm = pe.matmul(c.PS[:, lo:lo + m], c.ONES[:], c.SQ[:, (k % 2) * W + lo:(k % 2) * W + lo + m],
                                   start=(k == 0), stop=(k == nk - 1))
                mm.then_inc(s["summed"], 1)

        @block.vector
        def _(dve):
            if scale_prep is not None:
                scale_prep(dve, s["prep"])
            dve.wait_ge(s["summed"], nk)
            dve.tensor_scalar(c.MS[:, 0:n], c.PS[:, 0:n], 1.0 / size, EPS, ALU.mult, ALU.add).then_inc(s["mean"], 1)
            dve.wait_ge(s["root"], 1)
            dve.reciprocal(c.RS[:, 0:n], c.RS[:, 0:n]).then_inc(s["own"], 1)
            dve.wait_ge(s["own"], 1)
            for k in range(nk):
                for q, lo, m in parts:
                    dve.scalar_tensor_tensor(out(k, lo, m), src(k, lo, m), gain(k, q), c.RS[:, lo:lo + m],
                                             ALU.mult, ALU.mult).then_inc(s["scaled"], 1)
            if post is not None:
                post(dve, s["scaled"], s["own"])


def modulated_norm(c, l, g, part, n):
    conds = 2 if n > NL else 1

    def prep(dve, sem):
        i = 0
        for q in range(conds):
            o = l * 2 * NMOD * KT + 2 * (part + 1) * KT + q
            sc = c.MOD[:, o:o + 2 * KT - 1:2]
            a = c.AV[:, q * KT:(q + 1) * KT]
            dve.scalar_tensor_tensor(a, sc, 1.0, c.vec(g, 0, KT), ALU.add, ALU.mult).then_inc(sem, 1)
        dve.wait_ge(sem, conds)

    norm(c, c.x, c.h, KT, D, n, lambda k, q: c.AV[:, q * KT + k:q * KT + k + 1],
         lambda k, q: mod(c, l, part, k, q), prep)


def plain_norm(c, g, n=NL):
    norm(c, c.x, c.h, KT, D, n, lambda k, q: c.vec(g, k))


def linear(c, args, rhs, kt, tiles_out, n, scalar=None, vector=None, extra=(), credit=None, width=None, peel=0):
    u = -(-kt // UB)
    base = c.at
    turns = tiles_out // 4
    with phase(c, *extra, free=4) as (s, block):
        free = s["free"]

        def wait_acc(eng, i, m):
            eng.wait_ge(c.units_done, base + 4 * u * i + u * (m + 1))

        @block.sync
        def _(sp):
            prefetch(c, sp, args["stream"], tiles_out * u)

        @block.tensor
        def _(pe):
            for m in range(4):
                pe.sem_inc(free[m], 1)

            def turn(i):
                for m in range(4):
                    pe.wait_ge(free[m], i + 1)
                    for k in range(kt):
                        j = m * u + k // UB
                        slot = j % SLOTS
                        if k % UB == 0:
                            pe.wait_ge(c.filled[slot], 16 * (base // SLOTS + u * i + j // SLOTS + 1))
                        cols, rows = width(4 * i + m) if width else (n, P)
                        for b, lo, w in ((0, 0, min(cols, 512)), (1, 512, cols - 512)):
                            if w > 0:
                                mm = pe.matmul(c.bank(2 * m + b, w, p1=rows), c.block(slot, k % UB)[:, 0:rows],
                                               rhs(k, lo, w), start=(k == 0), stop=(k == kt - 1))
                        if k % UB == UB - 1 or k == kt - 1:
                            mm.then_inc(c.units_done, 1)
            loop(pe, turns, turn, peel)

        def evacuator(eng, take):
            def turn(i):
                for m in range(4):
                    wait_acc(eng, i, m)
                    take(eng, i, m, c.PS[:, 1024 * m:1024 * m + n], s)
            loop(eng, turns, turn, peel)

        if scalar is not None:
            @block.scalar
            def _(act):
                evacuator(act, scalar)

        if vector is not None:
            @block.vector
            def _(dve):
                if credit is not None:
                    credit(dve, s)
                evacuator(dve, vector)
    c.at += tiles_out * u


def residual(c, l, part, n):
    conds = [(0, 0, NL)] + ([(1, NL, NC)] if n > NL else [])

    def take(dve, i, m, acc, s):
        for q, lo, w in conds:
            x = c.x(4 * i + m, lo, w)
            ins = dve.scalar_tensor_tensor(x, acc[:, lo:lo + w], mod(c, l, part, 4 * i + m, q), x, ALU.mult, ALU.add)
        ins.then_inc(s["free"][m], 1)
    return take


def load(sp, sem, *pairs):
    for dst, src in pairs:
        sp.dma_start(dst, src).then_inc(sem, 16)
    sp.wait_ge(sem, 16 * len(pairs))


def const(args, name, p=P):
    o, n = CAT[name]
    return args["consts"][0:p, o:o + n]


def ffn_up(c, args, l, n):
    parts = [(0, NL)] + ([(NL, NC)] if n > NL else [])
    CV = FT1 * W
    SG = CV + 4 * W

    def col(name, i, m):
        j = COL[f"{name}{l}"] + (m % 2) * FT1 + 2 * i + m // 2
        return c.VEC[:, j:j + 1] if isinstance(i, int) else c.VEC[:, ds(j, 1)]

    def scalar(act, i, m, acc, s):
        pair = 2 * i + m // 2
        act.wait_ge(s["product"], pair + 1)
        act.activation(c.a(CV + m * W, n), acc, ACT.Identity, bias=col("b_dw", i, m),
                       scale=col("dw1_", i, m)).then_inc(s["centre"], 1)
        if m % 2:
            act.wait_ge(s["free"][m - 1], i + 2)
            act.wait_ge(s["product"], pair + 2)
            act.activation(c.a(SG, n), c.a(CV + (m - 1) * W, n), ACT.Silu).then_inc(s["gate"], 1)

    def vector(dve, i, m, acc, s):
        free = s["free"][m]
        pair = 2 * i + m // 2
        dve.wait_ge(s["centre"], 4 * i + m + 1)
        for lo, w in parts:
            y = c.a(CV + m * W + lo + 1, w - 1)
            ins = dve.scalar_tensor_tensor(y, acc[:, lo:lo + w - 1], col("dw0_", i, m), y, ALU.mult, ALU.add)
        ins.then_inc(s["left"], 1)
        dve.wait_ge(s["left"], 4 * i + m + 1)
        for lo, w in parts:
            y = c.a(CV + m * W + lo, w - 1)
            ins = dve.scalar_tensor_tensor(y, acc[:, lo + 1:lo + w], col("dw2_", i, m), y, ALU.mult, ALU.add)
        ins.then_inc(free, 1)
        if m % 2:
            dve.wait_ge(free, i + 2)
            dve.wait_ge(s["gate"], pair + 1)
            dve.tensor_tensor(c.a(pair * W, n), c.a(SG, n), c.a(CV + m * W, n), ALU.mult).then_inc(s["product"], 1)

    linear(c, args, c.h, KT, 2 * FT1, n, scalar, vector, ("centre", "left", "gate", "product"),
           credit=lambda dve, s: dve.sem_inc(s["product"], 2))


def hid(c, w=W):
    return lambda k, lo, n: c.a(k * w + lo, n)


A1 = {}
_at = 0
for _name, _n in (("PROJ", 7 * W), ("WQ", 3 * NHEAD * 96), ("WKV", 2 * NHEAD * 64), ("WF", 2 * FW), ("V", 6 * NHEAD * 64),
                  ("COS", NL), ("SIN", NL), ("SWAP", P), ("UNION", 0)):
    A1[_name] = _at
    _at += _n
for _first, _parts in (("UNION", (("CB", 2 * P), ("DC", 4 * NL), ("DS", 4 * NL), ("DCC", 2 * NC), ("DSC", 2 * NC),
                                  ("UV", 12 * 2 * P), ("FT", 2 * W))),
                       ("UNION", (("QT", 4 * W), ("KTT", 4 * W), ("PP", 2 * W), ("PT", 6 * W), ("QR", W), ("T1", W),
                                  ("ST", 64)))):
    _at = A1[_first]
    for _name, _n in _parts:
        A1[_name] = _at
        _at += _n
    assert _at <= 31800, _at


def in_proj(c, args, l):
    pr = A1["PROJ"]
    nq = W if l == 0 else NL

    def width(t):
        return (2, P) if t == 7 else (W, DROPE) if t == 6 else (W, P) if t == 5 else (nq, P)

    def scalar(act, i, m, acc, s):
        n, rows = width(4 * i + m)
        o = c.a(pr + (4 * i + m) * W, n, 0, rows) if 4 * i + m < 7 else c.MS[:, 0:2]
        act.activation(o, c.PS[0:rows, 1024 * m:1024 * m + n], ACT.Copy).then_inc(s["free"][m], 1)

    linear(c, args, c.h, KT, 8, W, scalar, width=width)


def load_mixer(c, args, l):
    with phase(c, "dma") as (s, block):
        @block.sync
        def _(sp):
            load(sp, s["dma"],
                 (c.a(A1["WQ"], 3 * NHEAD * 96), args["wq"][l]), (c.a(A1["WKV"], 2 * NHEAD * 64), args["wkv"][l]),
                 (c.a(A1["WF"], 2 * FW), args["wf"][l]), (c.a(A1["COS"], NL), const(args, "cos1")),
                 (c.a(A1["SIN"], NL), const(args, "sin1")), (c.a(A1["SWAP"], P), const(args, "swap16")),
                 (c.a(A1["CB"], 2 * P), const(args, "cb")), (c.a(A1["DC"], 4 * NL), const(args, "dftc")),
                 (c.a(A1["DS"], 4 * NL), const(args, "dfts")), (c.a(A1["DCC"], 2 * NC), const(args, "dftcc")),
                 (c.a(A1["DSC"], 2 * NC), const(args, "dftcs")))


def fourier(c, args, l):
    pr, uv, ft = A1["PROJ"], A1["UV"], A1["FT"]
    parts = [(0, NL, "DC", "DS", 0)] + ([(NL, NC, "DCC", "DSC", 4)] if l == 0 else [])
    tt = 6 if l == 0 else 4
    with phase(c, "channels", "uv", "v", "v_out", "positions", "ft", "mixed", "h") as (s, block):

        @block.tensor
        def _(pe):
            for t in range(tt):
                for q in range(2):
                    mm = pe.matmul(c.bank(t, 2 * P, q * 2 * P), c.a(pr + q * W + t * P, P), c.a(A1["CB"], 2 * P),
                                   start=True, stop=True)
                mm.then_inc(s["channels"], 1)
            for t in range(6):
                b = 6 if t % 2 == 0 else 0
                if t:
                    pe.wait_ge(s["v_out"], t - 1) if t > 1 else pe.wait_ge(s["uv"], 2)
                for q, (lo, n) in enumerate(((0, 512), (512, 256))):
                    mm = pe.matmul(c.bank(b + q, n), c.a(pr + 5 * W + t * P, P), c.a(A1["WKV"] + 768 + lo, n),
                                   start=True, stop=True)
                mm.then_inc(s["v"], 1)
            pe.wait_ge(s["uv"], tt)
            for q in range(2):
                for r, (lo, n, cs, sn, t0) in enumerate(parts):
                    for t in range(n // P):
                        for z, tab in ((0, cs), (1, sn)):
                            mm = pe.matmul(c.bank(2 + 2 * q + r, n), c.a(uv + ((t0 + t) * 2 + q) * 2 * P + z * P, P),
                                           c.a(A1[tab] + t * n, n), start=(t == 0 and z == 0), stop=(t == n // P - 1 and z == 1))
                mm.then_inc(s["positions"], 1)
            pe.wait_ge(s["ft"], 2)
            pe.wait_ge(s["v_out"], 6)
            for q in range(2):
                for r, (lo, n, *_) in enumerate(parts):
                    for k in range(2):
                        mm = pe.matmul(c.bank((6, 0)[q] + r, n), c.a(A1["WF"] + k * FW + q * P, P), c.a(ft + k * W + lo, n),
                                       start=(k == 0), stop=(k == 1))
                mm.then_inc(s["mixed"], 1)

        n = W if l == 0 else NL

        @block.scalar
        def _(act):
            for t in range(6):
                act.wait_ge(s["v"], t + 1)
                b = 6 if t % 2 == 0 else 0
                act.activation(c.a(A1["V"] + t * 768, 768), c.PS[:, 512 * b:512 * b + 768], ACT.Copy).then_inc(s["v_out"], 1)
            for q in range(2):
                act.wait_ge(s["mixed"], q + 1)
                b = (6, 0)[q]
                act.activation(c.h(q, 0, n), c.PS[:, 512 * b:512 * b + n], ACT.Identity,
                               bias=c.vec(f"b_four{l}", q)).then_inc(s["h"], 1)

        @block.vector
        def _(dve):
            for t in range(tt):
                dve.wait_ge(s["channels"], t + 1)
                dve.tensor_copy(c.a(uv + t * 4 * P, 4 * P), c.bank(t)).then_inc(s["uv"], 1)
            for q in range(2):
                dve.wait_ge(s["positions"], q + 1)
                dve.tensor_copy(c.a(ft + q * W, n), c.PS[:, 1024 * (q + 1):1024 * (q + 1) + n]).then_inc(s["ft"], 1)


def key_rope(c):
    pr, kt, t1 = A1["PROJ"] + 6 * W, A1["KTT"], A1["T1"]
    with phase(c, "swapped", "own", "rows") as (s, block):

        @block.tensor
        def _(pe):
            pe.matmul(c.bank(0, NL, p1=DROPE), c.a(A1["SWAP"], DROPE, 0, DROPE), c.a(pr, NL, 0, DROPE),
                      start=True, stop=True).then_inc(s["swapped"], 1)

        @block.vector
        def _(dve):
            link = Chain(dve, s["own"])
            dve.wait_ge(s["swapped"], 1)
            link(dve.tensor_tensor(c.a(t1, NL, 0, DROPE), c.bank(0, NL, p1=DROPE), c.a(A1["SIN"], NL, 0, DROPE), ALU.mult))
            link(dve.tensor_tensor(c.a(pr, NL, 0, DROPE), c.a(pr, NL, 0, DROPE), c.a(A1["COS"], NL, 0, DROPE), ALU.mult))
            link(dve.tensor_tensor(c.a(pr, NL, 0, DROPE), c.a(pr, NL, 0, DROPE), c.a(t1, NL, 0, DROPE), ALU.add))
            for h in range(4):
                dve.tensor_copy(c.a(kt + h * W, W, 64, 96), c.a(pr, W, 0, DROPE))


def heads_qk(c, l, g):
    pr, qt, kt, qr, t1 = (A1[x] for x in ("PROJ", "QT", "KTT", "QR", "T1"))
    nq = W if l == 0 else NL
    cq, ckv = pr + 2 * W, pr + 5 * W
    with phase(c, "q", "k", "r", "r_out", "swapped", "own", "out") as (s, block):

        @block.tensor
        def _(pe):
            def project(b, w, kn, stride, x, n):
                for r, (lo, m) in enumerate(((0, min(n, 512)), (512, n - 512))):
                    for k in range(kn):
                        if m > 0:
                            mm = pe.matmul(c.bank(b + r, m), c.a(w + k * stride, P), c.a(x + k * W + lo, m),
                                           start=(k == 0), stop=(k == kn - 1))
                return mm
            project(0, A1["WQ"] + 768 + g * P, 3, 1152, cq, nq).then_inc(s["r"], 1)
            for j in range(2):
                project(2 + 2 * j, A1["WQ"] + (2 * g + j) * P, 3, 1152, cq, nq).then_inc(s["q"], 1)
            project(6, A1["WKV"] + 2 * g * P, 1, 0, ckv, W).then_inc(s["k"], 1)
            pe.wait_ge(s["r_out"], 1)
            pe.matmul(c.bank(0, NL), c.a(A1["SWAP"], P), c.a(qr, NL), start=True, stop=True).then_inc(s["swapped"], 1)
            pe.wait_ge(s["out"], 1)
            project(2, A1["WKV"] + (2 * g + 1) * P, 1, 0, ckv, W).then_inc(s["k"], 1)

        @block.scalar
        def _(act):
            act.wait_ge(s["r"], 1)
            act.activation(c.a(qr, nq), c.PS[:, 0:nq], ACT.Copy).then_inc(s["r_out"], 1)
            for j in range(2):
                act.wait_ge(s["k"], j + 1)
                b = (6, 2)[j]
                for p in range(2):
                    act.activation(c.a(kt + (2 * j + p) * W, W, 0, 64), c.PS[64 * p:64 * p + 64, 512 * b:512 * b + W], ACT.Copy)

        @block.vector
        def _(dve):
            link = Chain(dve, s["own"])
            for j in range(2):
                dve.wait_ge(s["q"], j + 1)
                for p in range(2):
                    b = 2 + 2 * j
                    ins = dve.tensor_copy(c.a(qt + (2 * j + p) * W, nq, 0, 64), c.PS[64 * p:64 * p + 64, 512 * b:512 * b + nq])
                ins.then_inc(s["out"], 1)
            dve.wait_ge(s["swapped"], 1)
            link(dve.tensor_tensor(c.a(t1, NL), c.bank(0, NL), c.a(A1["SIN"], NL), ALU.mult))
            link(dve.tensor_tensor(c.a(qr, NL), c.a(qr, NL), c.a(A1["COS"], NL), ALU.mult))
            for h in range(4):
                r = slice(32 * h, 32 * h + 32)
                dve.tensor_tensor(c.a(qt + h * W, NL, 64, 96), c.a(qr, NL, 32 * h, 32 * h + 32),
                                  c.a(t1, NL, 32 * h, 32 * h + 32), ALU.add)
                if nq > NL:
                    dve.tensor_copy(c.a(qt + h * W + NL, NC, 64, 96), c.a(qr + NL, NC, 32 * h, 32 * h + 32))


def attention1(c, l, g):
    qt, kt, pp, pt, st, vv = (A1[x] for x in ("QT", "KTT", "PP", "PT", "ST", "V"))
    tiles_q = 6 if l == 0 else 4
    steps = [(h, i, 0 if i < 4 else NL, W if i < 4 else NC) for h in range(4) for i in range(tiles_q)]
    SUM, NEG, REC = st, st + 24, st + 48
    products = tiles_q // 4 + tiles_q % 4 // 2

    def turned_half(eng, a, half):
        h, i, k0, n = steps[a]
        m = n // P // 2
        eng.wait_ge(s["turned"], a + 1)
        if h:
            eng.wait_ge(s["o"], (h - 1) * products + 1 + (i >= 4))
        dst = c.a(pt + (k0 // P + half * m) * W, m * W).rearrange("p (t q) -> p t q", q=W)[:, :, i * P:(i + 1) * P]
        return dst, c.bank(4 + half, m * P).rearrange("p (t q) -> p t q", q=P)

    def result(act, a):
        h, i, *_ = steps[a]
        part = i // 2 - 1
        head = 4 * g + h
        p0, w = 64 * (head % 2), (NL, NC)[part]
        act.wait_ge(s["o"], h * products + part + 1)
        o = (2 + head // 2) * W + part * NL
        act.activation(c.H[p0:p0 + 64, o:o + w], c.bank(6 + part, w, p0=p0, p1=p0 + 64), ACT.Copy).then_inc(s["o_out"], 1)

    with phase(c, "scores", "neg", "probs", "normed", "turned", "pt_a", "pt_v", "o", "o_out", "own") as (s, block):

        @block.tensor
        def _(pe):
            def score(a):
                h, i, k0, n = steps[a]
                if a >= 2:
                    pe.wait_ge(s["probs"], a - 1)
                for r, (lo, m) in enumerate(((0, min(n, 512)), (512, n - 512))):
                    if m > 0:
                        mm = pe.matmul(c.bank(2 * (a % 2) + r, m), c.a(qt + h * W + i * P, P, 0, 96),
                                       c.a(kt + h * W + k0 + lo, m, 0, 96), start=True, stop=True)
                mm.then_inc(s["scores"], 1)

            def turn(a):
                h, i, k0, n = steps[a]
                pe.wait_ge(s["normed"], a + 1)
                if a >= 1:
                    pe.wait_ge(s["pt_a"], a)
                    pe.wait_ge(s["pt_v"], a)
                for k in range(n // P):
                    half = n // P // 2
                    out = c.bank(4 + (k >= half), P, (k % half) * P)
                    mm = pe.transpose(out, c.a(pp + (a % 2) * W + k * P, P), c.ID[:])
                mm.then_inc(s["turned"], 1)

            def values(h, part):
                last = h * tiles_q + (3 if part == 0 else 5)
                pe.wait_ge(s["pt_a"], last + 1)
                pe.wait_ge(s["pt_v"], last + 1)
                j = h * products + part
                if j >= 1:
                    pe.wait_ge(s["o_out"], j)
                head = 4 * g + h
                p0 = 64 * (head % 2)
                n, ts = (NL, range(6)) if part == 0 else (NC, (4, 5))
                for t in ts:
                    mm = pe.matmul(c.bank(6 + part, n, p0=p0, p1=p0 + 64), c.a(vv + t * 768 + head * 64, 64),
                                   c.a(pt + t * W + part * NL, n), start=(t == ts[0]), stop=(t == ts[-1]))
                mm.then_inc(s["o"], 1)

            for a in range(len(steps) + 1):
                if a < len(steps):
                    score(a)
                if a >= 1:
                    turn(a - 1)
                    h, i = steps[a - 1][:2]
                    if i == 3:
                        values(h, 0)
                    if i == 5:
                        values(h, 1)

        @block.scalar
        def _(act):
            for a in range(len(steps) + 2):
                if a < len(steps):
                    h, i, k0, n = steps[a]
                    act.wait_ge(s["neg"], a + 1)
                    if a >= 2:
                        act.wait_ge(s["turned"], a - 1)
                    act.activation(c.a(pp + (a % 2) * W, n), c.PS[:, 1024 * (a % 2):1024 * (a % 2) + n], ACT.Exp,
                                   bias=c.a(NEG + a, 1), scale=SCALE1, accum_out=c.a(SUM + a, 1)).then_inc(s["probs"], 1)
                if a >= 2 and steps[a - 2][1] in (3, 5):
                    result(act, a - 2)
                if 1 <= a <= len(steps):
                    dst, src = turned_half(act, a - 1, 0)
                    act.activation(dst, src, ACT.Copy).then_inc(s["pt_a"], 1)

        @block.vector
        def _(dve):
            link = Chain(dve, s["own"])
            for a in range(len(steps) + 1):
                if a < len(steps):
                    h, i, k0, n = steps[a]
                    dve.wait_ge(s["scores"], a + 1)
                    link(dve.tensor_reduce(c.a(REC + 2, 1), c.PS[:, 1024 * (a % 2):1024 * (a % 2) + n], AX, ALU.max))
                    dve.tensor_scalar(c.a(NEG + a, 1), c.a(REC + 2, 1), -SCALE1, None, ALU.mult).then_inc(s["neg"], 1)
                if a >= 1:
                    dst, src = turned_half(dve, a - 1, 1)
                    dve.tensor_copy(dst, src).then_inc(s["pt_v"], 1)
                if a < len(steps):
                    dve.wait_ge(s["probs"], a + 1)
                    link(dve.reciprocal(c.a(REC + a % 2, 1), c.a(SUM + a, 1)))
                    dve.tensor_scalar(c.a(pp + (a % 2) * W, n), c.a(pp + (a % 2) * W, n), c.a(REC + a % 2, 1), None,
                                      ALU.mult).then_inc(s["normed"], 1)


TW = NH2 * NL
A2 = {}
_at = 0
for _name, _n in (("OA", TW), ("OB", TW), ("ROWS", 9 * NL), ("COLS", 128), ("MASK", P), ("SMALL", 256), ("STATE", 8 * P),
                  ("SEL", NH2 * P), ("Q", TW), ("K", TW), ("V", TW), ("Z", TW), ("U", 0)):
    A2[_name] = _at
    _at += _n
for _parts in ((("GATES", KT * P), ("RT", 2 * NL), ("RT2", 2 * NL), ("KEEP", NL), ("DROP", NL)),
               (("CV", 4 * NL),),
               (("DEC", NL), ("TMP", NL), ("TT", TW), ("ATT", TW), ("KB", TW), ("KD", TW), ("VB", TW), ("BT", 2 * NL),
                ("LV", P))):
    _at = A2["U"]
    for _name, _n in _parts:
        A2[_name] = _at
        _at += _n
    assert _at <= 31800, _at
A2["T"], A2["LT"], A2["Y"], A2["FLOOR"] = A2["OB"], A2["OA"], A2["DEC"], A2["TT"]
BETA, GCUM, GREST, ACOL, KEXP, MROW, MTROW, IEXP, BCUM = range(9)


def row(c, r, n=NL, lo=0):
    return c.a(A2["ROWS"] + r * NL + lo, n, 0, NH2)


def by_chunk(ap):
    return ap.rearrange("p (n t) -> p n t", t=CHUNK)


def gate_rows(c, args):
    G, RT, R2 = A2["GATES"], A2["RT"], A2["RT2"]
    KEEP, DROP, SM = A2["KEEP"], A2["DROP"], A2["SMALL"]
    with phase(c, "dma", "gates", "act", "own") as (s, block):

        @block.sync
        def _(sp):
            load(sp, s["dma"], (c.a(G, KT * P), args["gates"]), (c.a(KEEP, NL), const(args, "keep")),
                 (c.a(DROP, NL), const(args, "drop")), (c.a(A2["SEL"], NH2 * P), const(args, "sel")),
                 (c.a(A2["MASK"], P), const(args, "causal")))

        @block.tensor
        def _(pe):
            pe.wait_ge(s["dma"], 80)
            for k in range(KT):
                mm = pe.matmul(c.bank(0), c.a(G + k * P, P), c.h(k), start=(k == 0), stop=(k == KT - 1))
            mm.then_inc(s["gates"], 1)

        rt = lambda r: c.a(RT + r * NL, NL, 0, NH2)
        r2 = lambda r: c.a(R2 + r * NL, NL, 0, NH2)
        both = lambda o: c.a(o, 2 * NL, 0, NH2)
        bias = lambda j: c.VEC[0:NH2, COL["rowb"] + j:COL["rowb"] + j + 1]

        @block.scalar
        def _(act):
            act.wait_ge(s["gates"], 1)
            act.activation(row(c, BETA), c.bank(0, p1=NH2), ACT.Sigmoid).then_inc(s["act"], 1)
            act.activation(c.a(SM, 1, 0, NH2), bias(0), ACT.Exp).then_inc(s["act"], 1)
            act.wait_ge(s["own"], 6)
            act.activation(both(R2), both(RT), ACT.Abs).then_inc(s["act"], 1)
            act.wait_ge(s["act"], 3)
            act.activation(both(R2), both(R2), ACT.Exp, scale=-1.0).then_inc(s["act"], 1)
            act.wait_ge(s["act"], 4)
            act.activation(both(R2), both(R2), ACT.Ln, bias=1.0).then_inc(s["act"], 1)

        @block.vector
        def _(dve):
            link = Chain(dve, s["own"])
            dve.wait_ge(s["dma"], 80)
            dve.wait_ge(s["act"], 1)
            link(dve.tensor_copy(rt(0), c.bank(0, p0=32, p1=36)))
            link(dve.tensor_copy(row(c, MROW), c.bank(0, p0=64, p1=68)))
            link(dve.tensor_copy(rt(1), c.bank(0, p0=96, p1=100)))
            link(dve.tensor_scalar(rt(0), rt(0), bias(1), None, ALU.add))
            link(dve.tensor_scalar(rt(1), rt(1), bias(3), -1.0, ALU.add, ALU.mult))
            link(dve.tensor_scalar(row(c, MROW), row(c, MROW), bias(2), None, ALU.add))
            dve.wait_ge(s["act"], 5)
            link(dve.scalar_tensor_tensor(both(RT), both(RT), 0.0, both(R2), ALU.max, ALU.add))
            link(dve.tensor_scalar(rt(0), rt(0), c.a(SM, 1, 0, NH2), -1.0, ALU.mult, ALU.mult))
            link(dve.tensor_scalar(rt(1), rt(1), -1.0, None, ALU.mult))
            keep, drop = c.a(KEEP, NL, 0, NH2), c.a(DROP, NL, 0, NH2)
            link(dve.tensor_tensor_scan(row(c, GCUM), keep, rt(0), 0.0, ALU.mult, ALU.add))
            link(dve.tensor_tensor_scan(row(c, BCUM), keep, rt(1), 0.0, ALU.mult, ALU.add))
            last = lambda r: by_chunk(row(c, r))[:, :, CHUNK - 1:CHUNK]
            wide = lambda ap: ap.broadcast_to([NH2, NCH, CHUNK])
            link(dve.tensor_tensor(by_chunk(row(c, GREST)), wide(last(GCUM)), by_chunk(row(c, GCUM)), ALU.subtract))
            link(dve.tensor_tensor(row(c, ACOL), row(c, MROW), row(c, BCUM), ALU.subtract))
            link(dve.tensor_tensor_scan(row(c, KEXP), drop, row(c, ACOL), 0.0, ALU.add, ALU.max))
            m = lambda lo, n: c.a(SM + 16 + lo, n, 0, NH2)
            link(dve.memset(m(0, 1), 0.0))
            link(dve.tensor_copy(c.a(SM + 32, NCH, 0, NH2), last(KEXP)))
            link(dve.tensor_copy(c.a(SM + 48, NCH, 0, NH2), last(BCUM)))
            link(dve.tensor_tensor_scan(m(1, NCH), c.a(SM + 32, NCH, 0, NH2), c.a(SM + 48, NCH, 0, NH2), 0.0, ALU.max, ALU.add))
            before = wide(m(0, NCH).rearrange("p (n a) -> p n a", a=1))
            link(dve.tensor_tensor(by_chunk(row(c, MROW)), by_chunk(row(c, KEXP)), before, ALU.max))
            link(dve.tensor_tensor(row(c, MTROW), row(c, BCUM), row(c, MROW), ALU.add))
            link(dve.tensor_tensor(by_chunk(row(c, IEXP)), before, by_chunk(row(c, MROW)), ALU.subtract))
            link(dve.tensor_tensor(by_chunk(row(c, KEXP)), by_chunk(row(c, ACOL)), wide(last(MROW)), ALU.subtract))


def gate_columns(c):
    CO, TMP = A2["COLS"], A2["SMALL"]
    with phase(c, "turned", "copied", "exp", "own") as (s, block):
        @block.tensor
        def _(pe):
            for r in range(5):
                for t in range(4):
                    mm = pe.matmul(c.bank(0, NH2, (r * 4 + t) * NH2), row(c, r, P, t * P), c.ID[0:NH2, 0:NH2], start=True, stop=True)
            mm.then_inc(s["turned"], 1)

        @block.vector
        def _(dve):
            dve.wait_ge(s["turned"], 1)
            dve.tensor_copy(c.a(CO, 80), c.bank(0, 80)).then_inc(s["copied"], 1)
            dve.wait_ge(s["exp"], 3)
            dve.tensor_tensor(c.a(CO + 96, 16), c.a(CO + 80, 16), c.a(CO, 16), ALU.mult).then_inc(s["own"], 1)
            dve.wait_ge(s["own"], 1)

        @block.scalar
        def _(act):
            act.wait_ge(s["copied"], 1)
            act.activation(c.a(CO + 80, 16), c.a(CO + GCUM * 16, 16), ACT.Exp).then_inc(s["exp"], 1)
            act.activation(c.a(CO + GREST * 16, 16), c.a(CO + GREST * 16, 16), ACT.Exp).then_inc(s["exp"], 1)
            act.activation(c.a(CO + KEXP * 16, 16), c.a(CO + KEXP * 16, 16), ACT.Exp).then_inc(s["exp"], 1)


def token_col(c, r, t, h):
    o = A2["COLS"] + r * 16 + t * 4 + h
    return c.ARENA[:, o:o + 1]


EXPG, BEXPG = 5, 6


def project_a(c, args):
    CV = A2["CV"]

    def tap(k, i, m):
        j = COL[f"conv{k}"] + 4 * i + m
        return c.VEC[:, ds(j, 1)] if not isinstance(i, int) else c.VEC[:, j:j + 1]

    def out(i, m):
        return c.a(A2["Q"] + (4 * i + m) * NL, NL)

    def scalar(act, i, m, acc, s):
        if isinstance(i, int) and i == 3:
            act.activation(out(i, m), acc, ACT.Silu).then_inc(s["free"][m], 1)
            return
        act.wait_ge(s["cv_free"], 4 * i + m + 1)
        act.activation(c.a(CV + m * NL, NL), acc, ACT.Identity, scale=tap(3, i, m)).then_inc(s["tap3"], 1)
        act.wait_ge(s["free"][m], i + 2)
        act.activation(out(i, m), c.a(CV + m * NL, NL), ACT.Silu).then_inc(s["cv_free"], 1)

    def vector(dve, i, m, acc, s):
        if isinstance(i, int) and i == 3:
            return
        dve.wait_ge(s["tap3"], 4 * i + m + 1)
        for k in (2, 1, 0):
            d = 3 - k
            y = c.a(CV + m * NL + d, NL - d)
            ins = dve.scalar_tensor_tensor(y, acc[:, 0:NL - d], tap(k, i, m), y, ALU.mult, ALU.add)
            if k:
                ins.then_inc(s["taps"], 1)
                dve.wait_ge(s["taps"], 8 * i + 2 * m + 3 - k)
        ins.then_inc(s["free"][m], 1)

    linear(c, args, c.h, KT, 16, NL, scalar, vector, ("tap3", "taps", "cv_free"),
           credit=lambda dve, s: dve.sem_inc(s["cv_free"], 4), peel=1)


def unit_norms(c, tiles_of, scales, eps=EPS, gain=None, times=None):
    n = len(tiles_of)
    with phase(c, "squared", "summed", "mean", "root", "own", "done") as (s, block):
        MEAN = A2["CV"]

        @block.scalar
        def _(act):
            for j in range(n):
                if j >= 2:
                    act.wait_ge(s["summed"], j - 1)
                act.activation(c.SQ[:, (j % 2) * W:(j % 2) * W + NL], tiles_of[j], ACT.Square).then_inc(s["squared"], 1)
            for j in range(n):
                act.wait_ge(s["mean"], j + 1)
                act.activation(c.a(MEAN + j * NL, NL), c.a(MEAN + j * NL, NL), ACT.Sqrt).then_inc(s["root"], 1)

        @block.tensor
        def _(pe):
            for j in range(n):
                pe.wait_ge(s["squared"], j + 1)
                pe.matmul(c.bank(j), c.ONES[:], c.SQ[:, (j % 2) * W:(j % 2) * W + NL], start=True, stop=True).then_inc(s["summed"], 1)

        @block.vector
        def _(dve):
            for j in range(n):
                dve.wait_ge(s["summed"], j + 1)
                mul, add = scales[j]
                dve.tensor_scalar(c.a(MEAN + j * NL, NL), c.bank(j), mul, add, ALU.mult, ALU.add).then_inc(s["mean"], 1)
            link = Chain(dve, s["own"])
            for j in range(n):
                dve.wait_ge(s["root"], j + 1)
                r = c.a(MEAN + j * NL, NL)
                link(dve.reciprocal(r, r))
                if gain is None:
                    dve.tensor_tensor(tiles_of[j], tiles_of[j], r, ALU.mult).then_inc(s["done"], 1)
                else:
                    link(dve.scalar_tensor_tensor(tiles_of[j], tiles_of[j], gain(j), r, ALU.mult, ALU.mult))
                    dve.tensor_tensor(tiles_of[j], tiles_of[j], times[j], ALU.mult).then_inc(s["done"], 1)


def delta_inner(c, args):
    o = A2
    sel = lambda h: c.a(o["SEL"] + h * P, P, 0, NH2)
    with phase(c, "dma", "bank_g", "bank_b", "bank_k", "bank_a", "bank_t", "act_done", "dec", "exp", "masked", "lt",
               "turn_k", "turn_v", "kb", "vb", "own", "att", "own_act", "rounds") as (s, block):

        @block.tensor
        def _(pe):
            for h in range(NH2):
                if h:
                    pe.wait_ge(s["rounds"], h)
                    pe.wait_ge(s["act_done"], h)
                pe.matmul(c.bank(0), sel(h), row(c, GCUM), start=True, stop=True).then_inc(s["bank_g"], 1)
                pe.matmul(c.bank(1), sel(h), row(c, BETA), start=True, stop=True).then_inc(s["bank_b"], 1)
                for b, x, sem in ((2, "K", s["bank_k"]), (3, "Q", s["bank_a"])):
                    for t in range(4):
                        mm = pe.matmul(c.bank(b, P, t * P), c.a(o["K"] + h * NL + t * P, P), c.a(o[x] + h * NL + t * P, P),
                                       start=True, stop=True)
                    mm.then_inc(sem, 1)
                for b, x, sem in ((4, "K", s["turn_k"]), (5, "V", s["turn_v"])):
                    for t in range(4):
                        mm = pe.transpose(c.bank(b, P, t * P), c.a(o[x] + h * NL + t * P, P), c.ID[:])
                    mm.then_inc(sem, 1)

        @block.vector
        def _(dve):
            link = Chain(dve, s["own"])
            m4 = lambda ap: ap.rearrange("p (t q) -> p t q", q=P)
            mask = c.a(o["MASK"], P).rearrange("p (a q) -> p a q", a=1).broadcast_to([P, 4, P])
            for h in range(NH2):
                dec, tmp = c.a(o["DEC"], NL), c.a(o["TMP"], NL)
                dve.wait_ge(s["bank_g"], h + 1)
                if h:
                    dve.wait_ge(s["exp"], 2 * h)
                for t in range(4):
                    ins = dve.scalar_tensor_tensor(c.a(o["DEC"] + t * P, P), c.bank(0, P, t * P), token_col(c, GCUM, t, h),
                                                   c.a(o["MASK"], P), ALU.subtract, ALU.mult)
                ins.then_inc(s["dec"], 1)
                dve.wait_ge(s["exp"], 2 * h + 1)
                link(dve.tensor_tensor(m4(dec), m4(dec), mask, ALU.mult))
                dve.wait_ge(s["bank_k"], h + 1)
                lt = c.a(o["LT"] + h * NL, NL)
                link(dve.tensor_tensor(lt, dec, c.bank(2), ALU.mult))
                dve.wait_ge(s["bank_b"], h + 1)
                link(dve.tensor_tensor(lt, lt, c.bank(1), ALU.mult))
                dve.wait_ge(s["bank_a"], h + 1)
                link(dve.tensor_tensor(c.a(o["ATT"] + h * NL, NL), dec, c.bank(3), ALU.mult))
                dve.wait_ge(s["exp"], 2 * h + 2)
                dve.tensor_copy(c.a(o["SMALL"] + 64 + h * NCH, NCH).rearrange("p (n a) -> p n a", a=1),
                                by_chunk(tmp)[:, :, CHUNK - 1:CHUNK])
                q = c.a(o["Q"] + h * NL, NL)
                link(dve.tensor_tensor(q, q, tmp, ALU.mult))
                dve.wait_ge(s["turn_v"], h + 1)
                for t in range(4):
                    ins = dve.tensor_scalar(c.a(o["VB"] + h * NL + t * P, P), c.bank(5, P, t * P), token_col(c, BETA, t, h), None, ALU.mult)
                ins.then_inc(s["rounds"], 1)

        @block.scalar
        def _(act):
            for h in range(NH2):
                act.wait_ge(s["dec"], h + 1)
                act.activation(c.a(o["DEC"], NL), c.a(o["DEC"], NL), ACT.Exp).then_inc(s["exp"], 1)
                if h:
                    act.wait_ge(s["rounds"], h)
                act.activation(c.a(o["TMP"], NL), c.bank(0), ACT.Exp).then_inc(s["exp"], 1)
                act.wait_ge(s["turn_k"], h + 1)
                for t in range(4):
                    act.activation(c.a(o["KB"] + h * NL + t * P, P), c.bank(4, P, t * P), ACT.Copy, scale=token_col(c, BEXPG, t, h))
                    ins = act.activation(c.a(o["KD"] + h * NL + t * P, P), c.bank(4, P, t * P), ACT.Copy,
                                         scale=token_col(c, GREST, t, h))
                ins.then_inc(s["act_done"], 1)

    tt = lambda h: c.a(o["TT"] + h * NL, NL)
    tn = lambda h: c.a(o["T"] + h * NL, NL)
    id4 = c.ID[:].rearrange("p (a q) -> p a q", a=1).broadcast_to([P, 4, P])
    m4 = lambda ap: ap.rearrange("p (t q) -> p t q", q=P)
    for lv in range(6):
        with phase(c, "dma", "bt", "y", "y_out", "z", "zt", "t_new", "tt_new") as (s, block):
            @block.sync
            def _(sp):
                load(sp, s["dma"], (c.a(o["LV"], P), const(args, f"lv{lv}")))

            @block.tensor
            def _(pe):
                def second(h):
                    pe.wait_ge(s["y_out"], h + 1)
                    if h >= 2:
                        pe.wait_ge(s["tt_new"], h - 1)
                        pe.wait_ge(s["t_new"], h - 1)
                    for t in range(4):
                        mm = pe.matmul(c.bank(2 + h % 2, P, t * P), c.a(o["TT"] + h * NL + t * P, P),
                                       c.a(o["Y"] + (h % 2) * NL + t * P, P), start=True, stop=True)
                    mm.then_inc(s["z"], 1)
                    for t in range(4):
                        mm = pe.matmul(c.bank(4 + h % 2, P, t * P), c.a(o["Y"] + (h % 2) * NL + t * P, P),
                                       c.a(o["TT"] + h * NL + t * P, P), start=True, stop=True)
                    mm.then_inc(s["zt"], 1)
                for h in range(NH2):
                    pe.wait_ge(s["bt"], h + 1)
                    for t in range(4):
                        rhs = c.ID[:] if lv == 0 else c.a(o["T"] + h * NL + t * P, P)
                        mm = pe.matmul(c.bank(h % 2, P, t * P), c.a(o["BT"] + (h % 2) * NL + t * P, P), rhs, start=True, stop=True)
                    mm.then_inc(s["y"], 1)
                    if lv and h:
                        second(h - 1)
                if lv:
                    second(NH2 - 1)

            @block.vector
            def _(dve):
                lvm = c.a(o["LV"], P).rearrange("p (a q) -> p a q", a=1).broadcast_to([P, 4, P])
                dve.wait_ge(s["dma"], 16)

                def masked(h):
                    if h >= 2:
                        dve.wait_ge(s["y"], h - 1)
                        dve.wait_ge(s["tt_new"], h - 1)
                    dve.tensor_tensor(m4(c.a(o["BT"] + (h % 2) * NL, NL)), m4(c.a(o["LT"] + h * NL, NL)), lvm, ALU.mult).then_inc(s["bt"], 1)

                masked(0)
                for h in range(NH2):
                    if h + 1 < NH2:
                        masked(h + 1)
                    if lv == 0:
                        dve.wait_ge(s["bt"], h + 1)
                        dve.tensor_tensor(m4(tt(h)), id4, m4(c.a(o["BT"] + (h % 2) * NL, NL)), ALU.subtract).then_inc(s["tt_new"], 1)
                        dve.wait_ge(s["y"], h + 1)
                        dve.tensor_tensor(m4(tn(h)), id4, m4(c.bank(h % 2)), ALU.subtract).then_inc(s["t_new"], 1)
                    else:
                        dve.wait_ge(s["z"], h + 1)
                        dve.wait_ge(s["zt"], h + 1)
                        dve.tensor_tensor(tn(h), tn(h), c.bank(2 + h % 2), ALU.subtract).then_inc(s["t_new"], 1)
                        dve.tensor_tensor(tt(h), tt(h), c.bank(4 + h % 2), ALU.subtract).then_inc(s["tt_new"], 1)

            if lv:
                @block.scalar
                def _(act):
                    for h in range(NH2):
                        act.wait_ge(s["y"], h + 1)
                        if h >= 2:
                            act.wait_ge(s["zt"], h - 1)
                        act.activation(c.a(o["Y"] + (h % 2) * NL, NL), c.bank(h % 2), ACT.Copy).then_inc(s["y_out"], 1)
    with phase(c, "w", "u", "kb", "vb") as (s, block):
        @block.tensor
        def _(pe):
            for h in range(NH2):
                if h >= 2:
                    pe.wait_ge(s["kb"], h - 1)
                    pe.wait_ge(s["vb"], h - 1)
                for b, sem in ((0, s["w"]), (2, s["u"])):
                    for t in range(4):
                        f = h * NL + t * P
                        x, y = (o["KB"], o["TT"]) if b == 0 else (o["TT"], o["VB"])
                        mm = pe.matmul(c.bank(b + h % 2, P, t * P), c.a(x + f, P), c.a(y + f, P), start=True, stop=True)
                    mm.then_inc(sem, 1)

        @block.scalar
        def _(act):
            for h in range(NH2):
                act.wait_ge(s["w"], h + 1)
                act.activation(c.a(o["KB"] + h * NL, NL), c.bank(h % 2), ACT.Copy).then_inc(s["kb"], 1)

        @block.vector
        def _(dve):
            for h in range(NH2):
                dve.wait_ge(s["u"], h + 1)
                dve.tensor_copy(c.a(o["VB"] + h * NL, NL), c.bank(2 + h % 2)).then_inc(s["vb"], 1)


def heads(c, name, lo, n, p0=0, p1=P):
    return c.a(A2[name], TW, p0, p1).rearrange("p (h t) -> p h t", t=NL)[:, :, lo:lo + n]


def delta_scan(c):
    o = A2
    ST, VN = o["STATE"], o["BT"]
    with phase(c, "zero", "ws", "vn", "out", "ds", "oa", "state") as (s, block):

        @block.tensor
        def _(pe):
            pe.wait_ge(s["zero"], 1)
            for n in range(NCH):
                t, r, b = n // 2, 64 * (n % 2), 3 * (n % 2)
                lo = t * P + r
                if n:
                    pe.wait_ge(s["state"], 4 * n)
                if n >= 2:
                    pe.wait_ge(s["oa"], n - 1)
                for h in range(NH2):
                    mm = pe.matmul(c.bank(b, P, h * P, r, r + 64), c.a(o["KB"] + h * NL + lo, 64), c.a(ST + h * P, P), start=True, stop=True)
                mm.then_inc(s["ws"], 1)
                pe.wait_ge(s["vn"], n + 1)
                for h in range(NH2):
                    pe.matmul(c.bank(b + 1, 64, h * 64), c.a(ST + h * P, P), c.a(o["Q"] + h * NL + lo, 64), start=True, stop=False)
                    mm = pe.matmul(c.bank(b + 1, 64, h * 64), c.a(VN + h * P, P, r, r + 64),
                                   c.a(o["ATT"] + h * NL + lo, 64, r, r + 64), start=False, stop=True)
                mm.then_inc(s["out"], 1)
                for h in range(NH2):
                    mm = pe.matmul(c.bank(b + 2, P, h * P), c.a(o["KD"] + h * NL + t * P, P, r, r + 64),
                                   c.a(VN + h * P, P, r, r + 64), start=True, stop=True)
                mm.then_inc(s["ds"], 1)

        @block.scalar
        def _(act):
            for n in range(NCH):
                act.wait_ge(s["out"], n + 1)
                act.activation(heads(c, "OA", n * CHUNK, CHUNK), c.bank(3 * (n % 2) + 1, 256).rearrange("p (h t) -> p h t", t=64),
                               ACT.Copy).then_inc(s["oa"], 1)

        @block.vector
        def _(dve):
            dve.memset(c.a(ST, 4 * P), 0.0).then_inc(s["zero"], 1)
            dve.wait_ge(s["zero"], 1)
            for n in range(NCH):
                t, r, b = n // 2, 64 * (n % 2), 3 * (n % 2)
                dve.wait_ge(s["ws"], n + 1)
                if n:
                    dve.wait_ge(s["ds"], n)
                dve.tensor_tensor(c.a(VN, 4 * P, r, r + 64).rearrange("p (h q) -> p h q", q=P),
                                  heads(c, "VB", t * P, P, r, r + 64),
                                  c.bank(b, 512, 0, r, r + 64).rearrange("p (h q) -> p h q", q=P), ALU.subtract).then_inc(s["vn"], 1)
                dve.wait_ge(s["ds"], n + 1)
                for h in range(NH2):
                    st = c.a(ST + h * P, P)
                    dve.scalar_tensor_tensor(st, st, c.a(o["SMALL"] + 64 + h * NCH + n, 1), c.bank(b + 2, P, h * P),
                                             ALU.mult, ALU.add).then_inc(s["state"], 1)
                dve.wait_ge(s["state"], 4 * n + 4)


def project_b(c, args):
    def scalar(act, i, m, acc, s):
        free = s["free"][m]
        dst = c.a(A2[("Q", "K", "Z")[i]] + m * NL, NL)
        if i == 2:
            act.activation(dst, acc, ACT.Sigmoid).then_inc(free, 1)
        else:
            act.activation(dst, acc, ACT.Copy, scale=(SCALE2, 1.0)[i]).then_inc(free, 1)

    linear(c, args, c.h, KT, 12, NL, scalar, peel=3)
    values_by_token(c, args, A2["V"], 4, NH2 * P, NL)


def values_by_token(c, args, dst, slots, n, stride, first_slot=0, bias=None):
    with phase(c, "v", "out") as (s, block):
        @block.sync
        def _(sp):
            prefetch(c, sp, args["stream"], SLOTS)

        @block.tensor
        def _(pe):
            for m in range(SLOTS):
                pe.wait_ge(c.filled[m], 16 * (c.at // SLOTS + 1))
            ring = c.RING[:].rearrange("p (s k n) -> p s k n", s=SLOTS, k=UB)
            for t in range(4):
                for k in range(KT):
                    mm = pe.matmul(c.bank(t, n).rearrange("p (s q) -> p s q", q=P), c.h(k, t * P, P),
                                   ring[:, first_slot:first_slot + slots, k, :], start=(k == 0), stop=(k == KT - 1 and bias is None))
                if bias is not None:
                    mm = pe.matmul(c.bank(t, n), c.ONES[0:1, :], bias, start=False, stop=True)
                mm.then_inc(s["v"], 1)
            for m in range(SLOTS):
                pe.matmul(c.bank(4 + m, 2), c.block(m, 0), c.h(0, 0, 2), start=True, stop=True).then_inc(c.units_done, 1)

        @block.vector
        def _(dve):
            for t in range(4):
                dve.wait_ge(s["v"], t + 1)
                dve.tensor_copy(c.a(dst + t * stride, n), c.bank(t, n)).then_inc(s["out"], 1)
    c.at += SLOTS


def mlstm_inner(c):
    o = A2
    sel = lambda h: c.a(o["SEL"] + h * P, P, 0, NH2)
    with phase(c, "bank_m", "bank_i", "bank_t", "bank_a", "turn_k", "dec", "exp", "own", "rounds", "act_done") as (s, block):

        @block.tensor
        def _(pe):
            for h in range(NH2):
                if h:
                    pe.wait_ge(s["rounds"], h)
                    pe.wait_ge(s["act_done"], h)
                for b, r, sem in ((0, MROW, s["bank_m"]), (1, IEXP, s["bank_i"]), (2, MTROW, s["bank_t"])):
                    pe.matmul(c.bank(b), sel(h), row(c, r), start=True, stop=True).then_inc(sem, 1)
                for t in range(4):
                    mm = pe.matmul(c.bank(3, P, t * P), c.a(o["K"] + h * NL + t * P, P), c.a(o["Q"] + h * NL + t * P, P),
                                   start=True, stop=True)
                mm.then_inc(s["bank_a"], 1)
                for t in range(4):
                    mm = pe.transpose(c.bank(4, P, t * P), c.a(o["K"] + h * NL + t * P, P), c.ID[:])
                mm.then_inc(s["turn_k"], 1)

        @block.vector
        def _(dve):
            link = Chain(dve, s["own"])
            m4 = lambda ap: ap.rearrange("p (t q) -> p t q", q=P)
            mask = c.a(o["MASK"], P).rearrange("p (a q) -> p a q", a=1).broadcast_to([P, 4, P])
            for h in range(NH2):
                dec, tmp = c.a(o["DEC"], NL), c.a(o["TMP"], NL)
                dve.wait_ge(s["bank_m"], h + 1)
                for t in range(4):
                    ins = dve.scalar_tensor_tensor(c.a(o["DEC"] + t * P, P), c.bank(0, P, t * P), token_col(c, ACOL, t, h),
                                                   c.a(o["MASK"], P), ALU.subtract, ALU.mult)
                ins.then_inc(s["dec"], 1)
                dve.wait_ge(s["exp"], 3 * h + 1)
                link(dve.tensor_tensor(m4(dec), m4(dec), mask, ALU.mult))
                dve.wait_ge(s["bank_a"], h + 1)
                link(dve.tensor_tensor(c.a(o["ATT"] + h * NL, NL), dec, c.bank(3), ALU.mult))
                dve.wait_ge(s["exp"], 3 * h + 2)
                dve.tensor_copy(c.a(o["SMALL"] + 64 + h * NCH, NCH).rearrange("p (n a) -> p n a", a=1),
                                by_chunk(tmp)[:, :, CHUNK - 1:CHUNK])
                q = c.a(o["Q"] + h * NL, NL)
                dve.tensor_tensor(q, q, tmp, ALU.mult).then_inc(s["rounds"], 1)

        @block.scalar
        def _(act):
            for h in range(NH2):
                act.wait_ge(s["dec"], h + 1)
                act.activation(c.a(o["DEC"], NL), c.a(o["DEC"], NL), ACT.Exp, scale=-1.0).then_inc(s["exp"], 1)
                if h:
                    act.wait_ge(s["rounds"], h)
                act.wait_ge(s["bank_i"], h + 1)
                act.activation(c.a(o["TMP"], NL), c.bank(1), ACT.Exp).then_inc(s["exp"], 1)
                act.wait_ge(s["bank_t"], h + 1)
                act.activation(c.a(o["FLOOR"] + h * NL, NL), c.bank(2), ACT.Exp, scale=-1.0).then_inc(s["exp"], 1)
                act.wait_ge(s["turn_k"], h + 1)
                for t in range(4):
                    ins = act.activation(c.a(o["KD"] + h * NL + t * P, P), c.bank(4, P, t * P), ACT.Copy,
                                         scale=token_col(c, KEXP, t, h))
                ins.then_inc(s["act_done"], 1)


def mlstm_scan(c):
    o = A2
    ST = o["STATE"]
    with phase(c, "zero", "out", "ds", "ob", "state") as (s, block):

        @block.tensor
        def _(pe):
            pe.wait_ge(s["zero"], 1)
            for n in range(NCH):
                t, r, b = n // 2, 64 * (n % 2), 3 * (n % 2)
                lo = t * P + r
                if n:
                    pe.wait_ge(s["state"], 8 * n)
                if n >= 2:
                    pe.wait_ge(s["ob"], n - 1)
                for h in range(NH2):
                    att = c.a(o["ATT"] + h * NL + lo, 64, r, r + 64)
                    for z in range(2):
                        out = c.bank(b, 64, z * 256 + h * 64)
                        pe.matmul(out, c.a(ST + (z * 4 + h) * P, P), c.a(o["Q"] + h * NL + lo, 64), start=True, stop=False)
                        inner = c.a(o["V"] + t * NL + h * P, P, r, r + 64) if z == 0 else c.ONES[r:r + 64, :]
                        mm = pe.matmul(out, inner, att, start=False, stop=True)
                mm.then_inc(s["out"], 1)
                for h in range(NH2):
                    kw = c.a(o["KD"] + h * NL + t * P, P, r, r + 64)
                    pe.matmul(c.bank(b + 1, P, h * P), kw, c.a(o["V"] + t * NL + h * P, P, r, r + 64), start=True, stop=True)
                    mm = pe.matmul(c.bank(b + 2, P, h * P), kw, c.ONES[r:r + 64, :], start=True, stop=True)
                mm.then_inc(s["ds"], 1)

        @block.scalar
        def _(act):
            for n in range(NCH):
                act.wait_ge(s["out"], n + 1)
                for z, name in ((0, "OB"), (1, "KB")):
                    ins = act.activation(heads(c, name, n * CHUNK, CHUNK),
                                         c.bank(3 * (n % 2), 256, z * 256).rearrange("p (h t) -> p h t", t=64), ACT.Copy)
                ins.then_inc(s["ob"], 1)

        @block.vector
        def _(dve):
            dve.memset(c.a(ST, 8 * P), 0.0).then_inc(s["zero"], 1)
            dve.wait_ge(s["zero"], 1)
            for n in range(NCH):
                b = 3 * (n % 2)
                dve.wait_ge(s["ds"], n + 1)
                for z in range(2):
                    for h in range(NH2):
                        st = c.a(ST + (z * 4 + h) * P, P)
                        dve.scalar_tensor_tensor(st, st, c.a(o["SMALL"] + 64 + h * NCH + n, 1), c.bank(b + 1 + z, P, h * P),
                                                 ALU.mult, ALU.add).then_inc(s["state"], 1)
                dve.wait_ge(s["state"], 8 * n + 8)
    with phase(c, "own") as (s, block):
        @block.vector
        def _(dve):
            link = Chain(dve, s["own"])
            den, num, floor = c.a(o["KB"], TW), c.a(o["OB"], TW), c.a(o["FLOOR"], TW)
            link(dve.scalar_tensor_tensor(den, den, -1.0, den, ALU.mult, ALU.max))
            link(dve.tensor_tensor(den, den, floor, ALU.max))
            link(dve.reciprocal(den, den))
            link(dve.tensor_tensor(num, num, den, ALU.mult))


def after(c, args, weights_kt, rhs, gain, dst=None, bias=None):
    dst = dst or c.h

    def scalar(act, i, m, acc, s):
        h, free = dst(4 * i + m, 0, NL), s["free"][m]
        if bias is None:
            act.activation(h, acc, ACT.Copy).then_inc(free, 1)
        else:
            act.activation(h, acc, ACT.Identity, bias=c.vec(bias, 4 * i + m)).then_inc(free, 1)
    linear(c, args, rhs, weights_kt, KT, NL, scalar)

    def add(dve, scaled, own):
        dve.wait_ge(scaled, KT)
        for k in range(KT):
            dve.tensor_tensor(c.x(k), c.x(k), dst(k, 0, NL), ALU.add)
    norm(c, dst, dst, KT, D, NL, lambda k, q: c.vec(gain, k), post=add)


def ffn2(c, args, l):
    plain_norm(c, f"gain{l}2")
    RE = 32 * NL

    def scalar(act, i, m, acc, s):
        act.wait_ge(s["free"][m], i + 1)
        act.activation(c.a(RE + m * NL, NL), acc, ACT.Relu).then_inc(s["relu"], 1)

    def vector(dve, i, m, acc, s):
        dve.wait_ge(s["relu"], 4 * i + m + 1)
        dve.tensor_tensor(c.a((4 * i + m) * NL, NL), acc, c.a(RE + m * NL, NL), ALU.mult).then_inc(s["free"][m], 1)
    linear(c, args, c.h, KT, 32, NL, scalar, vector, ("relu",))


def gated_embedding(c, args, l):
    WP, PL, SG = 0, 2 * D, 2 * D + 2 * NL
    with phase(c, "dma", "sums", "copied") as (s, block):
        @block.sync
        def _(sp):
            load(sp, s["dma"], (c.a(WP, 2 * D), args["wple"][l]), (c.a(PL, 2 * NL), args["ple"][l]))

        @block.tensor
        def _(pe):
            pe.wait_ge(s["dma"], 32)
            for m in range(KT):
                for k in range(2):
                    mm = pe.matmul(c.bank(m), c.a(WP + k * D + m * P, P), c.a(PL + k * NL, NL), start=(k == 0), stop=(k == 1))
                mm.then_inc(s["sums"], 1)

        @block.vector
        def _(dve):
            for m in range(KT):
                dve.wait_ge(s["sums"], m + 1)
                dve.tensor_copy(c.h(m), c.bank(m)).then_inc(s["copied"], 1)

    def scalar(act, i, m, acc, s):
        act.wait_ge(s["free"][m], i + 1)
        act.activation(c.a(SG + m * NL, NL), acc, ACT.Sigmoid).then_inc(s["sig"], 1)

    def vector(dve, i, m, acc, s):
        h = c.h(4 * i + m)
        dve.wait_ge(s["sig"], 4 * i + m + 1)
        dve.tensor_tensor(h, h, c.a(SG + m * NL, NL), ALU.mult).then_inc(s["prod"], 1)
        dve.wait_ge(s["prod"], 4 * i + m + 1)
        dve.tensor_tensor(h, h, c.x(4 * i + m), ALU.add).then_inc(s["free"][m], 1)
    linear(c, args, c.x, KT, KT, NL, scalar, vector, ("sig", "prod"))
    c.X, c.H = c.H, c.X


A3 = {}
_at = 0
for _name, _n in (("Q", 8 * NL), ("K", 2 * (NL + P)), ("V", 5 * 256), ("COS", NL), ("SIN", NL), ("SWAP", P), ("MASK", 4 * 2 * WIN),
                  ("VBIAS", 256), ("S", 2 * 4 * 2 * WIN), ("PT", 2 * 4 * 2 * WIN), ("ST", 64), ("T", 4 * NL)):
    A3[_name] = _at
    _at += _n


def positions(c, args):
    o = A3
    T = o["T"]
    two_pi = 2 * np.pi
    c1 = 6.28125
    c2 = float(np.float32(np.floor((two_pi - c1) * 2 ** 21) / 2 ** 21))
    c3 = float(two_pi - c1 - c2)
    magic = float(1.5 * 2 ** 23)
    with phase(c, "dma", "own", "sin") as (s, block):
        @block.sync
        def _(sp):
            load(sp, s["dma"], (c.a(o["SWAP"], P), const(args, "swap32")), (c.a(o["MASK"], 1024), const(args, "window")),
                 (c.a(o["VBIAS"], 256, 0, 1), args["v_bias"]),
                 (c.a(T, NL).bitcast(I32), args["positions"]))

        @block.vector
        def _(dve):
            link = Chain(dve, s["own"])
            ang, k, t = (c.a(T + j * NL, NL) for j in (1, 2, 3))
            dve.wait_ge(s["dma"], 64)
            link(dve.tensor_copy(ang, c.a(T, NL).bitcast(I32)))
            link(dve.tensor_scalar(ang, ang, c.vec("inv_freq"), None, ALU.mult))
            link(dve.tensor_scalar(k, ang, 1.0 / two_pi, magic, ALU.mult, ALU.add))
            link(dve.tensor_scalar(k, k, magic, None, ALU.subtract))
            for part in (c1, c2, c3):
                link(dve.scalar_tensor_tensor(ang, k, -part, ang, ALU.mult, ALU.add))
            link(dve.tensor_scalar(ang, ang, 3.141592, -3.141592, ALU.min, ALU.max))
            link(dve.scalar_tensor_tensor(t, ang, -1.0, ang, ALU.mult, ALU.min))
            link(dve.tensor_scalar(t, t, float(np.pi / 2), None, ALU.add))
            dve.wait_ge(s["sin"], 2)
            link(dve.tensor_scalar(c.a(o["SIN"], NL), c.a(o["SIN"], NL), c.vec("sign"), None, ALU.mult))
            for g in range(2):
                link(dve.memset(c.a(o["K"] + g * (NL + P), P), 0.0))
            link(dve.memset(c.a(o["V"], 256), 0.0))

        @block.scalar
        def _(act):
            act.wait_ge(s["own"], 10)
            act.activation(c.a(o["SIN"], NL), c.a(T + NL, NL), ACT.Sin).then_inc(s["sin"], 1)
            act.activation(c.a(o["COS"], NL), c.a(T + 3 * NL, NL), ACT.Sin).then_inc(s["sin"], 1)


def project_c(c, args):
    o = A3

    def place(j):
        return o["Q"] + j * NL if j < 8 else o["K"] + (j - 8) * (NL + P) + P

    def scalar(act, i, m, acc, s):
        act.activation(c.a(place(4 * i + m), NL), acc, ACT.Identity, bias=c.vec("b_qkv", 4 * i + m))\
            .then_inc(s["free"][m], 1)
    linear(c, args, c.h, KT, 8, NL, scalar)

    with phase(c, "k", "k_out", "v", "out") as (s, block):
        @block.sync
        def _(sp):
            prefetch(c, sp, args["stream"], SLOTS)

        @block.tensor
        def _(pe):
            for m in range(SLOTS):
                pe.wait_ge(c.filled[m], 16 * (c.at // SLOTS + 1))
            for m in range(2):
                for k in range(KT):
                    mm = pe.matmul(c.bank(4 + m), c.block(m, k), c.h(k), start=(k == 0), stop=(k == KT - 1))
                mm.then_inc(c.units_done, 1)
            ring = c.RING[:].rearrange("p (s k n) -> p s k n", s=SLOTS, k=UB)
            for t in range(4):
                for k in range(KT):
                    pe.matmul(c.bank(t, 256).rearrange("p (s q) -> p s q", q=P), c.h(k, t * P, P), ring[:, 2:4, k, :],
                              start=(k == 0), stop=False)
                pe.matmul(c.bank(t, 256), c.ONES[0:1, :], c.a(o["VBIAS"], 256, 0, 1), start=False, stop=True).then_inc(s["v"], 1)
            for m in range(2):
                pe.matmul(c.bank(6, 2), c.block(2 + m, 0), c.h(0, 0, 2), start=True, stop=True).then_inc(c.units_done, 1)

        @block.scalar
        def _(act):
            for m in range(2):
                act.wait_ge(c.units_done, c.at + m + 1)
                act.activation(c.a(place(8 + m), NL), c.bank(4 + m), ACT.Identity, bias=c.vec("b_qkv", 8 + m)).then_inc(s["k_out"], 1)

        @block.vector
        def _(dve):
            for t in range(4):
                dve.wait_ge(s["v"], t + 1)
                dve.tensor_copy(c.a(o["V"] + (t + 1) * 256, 256), c.bank(t, 256)).then_inc(s["out"], 1)
    c.at += SLOTS

    with phase(c, "swapped", "sined", "own", "done") as (s, block):
        @block.tensor
        def _(pe):
            for j in range(10):
                if j >= 8:
                    pe.wait_ge(s["sined"], j - 7)
                pe.matmul(c.bank(j % 8), c.a(o["SWAP"], P), c.a(place(j), NL), start=True, stop=True).then_inc(s["swapped"], 1)

        @block.vector
        def _(dve):
            for j in range(10):
                x, t = c.a(place(j), NL), c.a(o["T"] + (j % 4) * NL, NL)
                dve.wait_ge(s["swapped"], j + 1)
                dve.tensor_tensor(t, c.bank(j % 8), c.a(o["SIN"], NL), ALU.mult).then_inc(s["sined"], 1)
                dve.tensor_tensor(x, x, c.a(o["COS"], NL), ALU.mult).then_inc(s["own"], 1)
                dve.wait_ge(s["sined"], j + 1)
                dve.wait_ge(s["own"], j + 1)
                dve.tensor_tensor(x, x, t, ALU.add).then_inc(s["done"], 1)


def attention2(c):
    o = A3
    scale = float(HD2 ** -0.5)
    NK = 4 * 2 * WIN
    S, PT, ST = o["S"], o["PT"], o["ST"]
    col = lambda r, a: ST + 4 * (2 * r + a % 2)
    MAX, NEG, SUM, SINK, REC = range(5)
    sink_of = [h for g in range(2) for j in range(4) for h in (8 * g + j, 8 * g + 4 + j)]
    with phase(c, "scores", "masked", "neg", "sink", "probs", "normed", "turned", "pt_a", "pt_v", "o", "o_out", "own") as (s, block):

        @block.tensor
        def _(pe):
            def score(a):
                t, r = a // 2, 64 * (a % 2)
                if a >= 2:
                    pe.wait_ge(s["masked"], a - 1)
                for j in range(4):
                    mm = pe.matmul(c.PS[:, (a % 2) * 1024 + j * 256:(a % 2) * 1024 + j * 256 + 256],
                                   c.a(o["Q"] + t * NL + j * P, P, r, r + 64),
                                   c.a(o["K"] + (t // 4) * (NL + P) + j * P, 2 * WIN, r, r + 64), start=True, stop=True)
                mm.then_inc(s["scores"], 1)

            def turn(a):
                pe.wait_ge(s["normed"], a + 1)
                if a:
                    pe.wait_ge(s["pt_a"], a)
                    pe.wait_ge(s["pt_v"], a)
                for j in range(8):
                    mm = pe.transpose(c.PS[:, 2048 + j * P:2048 + j * P + P], c.a(S + (a % 2) * NK + j * P, P), c.ID[:])
                mm.then_inc(s["turned"], 1)

            def values(a):
                t, r = a // 2, 64 * (a % 2)
                pe.wait_ge(s["pt_a"], a + 1)
                pe.wait_ge(s["pt_v"], a + 1)
                if a >= 2:
                    pe.wait_ge(s["o_out"], a - 1)
                kv = 2 * (t // 4) + a % 2
                for j in range(4):
                    for z in range(2):
                        mm = pe.matmul(c.bank(6 + a % 2, P, j * P, r, r + 64), c.a(o["V"] + (j + z) * 256 + kv * 64, 64),
                                       c.a(PT + (a % 2) * NK + (2 * j + z) * P, P), start=(z == 0), stop=(z == 1))
                mm.then_inc(s["o"], 1)

            for a in range(NQH + 2):
                if a < NQH:
                    score(a)
                if 1 <= a <= NQH:
                    turn(a - 1)
                if a >= 2:
                    values(a - 2)

        @block.scalar
        def _(act):
            for a in range(NQH + 3):
                if a < NQH:
                    act.wait_ge(s["neg"], a + 1)
                    act.activation(c.a(col(SINK, a), 4), c.a(col(NEG, a), 4), ACT.Exp, bias=c.vec("sink", sink_of[a])).then_inc(s["sink"], 1)
                    for j in range(4):
                        x = c.a(S + (a % 2) * NK + j * 256, 256)
                        ins = act.activation(x, x, ACT.Exp, bias=c.a(col(NEG, a) + j, 1), accum_out=c.a(col(SUM, a) + j, 1))
                        ins.then_inc(s["probs"], 1)
                if 1 <= a <= NQH:
                    act.wait_ge(s["turned"], a)
                    if a >= 3:
                        act.wait_ge(s["o"], a - 2)
                    act.activation(c.a(PT + ((a - 1) % 2) * NK, 512), c.bank(4), ACT.Copy).then_inc(s["pt_a"], 1)
                if a >= 3:
                    b = a - 3
                    r = 64 * (b % 2)
                    act.wait_ge(s["o"], b + 1)
                    x = c.H[r:r + 64, (b // 2) * W:(b // 2) * W + NL]
                    act.activation(x, c.bank(6 + b % 2, p0=r, p1=r + 64), ACT.Copy).then_inc(s["o_out"], 1)

        @block.vector
        def _(dve):
            link = Chain(dve, s["own"])
            for a in range(NQH + 1):
                if a < NQH:
                    x = c.a(S + (a % 2) * NK, NK)
                    dve.wait_ge(s["scores"], a + 1)
                    if a >= 2:
                        dve.wait_ge(s["turned"], a - 1)
                    dve.scalar_tensor_tensor(x, c.PS[:, (a % 2) * 1024:(a % 2) * 1024 + NK], scale, c.a(o["MASK"], NK),
                                             ALU.mult, ALU.add).then_inc(s["masked"], 1)
                    dve.wait_ge(s["masked"], a + 1)
                    m = c.a(col(MAX, a), 4)
                    link(dve.tensor_reduce(m, x.rearrange("p (j k) -> p j k", j=4), AX, ALU.max))
                    dve.tensor_scalar(c.a(col(NEG, a), 4), m, c.vec("sink", sink_of[a]), -1.0, ALU.max, ALU.mult).then_inc(s["neg"], 1)
                if a:
                    dve.wait_ge(s["turned"], a)
                    if a >= 3:
                        dve.wait_ge(s["o"], a - 2)
                    dve.tensor_copy(c.a(PT + ((a - 1) % 2) * NK + 512, 512), c.bank(5)).then_inc(s["pt_v"], 1)
                if a < NQH:
                    dve.wait_ge(s["probs"], 4 * a + 4)
                    dve.wait_ge(s["sink"], a + 1)
                    den, rec = c.a(col(SUM, a), 4), c.a(col(REC, a), 4)
                    link(dve.tensor_tensor(den, den, c.a(col(SINK, a), 4), ALU.add))
                    link(dve.reciprocal(rec, den))
                    for j in range(4):
                        x = c.a(S + (a % 2) * NK + j * 256, 256)
                        ins = dve.tensor_scalar(x, x, c.a(col(REC, a) + j, 1), None, ALU.mult)
                    ins.then_inc(s["normed"], 1)


def block2(c, args):
    o = A2
    tile = lambda name, h: c.a(o[name] + h * NL, NL)
    plain_norm(c, "gain00")
    gate_rows(c, args)
    gate_columns(c)
    project_a(c, args)
    unit_norms(c, [tile("Q", h) for h in range(NH2)] + [tile("K", h) for h in range(NH2)],
               [(float(P), float(P) * EPS)] * NH2 + [(1.0, EPS)] * NH2)
    delta_inner(c, args)
    delta_scan(c)
    unit_norms(c, [tile("OA", h) for h in range(NH2)], [(1.0 / P, EPS)] * NH2, gain=lambda h: c.vec("norm_a"),
               times=[tile("Z", h) for h in range(NH2)])
    project_b(c, args)
    mlstm_inner(c)
    mlstm_scan(c)
    unit_norms(c, [tile("OB", h) for h in range(NH2)], [(1.0 / P, EPS)] * NH2, gain=lambda h: c.vec("norm_b", h),
               times=[tile("Z", h) for h in range(NH2)])
    after(c, args, KT, lambda k, lo, n: c.a(o["OA"] + k * NL + lo, n), "gain01")
    ffn2(c, args, 0)
    after(c, args, 32, hid(c, NL), "gain03")
    gated_embedding(c, args, 0)
    plain_norm(c, "gain10")
    positions(c, args)
    project_c(c, args)
    attention2(c)
    after(c, args, KT, c.h, "gain11", dst=lambda k, lo, n: c.a(k * NL + lo, n), bias="b_o")
    ffn2(c, args, 1)
    after(c, args, 32, hid(c, NL), "gain13")
    gated_embedding(c, args, 1)


def block1(c, args):
    for l in range(DEPTH):
        n = W if l == 0 else NL
        pr = A1["PROJ"]
        modulated_norm(c, l, f"g_mix{l}", 0, W)
        in_proj(c, args, l)
        load_mixer(c, args, l)
        cq = lambda k, lo, m: c.a(pr + (2 + k) * W + lo, m)
        ckv = lambda k, lo, m: c.a(pr + 5 * W + lo, m)
        norm(c, cq, cq, 3, QRANK, n, lambda k, q: c.vec(f"g_q{l}", k))
        norm(c, ckv, ckv, 1, KVRANK, W, lambda k, q: c.vec(f"g_kv{l}"))
        fourier(c, args, l)
        key_rope(c)
        for g in range(3):
            heads_qk(c, l, g)
            attention1(c, l, g)
        linear(c, args, c.h, KT, KT, n, vector=residual(c, l, 2, n))
        modulated_norm(c, l, f"g_ffn{l}", 3, n)
        ffn_up(c, args, l, n)
        linear(c, args, hid(c), FT1, KT, n, vector=residual(c, l, 5, n))
    plain_norm(c, "g_final")
    c.X, c.H = c.H, c.X


def store(c, args, name):
    with phase(c, "out") as (s, block):
        @block.sync
        def _(sp):
            sp.dma_start(args[name].rearrange("p (k n) -> p k n", k=KT),
                         c.X[:].rearrange("p (k n) -> p k n", k=KT)[:, :, 0:NL]).then_inc(s["out"], 16)
            sp.wait_ge(s["out"], 16)


def build(nc, args, total_units):
    with ExitStack() as stack:
        c = Core(nc, stack, total_units)
        start(c, args)
        ada(c, args)
        block1(c, args)
        block2(c, args)
        store(c, args, "out_dram")


def lay_out(x, c, ctx, c_ctx, w_ada, b_ada, g_mix, w_in, w_fourier, b_fourier, g_q_a, w_q_b, g_kv_a, w_kv_b, w_out,
            g_ffn, w_up, w_dw, b_dw, w_down, g_final, p_2, positions_2, norm_gains_2, w_in_ab_2, conv_a_2, a_log_2,
            dt_bias_2, norm_a_2, i_bias_b_2, f_bias_b_2, norm_b_2, w_out_ab_2, w_qkv_c_2, b_qkv_c_2, sinks_c_2, w_o_c_2,
            b_o_c_2, w_up_2, w_down_2, w_ple_2, w_ple_gate_2):
    x, ctx = np.asarray(x), np.asarray(ctx)
    x_in = np.concatenate([x[0], ctx[0]], 0).T
    vecs = np.zeros((P, NV), np.float32)

    def put(name, v):
        v = np.asarray(v)
        if v.ndim == 1:
            v = v.reshape(-1, P).T
        vecs[:v.shape[0], COL[name]:COL[name] + v.shape[1]] = v

    cc = np.stack([np.asarray(c)[0], np.asarray(c_ctx)], 1)
    put("c", tiles(cc))
    for l in range(DEPTH):
        for name, v in (("g_mix", g_mix), ("g_ffn", g_ffn), ("b_ada", b_ada), ("b_four", b_fourier), ("g_q", g_q_a),
                        ("g_kv", g_kv_a), ("b_dw", b_dw)):
            put(f"{name}{l}", np.asarray(v)[l])
        for k in range(3):
            put(f"dw{k}_{l}", np.asarray(w_dw)[l, k])
    put("g_final", g_final)
    for l in range(2):
        for i in range(4):
            put(f"gain{l}{i}", np.asarray(norm_gains_2)[l, i])
    for k in range(4):
        put(f"conv{k}", np.asarray(conv_a_2)[0, k])
    put("norm_a", np.asarray(norm_a_2)[0])
    put("norm_b", np.asarray(norm_b_2)[0].reshape(-1))
    heads = [h for g in range(2) for j in range(4) for h in (8 * g + j, 8 * g + 4 + j)]
    q_cols = [(h * HD2, h * HD2 + HD2) for h in heads]
    bq = np.asarray(b_qkv_c_2)[0]
    put("b_qkv", np.concatenate([bq[a:b] for a, b in q_cols] + [bq[1024:1280]]))
    put("b_o", np.asarray(b_o_c_2)[0])
    put("sink", np.broadcast_to(np.asarray(sinks_c_2)[0], (P, NQH)))
    put("inv_freq", np.tile(INV32, 4))
    put("sign", np.where(np.arange(P) % 64 < 32, np.float32(-1), np.float32(1)))
    put("rowb", np.stack([np.asarray(v)[0] for v in (a_log_2, dt_bias_2, i_bias_b_2, f_bias_b_2)], 1))

    w_ada, w_in, w_out, w_up, w_down = (np.asarray(v) for v in (w_ada, w_in, w_out, w_up, w_down))
    stream = [units(w_ada[l]) for l in range(DEPTH)]
    for l in range(DEPTH):
        stream += [units(w_in[l]), np.zeros((1, P, UB * P), np.float32), units(w_out[l]),
                   units(w_up[l], [(o + j * P, o + j * P + P) for j in range(FT1) for o in (0, DFF)]), units(w_down[l])]
    wab = np.asarray(w_in_ab_2)[0]
    A0, B0 = 0, 2056
    stream += [units(wab, [(0, 1536), (A0 + 1544, A0 + 2056)]),
               units(wab, [(B0, B0 + 1024), (B0 + 1544, B0 + 2056), (B0 + 1024, B0 + 1536)]), units(np.asarray(w_out_ab_2)[0]),
               units(np.asarray(w_up_2)[0]), units(np.asarray(w_down_2)[0]), units(np.asarray(w_ple_gate_2)[0])]
    w_o = np.asarray(w_o_c_2)[0]
    stream += [units(np.asarray(w_qkv_c_2)[0], q_cols + [(1024, 1536)]),
               units(np.concatenate([w_o[a:b] for a, b in q_cols], 0)),
               units(np.asarray(w_up_2)[1]), units(np.asarray(w_down_2)[1]), units(np.asarray(w_ple_gate_2)[1])]
    stream = np.concatenate(stream, 0)
    assert len(stream) == sum(n for _, n in stages())

    wq = np.asarray(w_q_b).reshape(DEPTH, QRANK, NHEAD, 96)
    wq = np.concatenate([wq[..., :64].reshape(DEPTH, QRANK, -1), wq[..., 64:].reshape(DEPTH, QRANK, -1)], -1)
    wkv = np.asarray(w_kv_b).reshape(DEPTH, KVRANK, NHEAD, 128)
    wkv = np.concatenate([wkv[..., :64].reshape(DEPTH, KVRANK, -1), wkv[..., 64:].reshape(DEPTH, KVRANK, -1)], -1)
    gates = np.zeros((D, P), np.float32)
    for i, o in enumerate((A0 + 1536, A0 + 1540, B0 + 1536, B0 + 1540)):
        gates[:, 32 * i:32 * i + 4] = wab[:, o:o + 4]
    brow = np.zeros((1, 256), np.float32)
    brow[0] = bq[1280:1536]
    return {
        "x_in": tiles(x_in), "vecs": vecs, "stream": stream, "consts": CONST,
        "wq": np.stack([tiles(wq[l]) for l in range(DEPTH)]), "wkv": wkv,
        "wf": np.stack([tiles(np.asarray(w_fourier)[l]) for l in range(DEPTH)]),
        "gates": tiles(gates), "v_bias": brow,
        "wple": np.stack([tiles(np.asarray(w_ple_2)[l]) for l in range(2)]),
        "ple": np.stack([tiles(np.asarray(p_2)[l, 0].T) for l in range(2)]),
        "positions": np.ascontiguousarray(np.broadcast_to(np.asarray(positions_2), (P, NL))),
    }


def kernel(**inputs):
    import concourse.bacc as bacc
    from concourse.bass_utils import run_bass_kernel_spmd

    arrays = {f"in_{k}": np.ascontiguousarray(v) for k, v in lay_out(**inputs).items()}
    nc = bacc.Bacc("TRN2", target_bir_lowering=False, num_devices=1)
    args = {k[3:]: nc.dram_tensor(k, a.shape, mybir.dt.from_np(a.dtype), kind="ExternalInput").ap()
            for k, a in arrays.items()}
    args["out_dram"] = nc.dram_tensor("out_dram", (P, KT * NL), F32, kind="ExternalOutput").ap()
    build(nc, args, len(arrays["in_stream"]))
    r = run_bass_kernel_spmd(nc, [arrays], core_ids=[0])
    out = r.results[0]["out_dram"]
    return out.reshape(P, KT, NL).transpose(2, 1, 0).reshape(1, NL, D)
```

```python
from contextlib import ExitStack, contextmanager

import numpy as np

import concourse.bass as bass
from concourse import mybir
from concourse.alu_op_type import AluOpType as ALU

ACT = mybir.ActivationFunctionType
F32 = mybir.dt.float32
I32 = mybir.dt.int32
AX = mybir.AxisListType.X
ds = bass.ds

P = 128
D = 1024
KT = D // P
NL, NC = 512, 256
W = NL + NC
EPS = 1e-6
DEPTH = 2
NMOD = 6
NHEAD, DV1, DNOPE, DROPE = 12, 64, 64, 32
QRANK, KVRANK, FW = 384, 128, 256
SCALE1 = float((DNOPE + DROPE) ** -0.5)
DFF = 2816
FT1 = DFF // P
NH2 = 4
CHUNK = 64
NCH = NL // CHUNK
DFF2 = 4096
HD2 = 64
NQH, NKVH = 16, 4
WIN = 128
PLE = 256
SCALE2 = float(P ** -0.5)
SLOTS = 2
UB = 8
UN = UB * P
F32R = mybir.dt.float32r
ADA_SLOTS = 8


def vector_columns():
    at, n = {}, 0
    for name, cols in (
        [("c", 2 * KT)]
        + [(f"{v}{l}", m) for l in range(DEPTH) for v, m in (
            ("g_mix", KT), ("g_ffn", KT), ("b_ada", NMOD * KT), ("b_four", 2), ("g_q", 3), ("g_kv", 1),
            ("dw0_", 2 * FT1), ("dw1_", 2 * FT1), ("dw2_", 2 * FT1), ("b_dw", 2 * FT1))]
        + [("g_final", KT)]
        + [(f"gain{l}{i}", KT) for l in range(2) for i in range(4)]
        + [("conv0", 12), ("conv1", 12), ("conv2", 12), ("conv3", 12)]
        + [("norm_a", 1), ("norm_b", NH2), ("b_qkv", 12), ("b_o", KT), ("sink", NQH), ("inv_freq", 1)]
        + [("rowb", 4), ("sign", 1)]
    ):
        at[name] = n
        n += cols
    return at, n


COL, NV = vector_columns()


def shape_constants():
    parts = {}
    parts["ident"] = np.eye(P)
    n_freq = DROPE // 4
    inv = 10000.0 ** (-np.arange(n_freq, dtype=np.float32) / np.float32(n_freq))
    inv = inv.astype(np.float32)
    rows = np.repeat(np.arange(NL // 64), 64).astype(np.float32)
    cols = np.tile(np.arange(64), NL // 64).astype(np.float32)
    ang = np.concatenate([rows[:, None] * inv, cols[:, None] * inv], -1).astype(np.float32).T
    parts["cos1"] = np.tile(np.cos(ang), (8, 1))
    parts["sin1"] = np.tile(np.concatenate([-np.sin(ang), np.sin(ang)]), (4, 1))
    swap = np.zeros((P, P))
    for i in range(P):
        swap[i ^ 16, i] = 1.0
    parts["swap16"] = swap
    k = np.arange(64)
    w64 = 2 * np.pi * np.outer(k, k) % (2 * np.pi * 64) / 64
    cb = np.zeros((P, 2 * P))
    for g in range(2):
        cb[64 * g:64 * g + 64, 64 * g:64 * g + 64] = np.cos(w64) / 8
        cb[64 * g:64 * g + 64, P + 64 * g:P + 64 * g + 64] = np.sin(w64) / 8
    parts["cb"] = cb
    for name, n in (("dft", NL), ("dftc", NC)):
        i = np.arange(n)
        w = 2 * np.pi * (np.outer(i, i) % n) / n
        for s, m in (("c", np.cos(w) / np.sqrt(n)), ("s", -np.sin(w) / np.sqrt(n))):
            parts[name + s] = m.reshape(n // P, P, n).transpose(1, 0, 2).reshape(P, -1)
    e, c = np.arange(P)[:, None], np.arange(P)[None, :]
    same = e // CHUNK == c // CHUNK
    parts["causal"] = (same & (e <= c)) * 1.0
    for lv in range(6):
        b = 1 << lv
        parts[f"lv{lv}"] = ((e // (2 * b) == c // (2 * b)) & (c % (2 * b) >= b) & (e % (2 * b) < b)) * 1.0
    sel = np.zeros((P, NH2 * P))
    for h in range(NH2):
        sel[h, h * P:(h + 1) * P] = 1.0
    parts["sel"] = sel
    start = np.zeros((P, NL))
    start[:, ::CHUNK] = 1.0
    parts["keep"] = 1.0 - start
    parts["drop"] = start * -1e30
    sw = np.zeros((P, P))
    for i in range(P):
        sw[i ^ 32, i] = 1.0
    parts["swap32"] = sw
    q, s = np.arange(WIN)[:, None], np.arange(2 * WIN)[None, :]
    band = (s > q) & (s <= q + WIN)
    m = np.zeros((WIN, NL // WIN, 2 * WIN))
    for j in range(NL // WIN):
        m[:, j] = np.where(band & (j * WIN - WIN + s >= 0), 0.0, -1e30)
    parts["window"] = m.reshape(WIN, -1)
    at, n = {}, 0
    for name, a in parts.items():
        at[name] = (n, a.shape[1])
        n += a.shape[1]
    return at, np.concatenate([np.asarray(a, np.float32) for a in parts.values()], 1)


CAT, CONST = shape_constants()
INV32 = (10000.0 ** (-np.arange(32, dtype=np.float32) / np.float32(32))).astype(np.float32)


def ffn_parts(hidden_tiles):
    return [(p, min(UB, hidden_tiles - p)) for p in range(0, hidden_tiles, UB)]


def stages():
    out = []
    for l in range(DEPTH):
        out += [(f"in{l}", 8), (f"out{l}", 8)] + [(f"ffn{l}_{p}", 2 * m + 8) for p, m in ffn_parts(FT1)]
    for l, first in enumerate(([("projA", 16), ("projB", 16), ("outAB", 8)], [("qkv", 12), ("outC", 8)])):
        out += first + [(f"ffn2_{l}_{p}", m + 8) for p, m in ffn_parts(32)] + [(f"gate2_{l}", 8)]
    return out


def units(w, order=None):
    w = np.asarray(w)
    if order is not None:
        w = np.concatenate([w[:, a:b] for a, b in order], 1)
    kp, mp = -w.shape[0] % (UB * P), -w.shape[1] % P
    if kp or mp:
        full = np.zeros((w.shape[0] + kp, w.shape[1] + mp), w.dtype)
        full[:w.shape[0], :w.shape[1]] = w
        w = full
    u, m = w.shape[0] // (UB * P), w.shape[1] // P
    return w.reshape(u, UB, P, m, P).transpose(3, 0, 2, 1, 4).reshape(m * u, P, UB * P)


def tiles(a):
    a = np.asarray(a)
    return a.reshape(a.shape[0] // P, P, -1).transpose(1, 0, 2).reshape(P, -1)


class Core:

    def __init__(self, nc, stack, total_units):
        self.nc = nc
        self.total = total_units
        sb = lambda name, n, p=P, dt=F32: stack.enter_context(nc.sbuf_tensor(name, [p, n], dt))
        self.stack = stack
        self.X = sb("X", KT * W)
        self.H = sb("H", KT * W)
        self.RING = sb("RING", SLOTS * UN)
        self.WHI = sb("WHI", SLOTS * UN, dt=F32R)
        self.WLO = sb("WLO", SLOTS * UN, dt=F32R)
        self.VEC = sb("VEC", NV)
        self.MOD = sb("MOD", DEPTH * NMOD * KT * 2)
        self.ONES = sb("ONES", P)
        self.ID = sb("ID", P)
        self.RS = sb("RS", W)
        self.MS = sb("MS", W)
        self.SQ = sb("SQ", 2 * W)
        self.AV = sb("AV", 2 * KT)
        self.low = self.high = None
        self.border = 0
        self.rooms = 0
        self.PS = stack.enter_context(nc.psum_tensor("PS", [P, 8 * 512], F32))
        sem = lambda name: stack.enter_context(nc.semaphore(name))
        self.filled = [sem(f"ring_filled{i}") for i in range(SLOTS)]
        self.w_hi = sem("w_hi")
        self.w_lo = sem("w_lo")
        self.units_done = sem("units_done")
        self.at = 0
        self.pool = [stack.enter_context(nc.semaphore(f"phase{i}")) for i in range(40)]

    @contextmanager
    def room(self, n, dt=F32):
        self.rooms += 1
        with self.nc.sbuf_tensor(f"room{self.rooms}", [P, n], dt) as t:
            yield t

    @contextmanager
    def low_room(self, n):
        with self.room(n) as t:
            self.low, self.border = t, n
            yield
        self.low, self.border = None, 0

    @contextmanager
    def high_room(self, n):
        with self.room(n) as t:
            self.high = t
            yield
        self.high = None

    @contextmanager
    def pair(self, n):
        with self.room(KT * n, F32R) as hi, self.room(KT * n, F32R) as lo:
            yield (hi, lo, n)

    def bank(self, b, n=512, lo=0, p0=0, p1=P):
        return self.PS[p0:p1, 512 * b + lo:512 * b + lo + n]

    def x(self, k, lo=0, n=NL):
        return self.X[:, ds(k * W + lo, n)] if not isinstance(k, int) else self.X[:, k * W + lo:k * W + lo + n]

    def h(self, k, lo=0, n=NL):
        return self.H[:, ds(k * W + lo, n)] if not isinstance(k, int) else self.H[:, k * W + lo:k * W + lo + n]

    def vec(self, name, j=0, n=1):
        a = COL[name] + j
        return self.VEC[:, a:a + n] if isinstance(j, int) else self.VEC[:, ds(a, n)]

    def a(self, lo, n, p0=0, p1=P):
        if not isinstance(lo, int):
            return self.low[p0:p1, ds(lo, n)]
        if lo < self.border:
            assert lo + n <= self.border
            return self.low[p0:p1, lo:lo + n]
        return self.high[p0:p1, lo - self.border:lo - self.border + n]


@contextmanager
def phase(c, *names, **groups):
    wanted = [(name, None) for name in names] + list(groups.items())
    found, at = {}, 0
    for name, n in wanted:
        found[name] = c.pool[at] if n is None else c.pool[at:at + n]
        at += n or 1
    with c.nc.Block() as block:
        yield found, block
    c.nc.all_engine_barrier(sems_to_clear=range(c.pool[0].num, c.pool[-1].num + 1))


class Chain:

    def __init__(self, eng, sem):
        self.eng, self.sem, self.n = eng, sem, 0

    def __call__(self, ins):
        self.n += 1
        ins.then_inc(self.sem, 1)
        self.eng.wait_ge(self.sem, self.n)


def loop(eng, n, body, peel=0):
    rolled = n - peel if n - peel >= 3 else 0
    if rolled:
        with eng.Fori(0, rolled) as i:
            body(i)
    for i in range(rolled, n):
        body(i)


def fetch(c, sp, stream, u):
    slot = u % SLOTS if isinstance(u, int) else None
    sp.dma_start(c.RING[:, slot * UN:(slot + 1) * UN], stream[u]).then_inc(c.filled[slot], 16)


def split_hi(c, act, u, slot):
    act.wait_ge(c.filled[slot], 16 * (u // SLOTS + 1) if isinstance(u, int) else u * 8 + (16 - 8 * slot))
    act.activation(c.WHI[:, slot * UN:(slot + 1) * UN], c.RING[:, slot * UN:(slot + 1) * UN], ACT.Copy).then_inc(c.w_hi, 1)


def split_lo(c, dve, u, slot):
    dve.wait_ge(c.w_hi, u + 1)
    w = slice(slot * UN, (slot + 1) * UN)
    dve.tensor_tensor(c.WLO[:, w], c.RING[:, w], c.WHI[:, w].bitcast(F32), ALU.subtract).then_inc(c.w_lo, 1)


def start(c, args):
    with phase(c, "dma", "ones") as (s, block):

        @block.sync
        def _(sp):
            sp.dma_start(c.VEC[:], args["vecs"]).then_inc(s["dma"], 16)
            for u in range(SLOTS):
                fetch(c, sp, args["stream"], u)
            sp.dma_start(c.ID[:], args["consts"][:, CAT["ident"][0]:CAT["ident"][0] + P]).then_inc(s["dma"], 16)
            sp.dma_start(c.X[:], args["x_in"]).then_inc(s["dma"], 16)
            for u in range(SLOTS):
                sp.wait_ge(c.w_lo, u + 1)
                fetch(c, sp, args["stream"], u + SLOTS)
            sp.wait_ge(s["dma"], 48)

        @block.scalar
        def _(act):
            for u in range(SLOTS):
                split_hi(c, act, u, u)

        @block.vector
        def _(dve):
            dve.memset(c.ONES[:], 1.0).then_inc(s["ones"], 1)
            dve.wait_ge(s["ones"], 1)
            for u in range(SLOTS):
                split_lo(c, dve, u, u)


def ada(c, args):
    groups = NMOD * D // UN
    n = DEPTH * groups * KT
    tiles_l = NMOD * KT
    with phase(c, "silu", "summed", "row_out", "turned", "sums", "done", filled=ADA_SLOTS) as (s, block), \
            c.room(ADA_SLOTS * UN) as ring, c.room(2 * KT) as sc, c.room(NMOD * D) as rows:
        slot = lambda j: ring[:, j * UN:(j + 1) * UN]

        @block.sync
        def _(sp):
            for j in range(ADA_SLOTS):
                sp.dma_start(slot(j), args["w_ada"][j]).then_inc(s["filled"][j], 16)
            with sp.Fori(0, n // ADA_SLOTS - 1) as i:
                for j in range(ADA_SLOTS):
                    sp.wait_ge(s["done"], ADA_SLOTS * i + j + 1)
                    sp.dma_start(slot(j), args["w_ada"][ds(ADA_SLOTS * i + ADA_SLOTS + j, 1)]
                                 .rearrange("a p n -> p (a n)")).then_inc(s["filled"][j], 16)

        @block.scalar
        def _(act):
            act.activation(sc[:], c.vec("c", 0, 2 * KT), ACT.Silu).then_inc(s["silu"], 1)
            for g in range(DEPTH * groups):
                act.wait_ge(s["done"], KT * (g + 1))
                if g == groups:
                    act.wait_ge(s["turned"], 1)
                act.activation(rows[0:2, (g % groups) * UN:(g % groups + 1) * UN], c.PS[0:2, 1024 * (g % 2):1024 * (g % 2) + UN],
                               ACT.Copy).then_inc(s["row_out"], 1)

        @block.tensor
        def _(pe):
            pe.wait_ge(s["silu"], 1)
            for g in range(DEPTH * groups):
                if g >= 2:
                    pe.wait_ge(s["row_out"], g - 1)
                for k in range(KT):
                    pe.wait_ge(s["filled"][k], 16 * (g + 1))
                    for h in range(2):
                        mm = pe.matmul(c.bank(2 * (g % 2) + h, p1=2), sc[:, 2 * k:2 * k + 2],
                                       ring[:, k * UN + 512 * h:k * UN + 512 * h + 512], start=(k == 0), stop=(k == KT - 1))
                    mm.then_inc(s["done"], 1)
                if g % groups == groups - 1:
                    pe.wait_ge(s["row_out"], g + 1)
                    l = g // groups
                    for m in range(tiles_l):
                        mm = pe.matmul(c.bank(4 + l, 2, 2 * m), rows[0:2, m * P:(m + 1) * P], c.ID[0:2, 0:2], start=True, stop=True)
                    mm.then_inc(s["turned"], 1)

        @block.vector
        def _(dve):
            for l in range(DEPTH):
                dve.wait_ge(s["turned"], l + 1)
                b = c.vec(f"b_ada{l}", 0, tiles_l).rearrange("p (m a) -> p m a", a=1).broadcast_to([P, tiles_l, 2])
                dve.tensor_tensor(c.MOD[:, l * 2 * tiles_l:(l + 1) * 2 * tiles_l].rearrange("p (m a) -> p m a", a=2),
                                  c.bank(4 + l, 2 * tiles_l).rearrange("p (m a) -> p m a", a=2),
                                  b, ALU.add).then_inc(s["sums"], 1)


def mod(c, l, part, k, cond):
    o = l * 2 * NMOD * KT
    j = o + 2 * (part * KT + k) + cond
    return c.MOD[:, j:j + 1] if isinstance(k, int) else c.MOD[:, ds(j, 1)]


def norm(c, src, out, nk, size, n, gain, shift=None, scale_prep=None, post=None):
    parts = [(0, 0, min(n, NL))] + ([(1, NL, n - NL)] if n > NL else [])
    with phase(c, "squared", "summed", "mean", "root", "scaled", "own", "prep") as (s, block):

        @block.scalar
        def _(act):
            for k in range(nk):
                if k >= 2:
                    act.wait_ge(s["summed"], k - 1)
                act.activation(c.SQ[:, (k % 2) * W:(k % 2) * W + n], src(k, 0, n), ACT.Square).then_inc(s["squared"], 1)
            act.wait_ge(s["mean"], 1)
            act.activation(c.RS[:, 0:n], c.MS[:, 0:n], ACT.Sqrt).then_inc(s["root"], 1)
            if shift is not None:
                for k in range(nk):
                    act.wait_ge(s["scaled"], (k + 1) * len(parts))
                    for q, lo, m in parts:
                        o = out(k, lo, m)
                        act.activation(o, o, ACT.Identity, bias=shift(k, q))

        @block.tensor
        def _(pe):
            for k in range(nk):
                pe.wait_ge(s["squared"], k + 1)
                for q, lo, m in parts:
                    mm = pe.matmul(c.PS[:, lo:lo + m], c.ONES[:], c.SQ[:, (k % 2) * W + lo:(k % 2) * W + lo + m],
                                   start=(k == 0), stop=(k == nk - 1))
                mm.then_inc(s["summed"], 1)

        @block.vector
        def _(dve):
            if scale_prep is not None:
                scale_prep(dve, s["prep"])
            dve.wait_ge(s["summed"], nk)
            dve.tensor_scalar(c.MS[:, 0:n], c.PS[:, 0:n], 1.0 / size, EPS, ALU.mult, ALU.add).then_inc(s["mean"], 1)
            dve.wait_ge(s["root"], 1)
            dve.reciprocal(c.RS[:, 0:n], c.RS[:, 0:n]).then_inc(s["own"], 1)
            dve.wait_ge(s["own"], 1)
            for k in range(nk):
                for q, lo, m in parts:
                    dve.scalar_tensor_tensor(out(k, lo, m), src(k, lo, m), gain(k, q), c.RS[:, lo:lo + m],
                                             ALU.mult, ALU.mult).then_inc(s["scaled"], 1)
            if post is not None:
                post(dve, s["scaled"], s["own"])


def modulated_norm(c, l, g, part, n):
    conds = 2 if n > NL else 1

    def prep(dve, sem):
        i = 0
        for q in range(conds):
            o = l * 2 * NMOD * KT + 2 * (part + 1) * KT + q
            sc = c.MOD[:, o:o + 2 * KT - 1:2]
            a = c.AV[:, q * KT:(q + 1) * KT]
            dve.scalar_tensor_tensor(a, sc, 1.0, c.vec(g, 0, KT), ALU.add, ALU.mult).then_inc(sem, 1)
        dve.wait_ge(sem, conds)

    norm(c, c.x, c.h, KT, D, n, lambda k, q: c.AV[:, q * KT + k:q * KT + k + 1],
         lambda k, q: mod(c, l, part, k, q), prep)


def plain_norm(c, g, n=NL):
    norm(c, c.x, c.h, KT, D, n, lambda k, q: c.vec(g, k))


def linear(c, args, x, kt, n_tiles, n, scalar=None, vector=None, scalar2=None, vector2=None, extra=(), credit=None,
           width=None, peel=0, groups={}):
    base = c.at
    turns = n_tiles // 4
    source, (xh, xl, xw) = x if len(x) == 2 else (None, x)
    with phase(c, "x_hi", "x_lo", *extra, free=4, **groups) as (s, block):
        free = s["free"]

        def ahead(i, m, by):
            u = base + 4 * i + m + by
            if not isinstance(i, int):
                assert base + 4 * (turns - peel) + by <= c.total
            return u if not isinstance(i, int) or u < c.total else None

        @block.sync
        def _(sp):
            def turn(i):
                for m in range(4):
                    u = ahead(i, m, 4)
                    if u is not None:
                        sp.wait_ge(c.w_lo, base + 4 * i + m + 3)
                        src = args["stream"][u] if isinstance(u, int) else args["stream"][ds(u, 1)].rearrange("a p n -> p (a n)")
                        sp.dma_start(c.RING[:, (m % 2) * UN:(m % 2 + 1) * UN], src).then_inc(c.filled[m % 2], 16)
            loop(sp, turns, turn, peel)

        @block.tensor
        def _(pe):
            for m in range(4):
                pe.sem_inc(free[m], 1)

            def turn(i):
                for m in range(4):
                    pe.wait_ge(free[m], i + 1)
                    pe.wait_ge(c.w_lo, base + 4 * i + m + 1)
                    cols = width(4 * i + m) if width else n
                    for k in range(kt):
                        if source is not None and m == 0:
                            pe.wait_ge(s["x_lo"], k + 1)
                        w = slice((m % 2) * UN + k * P, (m % 2) * UN + k * P + P)
                        for z, (wt, xt) in enumerate(((c.WHI, xh), (c.WHI, xl), (c.WLO, xh))):
                            for b, lo, q in ((0, 0, min(cols, 512)), (1, 512, cols - 512)):
                                if q > 0:
                                    mm = pe.matmul(c.bank(2 * m + b, q), wt[:, w], xt[:, k * xw + lo:k * xw + lo + q],
                                                   start=(k == 0 and z == 0), stop=(k == kt - 1 and z == 2))
                    mm.then_inc(c.units_done, 1)
            loop(pe, turns, turn, peel)

        def evacuator(eng, take, split, then):
            def turn(i):
                for m in range(4):
                    eng.wait_ge(c.units_done, base + 4 * i + m + 1)
                    if take is not None:
                        take(eng, i, m, c.PS[:, 1024 * m:1024 * m + n], s)
                    u = ahead(i, m, 2)
                    if u is not None:
                        split(c, eng, u, m % 2)
                    if then is not None:
                        then(eng, i, m, s)
            loop(eng, turns, turn, peel)

        @block.scalar
        def _(act):
            if source is not None:
                for k in range(kt):
                    act.activation(xh[:, k * xw:k * xw + n], source(k, 0, n), ACT.Copy).then_inc(s["x_hi"], 1)
            evacuator(act, scalar, split_hi, scalar2)

        @block.vector
        def _(dve):
            if credit is not None:
                credit(dve, s)
            if source is not None:
                for k in range(kt):
                    dve.wait_ge(s["x_hi"], k + 1)
                    q = slice(k * xw, k * xw + n)
                    dve.tensor_tensor(xl[:, q], source(k, 0, n), xh[:, q].bitcast(F32), ALU.subtract).then_inc(s["x_lo"], 1)
            evacuator(dve, vector, split_lo, vector2)
    c.at += n_tiles


def residual(c, l, part, n):
    conds = [(0, 0, NL)] + ([(1, NL, NC)] if n > NL else [])

    def take(dve, i, m, acc, s):
        for q, lo, w in conds:
            x = c.x(4 * i + m, lo, w)
            ins = dve.scalar_tensor_tensor(x, acc[:, lo:lo + w], mod(c, l, part, 4 * i + m, q), x, ALU.mult, ALU.add)
        ins.then_inc(s["free"][m], 1)
    return take


def load(sp, sem, *pairs):
    for dst, src in pairs:
        sp.dma_start(dst, src).then_inc(sem, 16)
    sp.wait_ge(sem, 16 * len(pairs))


def const(args, name, p=P):
    o, n = CAT[name]
    return args["consts"][0:p, o:o + n]


def ffn_up(c, args, l, n, x, hidden, room, p0, tiles_p):
    parts = [(0, NL)] + ([(NL, NC)] if n > NL else [])
    hh, hl, hw = hidden
    cv = lambda m, lo, w: room[:, m * W + lo:m * W + lo + w]
    sg = room[:, 4 * W:4 * W + n]

    def col(name, i, m):
        j = COL[f"{name}{l}"] + (m % 2) * FT1 + p0 + 2 * i + m // 2
        return c.VEC[:, j:j + 1] if isinstance(i, int) else c.VEC[:, ds(j, 1)]

    def place(t, i, m):
        j = (2 * i + m // 2) * hw
        return t[:, j:j + n] if isinstance(i, int) else t[:, ds(j, n)]

    def scalar(act, i, m, acc, s):
        pair = 2 * i + m // 2
        act.wait_ge(s["lo"], pair + 1)
        act.activation(cv(m, 0, n), acc, ACT.Identity, bias=col("b_dw", i, m),
                       scale=col("dw1_", i, m)).then_inc(s["centre"], 1)
        if m % 2:
            act.wait_ge(s["free"][m - 1], i + 2)
            act.wait_ge(s["lo"], pair + 2)
            act.activation(sg, cv(m - 1, 0, n), ACT.Silu).then_inc(s["gate"], 1)

    def scalar2(act, i, m, s):
        if m % 2:
            act.wait_ge(s["product"], 2 * i + m // 2 + 1)
            act.activation(place(hh, i, m), sg, ACT.Copy).then_inc(s["hi"], 1)

    def vector(dve, i, m, acc, s):
        free = s["free"][m]
        dve.wait_ge(s["centre"], 4 * i + m + 1)
        for lo, w in parts:
            y = cv(m, lo + 1, w - 1)
            ins = dve.scalar_tensor_tensor(y, acc[:, lo:lo + w - 1], col("dw0_", i, m), y, ALU.mult, ALU.add)
        ins.then_inc(s["left"], 1)
        dve.wait_ge(s["left"], 4 * i + m + 1)
        for lo, w in parts:
            y = cv(m, lo, w - 1)
            ins = dve.scalar_tensor_tensor(y, acc[:, lo + 1:lo + w], col("dw2_", i, m), y, ALU.mult, ALU.add)
        ins.then_inc(free, 1)
        if m % 2:
            pair = 2 * i + m // 2
            dve.wait_ge(free, i + 2)
            dve.wait_ge(s["gate"], pair + 1)
            dve.tensor_tensor(sg, sg, cv(m, 0, n), ALU.mult).then_inc(s["product"], 1)

    def vector2(dve, i, m, s):
        if m % 2:
            dve.wait_ge(s["hi"], 2 * i + m // 2 + 1)
            dve.tensor_tensor(place(hl, i, m), sg, place(hh, i, m).bitcast(F32), ALU.subtract).then_inc(s["lo"], 1)

    linear(c, args, x, KT, 2 * tiles_p, n, scalar, vector, scalar2, vector2, ("centre", "left", "gate", "product", "hi", "lo"),
           credit=lambda dve, s: dve.sem_inc(s["lo"], 2))


def ffn1(c, args, l, n):
    with c.pair(n) as xp, c.pair(n) as hidden, c.room(5 * W) as room:
        x = (c.h, xp)
        for p, m in ffn_parts(FT1):
            ffn_up(c, args, l, n, x, hidden, room, p, m)
            x = xp
            linear(c, args, hidden, m, KT, n, vector=residual(c, l, 5, n))


A1 = {}
_at = 0
for _name, _n in (("PROJ", 7 * W), ("WQ", 3 * NHEAD * 96), ("WKV", 2 * NHEAD * 64), ("WF", 2 * FW), ("V", 6 * NHEAD * 64),
                  ("COS", NL), ("SIN", NL), ("SWAP", P), ("UNION", 0)):
    A1[_name] = _at
    _at += _n
for _first, _parts in (("UNION", (("CB", 2 * P), ("DC", 4 * NL), ("DS", 4 * NL), ("DCC", 2 * NC), ("DSC", 2 * NC),
                                  ("UV", 12 * 2 * P), ("FT", 2 * W))),
                       ("UNION", (("QT", 4 * W), ("KTT", 4 * W), ("PP", 2 * W), ("PT", 6 * W), ("QR", W), ("T1", NL),
                                  ("ST", 64)))):
    _at = A1[_first]
    for _name, _n in _parts:
        A1[_name] = _at
        _at += _n
    assert _at <= 30400, _at
A1["END"] = A1["UNION"] + 13632


def in_proj(c, args, l):
    pr = A1["PROJ"]
    nq = W if l == 0 else NL

    def width(t):
        return 2 if t == 7 else W if t >= 5 else nq

    def scalar(act, i, m, acc, s):
        t = 4 * i + m
        n, rows = width(t), DROPE if t == 6 else P
        o = c.a(pr + t * W, n, 0, rows) if t < 7 else c.MS[:, 0:2]
        act.activation(o, c.PS[0:rows, 1024 * m:1024 * m + n], ACT.Copy).then_inc(s["free"][m], 1)

    with c.pair(W) as xp:
        linear(c, args, (c.h, xp), KT, 8, W, scalar, width=width)


def load_mixer(c, args, l):
    with phase(c, "dma") as (s, block):
        @block.sync
        def _(sp):
            load(sp, s["dma"],
                 (c.a(A1["WQ"], 3 * NHEAD * 96), args["wq"][l]), (c.a(A1["WKV"], 2 * NHEAD * 64), args["wkv"][l]),
                 (c.a(A1["WF"], 2 * FW), args["wf"][l]), (c.a(A1["COS"], NL), const(args, "cos1")),
                 (c.a(A1["SIN"], NL), const(args, "sin1")), (c.a(A1["SWAP"], P), const(args, "swap16")),
                 (c.a(A1["CB"], 2 * P), const(args, "cb")), (c.a(A1["DC"], 4 * NL), const(args, "dftc")),
                 (c.a(A1["DS"], 4 * NL), const(args, "dfts")), (c.a(A1["DCC"], 2 * NC), const(args, "dftcc")),
                 (c.a(A1["DSC"], 2 * NC), const(args, "dftcs")))


def fourier(c, args, l):
    pr, uv, ft = A1["PROJ"], A1["UV"], A1["FT"]
    parts = [(0, NL, "DC", "DS", 0)] + ([(NL, NC, "DCC", "DSC", 4)] if l == 0 else [])
    tt = 6 if l == 0 else 4
    with phase(c, "channels", "uv", "v", "v_out", "positions", "ft", "mixed", "h") as (s, block):

        @block.tensor
        def _(pe):
            for t in range(tt):
                for q in range(2):
                    mm = pe.matmul(c.bank(t, 2 * P, q * 2 * P), c.a(pr + q * W + t * P, P), c.a(A1["CB"], 2 * P),
                                   start=True, stop=True)
                mm.then_inc(s["channels"], 1)
            for t in range(6):
                b = 6 if t % 2 == 0 else 0
                if t:
                    pe.wait_ge(s["v_out"], t - 1) if t > 1 else pe.wait_ge(s["uv"], 2)
                for q, (lo, n) in enumerate(((0, 512), (512, 256))):
                    mm = pe.matmul(c.bank(b + q, n), c.a(pr + 5 * W + t * P, P), c.a(A1["WKV"] + 768 + lo, n),
                                   start=True, stop=True)
                mm.then_inc(s["v"], 1)
            pe.wait_ge(s["uv"], tt)
            for q in range(2):
                for r, (lo, n, cs, sn, t0) in enumerate(parts):
                    for t in range(n // P):
                        for z, tab in ((0, cs), (1, sn)):
                            mm = pe.matmul(c.bank(2 + 2 * q + r, n), c.a(uv + ((t0 + t) * 2 + q) * 2 * P + z * P, P),
                                           c.a(A1[tab] + t * n, n), start=(t == 0 and z == 0), stop=(t == n // P - 1 and z == 1))
                mm.then_inc(s["positions"], 1)
            pe.wait_ge(s["ft"], 2)
            pe.wait_ge(s["v_out"], 6)
            for q in range(2):
                for r, (lo, n, *_) in enumerate(parts):
                    for k in range(2):
                        mm = pe.matmul(c.bank((6, 0)[q] + r, n), c.a(A1["WF"] + k * FW + q * P, P), c.a(ft + k * W + lo, n),
                                       start=(k == 0), stop=(k == 1))
                mm.then_inc(s["mixed"], 1)

        n = W if l == 0 else NL

        @block.scalar
        def _(act):
            for t in range(6):
                act.wait_ge(s["v"], t + 1)
                b = 6 if t % 2 == 0 else 0
                act.activation(c.a(A1["V"] + t * 768, 768), c.PS[:, 512 * b:512 * b + 768], ACT.Copy).then_inc(s["v_out"], 1)
            for q in range(2):
                act.wait_ge(s["mixed"], q + 1)
                b = (6, 0)[q]
                act.activation(c.h(q, 0, n), c.PS[:, 512 * b:512 * b + n], ACT.Identity,
                               bias=c.vec(f"b_four{l}", q)).then_inc(s["h"], 1)

        @block.vector
        def _(dve):
            for t in range(tt):
                dve.wait_ge(s["channels"], t + 1)
                dve.tensor_copy(c.a(uv + t * 4 * P, 4 * P), c.bank(t)).then_inc(s["uv"], 1)
            for q in range(2):
                dve.wait_ge(s["positions"], q + 1)
                dve.tensor_copy(c.a(ft + q * W, n), c.PS[:, 1024 * (q + 1):1024 * (q + 1) + n]).then_inc(s["ft"], 1)


def key_rope(c):
    pr, kt, t1 = A1["PROJ"] + 6 * W, A1["KTT"], A1["T1"]
    with phase(c, "swapped", "own", "rows") as (s, block):

        @block.tensor
        def _(pe):
            pe.matmul(c.bank(0, NL, p1=DROPE), c.a(A1["SWAP"], DROPE, 0, DROPE), c.a(pr, NL, 0, DROPE),
                      start=True, stop=True).then_inc(s["swapped"], 1)

        @block.vector
        def _(dve):
            link = Chain(dve, s["own"])
            dve.wait_ge(s["swapped"], 1)
            link(dve.tensor_tensor(c.a(t1, NL, 0, DROPE), c.bank(0, NL, p1=DROPE), c.a(A1["SIN"], NL, 0, DROPE), ALU.mult))
            link(dve.tensor_tensor(c.a(pr, NL, 0, DROPE), c.a(pr, NL, 0, DROPE), c.a(A1["COS"], NL, 0, DROPE), ALU.mult))
            link(dve.tensor_tensor(c.a(pr, NL, 0, DROPE), c.a(pr, NL, 0, DROPE), c.a(t1, NL, 0, DROPE), ALU.add))
            for h in range(4):
                dve.tensor_copy(c.a(kt + h * W, W, 64, 96), c.a(pr, W, 0, DROPE))


def heads_qk(c, l, g):
    pr, qt, kt, qr, t1 = (A1[x] for x in ("PROJ", "QT", "KTT", "QR", "T1"))
    nq = W if l == 0 else NL
    cq, ckv = pr + 2 * W, pr + 5 * W
    with phase(c, "q", "k", "r", "r_out", "swapped", "own", "out") as (s, block):

        @block.tensor
        def _(pe):
            def project(b, w, kn, stride, x, n):
                for r, (lo, m) in enumerate(((0, min(n, 512)), (512, n - 512))):
                    for k in range(kn):
                        if m > 0:
                            mm = pe.matmul(c.bank(b + r, m), c.a(w + k * stride, P), c.a(x + k * W + lo, m),
                                           start=(k == 0), stop=(k == kn - 1))
                return mm
            project(0, A1["WQ"] + 768 + g * P, 3, 1152, cq, nq).then_inc(s["r"], 1)
            for j in range(2):
                project(2 + 2 * j, A1["WQ"] + (2 * g + j) * P, 3, 1152, cq, nq).then_inc(s["q"], 1)
            project(6, A1["WKV"] + 2 * g * P, 1, 0, ckv, W).then_inc(s["k"], 1)
            pe.wait_ge(s["r_out"], 1)
            pe.matmul(c.bank(0, NL), c.a(A1["SWAP"], P), c.a(qr, NL), start=True, stop=True).then_inc(s["swapped"], 1)
            pe.wait_ge(s["out"], 1)
            project(2, A1["WKV"] + (2 * g + 1) * P, 1, 0, ckv, W).then_inc(s["k"], 1)

        @block.scalar
        def _(act):
            act.wait_ge(s["r"], 1)
            act.activation(c.a(qr, nq), c.PS[:, 0:nq], ACT.Copy).then_inc(s["r_out"], 1)
            for j in range(2):
                act.wait_ge(s["k"], j + 1)
                b = (6, 2)[j]
                for p in range(2):
                    act.activation(c.a(kt + (2 * j + p) * W, W, 0, 64), c.PS[64 * p:64 * p + 64, 512 * b:512 * b + W], ACT.Copy)

        @block.vector
        def _(dve):
            link = Chain(dve, s["own"])
            for j in range(2):
                dve.wait_ge(s["q"], j + 1)
                for p in range(2):
                    b = 2 + 2 * j
                    ins = dve.tensor_copy(c.a(qt + (2 * j + p) * W, nq, 0, 64), c.PS[64 * p:64 * p + 64, 512 * b:512 * b + nq])
                ins.then_inc(s["out"], 1)
            dve.wait_ge(s["swapped"], 1)
            link(dve.tensor_tensor(c.a(t1, NL), c.bank(0, NL), c.a(A1["SIN"], NL), ALU.mult))
            link(dve.tensor_tensor(c.a(qr, NL), c.a(qr, NL), c.a(A1["COS"], NL), ALU.mult))
            for h in range(4):
                r = slice(32 * h, 32 * h + 32)
                dve.tensor_tensor(c.a(qt + h * W, NL, 64, 96), c.a(qr, NL, 32 * h, 32 * h + 32),
                                  c.a(t1, NL, 32 * h, 32 * h + 32), ALU.add)
                if nq > NL:
                    dve.tensor_copy(c.a(qt + h * W + NL, NC, 64, 96), c.a(qr + NL, NC, 32 * h, 32 * h + 32))


def attention1(c, l, g):
    qt, kt, pp, pt, st, vv = (A1[x] for x in ("QT", "KTT", "PP", "PT", "ST", "V"))
    tiles_q = 6 if l == 0 else 4
    steps = [(h, i, 0 if i < 4 else NL, W if i < 4 else NC) for h in range(4) for i in range(tiles_q)]
    SUM, NEG, REC = st, st + 24, st + 48
    products = tiles_q // 4 + tiles_q % 4 // 2

    def turned_half(eng, a, half):
        h, i, k0, n = steps[a]
        m = n // P // 2
        eng.wait_ge(s["turned"], a + 1)
        if h:
            eng.wait_ge(s["o"], (h - 1) * products + 1 + (i >= 4))
        dst = c.a(pt + (k0 // P + half * m) * W, m * W).rearrange("p (t q) -> p t q", q=W)[:, :, i * P:(i + 1) * P]
        return dst, c.bank(4 + half, m * P).rearrange("p (t q) -> p t q", q=P)

    def result(act, a):
        h, i, *_ = steps[a]
        part = i // 2 - 1
        head = 4 * g + h
        p0, w = 64 * (head % 2), (NL, NC)[part]
        act.wait_ge(s["o"], h * products + part + 1)
        o = (2 + head // 2) * W + part * NL
        act.activation(c.H[p0:p0 + 64, o:o + w], c.bank(6 + part, w, p0=p0, p1=p0 + 64), ACT.Copy).then_inc(s["o_out"], 1)

    with phase(c, "scores", "neg", "probs", "normed", "turned", "pt_a", "pt_v", "o", "o_out", "own") as (s, block):

        @block.tensor
        def _(pe):
            def score(a):
                h, i, k0, n = steps[a]
                if a >= 2:
                    pe.wait_ge(s["probs"], a - 1)
                for r, (lo, m) in enumerate(((0, min(n, 512)), (512, n - 512))):
                    if m > 0:
                        mm = pe.matmul(c.bank(2 * (a % 2) + r, m), c.a(qt + h * W + i * P, P, 0, 96),
                                       c.a(kt + h * W + k0 + lo, m, 0, 96), start=True, stop=True)
                mm.then_inc(s["scores"], 1)

            def turn(a):
                h, i, k0, n = steps[a]
                pe.wait_ge(s["normed"], a + 1)
                if a >= 1:
                    pe.wait_ge(s["pt_a"], a)
                    pe.wait_ge(s["pt_v"], a)
                for k in range(n // P):
                    half = n // P // 2
                    out = c.bank(4 + (k >= half), P, (k % half) * P)
                    mm = pe.transpose(out, c.a(pp + (a % 2) * W + k * P, P), c.ID[:])
                mm.then_inc(s["turned"], 1)

            def values(h, part):
                last = h * tiles_q + (3 if part == 0 else 5)
                pe.wait_ge(s["pt_a"], last + 1)
                pe.wait_ge(s["pt_v"], last + 1)
                j = h * products + part
                if j >= 1:
                    pe.wait_ge(s["o_out"], j)
                head = 4 * g + h
                p0 = 64 * (head % 2)
                n, ts = (NL, range(6)) if part == 0 else (NC, (4, 5))
                for t in ts:
                    mm = pe.matmul(c.bank(6 + part, n, p0=p0, p1=p0 + 64), c.a(vv + t * 768 + head * 64, 64),
                                   c.a(pt + t * W + part * NL, n), start=(t == ts[0]), stop=(t == ts[-1]))
                mm.then_inc(s["o"], 1)

            for a in range(len(steps) + 1):
                if a < len(steps):
                    score(a)
                if a >= 1:
                    turn(a - 1)
                    h, i = steps[a - 1][:2]
                    if i == 3:
                        values(h, 0)
                    if i == 5:
                        values(h, 1)

        @block.scalar
        def _(act):
            for a in range(len(steps) + 2):
                if a < len(steps):
                    h, i, k0, n = steps[a]
                    act.wait_ge(s["neg"], a + 1)
                    if a >= 2:
                        act.wait_ge(s["turned"], a - 1)
                    act.activation(c.a(pp + (a % 2) * W, n), c.PS[:, 1024 * (a % 2):1024 * (a % 2) + n], ACT.Exp,
                                   bias=c.a(NEG + a, 1), scale=SCALE1, accum_out=c.a(SUM + a, 1)).then_inc(s["probs"], 1)
                if a >= 2 and steps[a - 2][1] in (3, 5):
                    result(act, a - 2)
                if 1 <= a <= len(steps):
                    dst, src = turned_half(act, a - 1, 0)
                    act.activation(dst, src, ACT.Copy).then_inc(s["pt_a"], 1)

        @block.vector
        def _(dve):
            link = Chain(dve, s["own"])
            for a in range(len(steps) + 1):
                if a < len(steps):
                    h, i, k0, n = steps[a]
                    dve.wait_ge(s["scores"], a + 1)
                    link(dve.tensor_reduce(c.a(REC + 2, 1), c.PS[:, 1024 * (a % 2):1024 * (a % 2) + n], AX, ALU.max))
                    dve.tensor_scalar(c.a(NEG + a, 1), c.a(REC + 2, 1), -SCALE1, None, ALU.mult).then_inc(s["neg"], 1)
                if a >= 1:
                    dst, src = turned_half(dve, a - 1, 1)
                    dve.tensor_copy(dst, src).then_inc(s["pt_v"], 1)
                if a < len(steps):
                    dve.wait_ge(s["probs"], a + 1)
                    link(dve.reciprocal(c.a(REC + a % 2, 1), c.a(SUM + a, 1)))
                    dve.tensor_scalar(c.a(pp + (a % 2) * W, n), c.a(pp + (a % 2) * W, n), c.a(REC + a % 2, 1), None,
                                      ALU.mult).then_inc(s["normed"], 1)


TW = NH2 * NL
A2 = {}
_at = 0
for _name, _n in (("OA", TW), ("OB", TW), ("ROWS", 9 * NL), ("COLS", 128), ("MASK", P), ("SMALL", 128), 
                  ("SEL", NH2 * P), ("Q", TW), ("K", TW), ("V", TW), ("Z", TW), ("U", 0)):
    A2[_name] = _at
    _at += _n
for _parts in ((("GATES", KT * P), ("RT", 2 * NL), ("RT2", 2 * NL), ("KEEP", NL), ("DROP", NL)),
               (("MEANS", 8 * NL),),
               (("DEC", NL), ("TMP", NL), ("TT", TW), ("ATT", TW), ("KB", TW), ("KD", TW), ("VB", TW), ("BT", 2 * NL),
                ("LV", P))):
    _at = A2["U"]
    for _name, _n in _parts:
        A2[_name] = _at
        _at += _n
    assert _at <= 30400, _at
A2["END"] = _at
A2["T"], A2["LT"], A2["Y"], A2["FLOOR"] = A2["OB"], A2["OA"], A2["DEC"], A2["TT"]
A2["STATE"], A2["CV"] = A2["DEC"], A2["OA"]
BETA, GCUM, GREST, ACOL, KEXP, MROW, MTROW, IEXP, BCUM = range(9)


def row(c, r, n=NL, lo=0):
    return c.a(A2["ROWS"] + r * NL + lo, n, 0, NH2)


def by_chunk(ap):
    return ap.rearrange("p (n t) -> p n t", t=CHUNK)


def gate_rows(c, args):
    G, RT, R2 = A2["GATES"], A2["RT"], A2["RT2"]
    KEEP, DROP, SM = A2["KEEP"], A2["DROP"], A2["SMALL"]
    with phase(c, "dma", "gates", "act", "own") as (s, block):

        @block.sync
        def _(sp):
            load(sp, s["dma"], (c.a(G, KT * P), args["gates"]), (c.a(KEEP, NL), const(args, "keep")),
                 (c.a(DROP, NL), const(args, "drop")), (c.a(A2["SEL"], NH2 * P), const(args, "sel")),
                 (c.a(A2["MASK"], P), const(args, "causal")))

        @block.tensor
        def _(pe):
            pe.wait_ge(s["dma"], 80)
            for k in range(KT):
                mm = pe.matmul(c.bank(0), c.a(G + k * P, P), c.h(k), start=(k == 0), stop=(k == KT - 1))
            mm.then_inc(s["gates"], 1)

        rt = lambda r: c.a(RT + r * NL, NL, 0, NH2)
        r2 = lambda r: c.a(R2 + r * NL, NL, 0, NH2)
        both = lambda o: c.a(o, 2 * NL, 0, NH2)
        bias = lambda j: c.VEC[0:NH2, COL["rowb"] + j:COL["rowb"] + j + 1]

        @block.scalar
        def _(act):
            act.wait_ge(s["gates"], 1)
            act.activation(row(c, BETA), c.bank(0, p1=NH2), ACT.Sigmoid).then_inc(s["act"], 1)
            act.activation(c.a(SM, 1, 0, NH2), bias(0), ACT.Exp).then_inc(s["act"], 1)
            act.wait_ge(s["own"], 6)
            act.activation(both(R2), both(RT), ACT.Abs).then_inc(s["act"], 1)
            act.wait_ge(s["act"], 3)
            act.activation(both(R2), both(R2), ACT.Exp, scale=-1.0).then_inc(s["act"], 1)
            act.wait_ge(s["act"], 4)
            act.activation(both(R2), both(R2), ACT.Ln, bias=1.0).then_inc(s["act"], 1)

        @block.vector
        def _(dve):
            link = Chain(dve, s["own"])
            dve.wait_ge(s["dma"], 80)
            dve.wait_ge(s["act"], 1)
            link(dve.tensor_copy(rt(0), c.bank(0, p0=32, p1=36)))
            link(dve.tensor_copy(row(c, MROW), c.bank(0, p0=64, p1=68)))
            link(dve.tensor_copy(rt(1), c.bank(0, p0=96, p1=100)))
            link(dve.tensor_scalar(rt(0), rt(0), bias(1), None, ALU.add))
            link(dve.tensor_scalar(rt(1), rt(1), bias(3), -1.0, ALU.add, ALU.mult))
            link(dve.tensor_scalar(row(c, MROW), row(c, MROW), bias(2), None, ALU.add))
            dve.wait_ge(s["act"], 5)
            link(dve.scalar_tensor_tensor(both(RT), both(RT), 0.0, both(R2), ALU.max, ALU.add))
            link(dve.tensor_scalar(rt(0), rt(0), c.a(SM, 1, 0, NH2), -1.0, ALU.mult, ALU.mult))
            link(dve.tensor_scalar(rt(1), rt(1), -1.0, None, ALU.mult))
            keep, drop = c.a(KEEP, NL, 0, NH2), c.a(DROP, NL, 0, NH2)
            link(dve.tensor_tensor_scan(row(c, GCUM), keep, rt(0), 0.0, ALU.mult, ALU.add))
            link(dve.tensor_tensor_scan(row(c, BCUM), keep, rt(1), 0.0, ALU.mult, ALU.add))
            last = lambda r: by_chunk(row(c, r))[:, :, CHUNK - 1:CHUNK]
            wide = lambda ap: ap.broadcast_to([NH2, NCH, CHUNK])
            link(dve.tensor_tensor(by_chunk(row(c, GREST)), wide(last(GCUM)), by_chunk(row(c, GCUM)), ALU.subtract))
            link(dve.tensor_tensor(row(c, ACOL), row(c, MROW), row(c, BCUM), ALU.subtract))
            link(dve.tensor_tensor_scan(row(c, KEXP), drop, row(c, ACOL), 0.0, ALU.add, ALU.max))
            m = lambda lo, n: c.a(SM + 16 + lo, n, 0, NH2)
            link(dve.memset(m(0, 1), 0.0))
            link(dve.tensor_copy(c.a(SM + 32, NCH, 0, NH2), last(KEXP)))
            link(dve.tensor_copy(c.a(SM + 48, NCH, 0, NH2), last(BCUM)))
            link(dve.tensor_tensor_scan(m(1, NCH), c.a(SM + 32, NCH, 0, NH2), c.a(SM + 48, NCH, 0, NH2), 0.0, ALU.max, ALU.add))
            before = wide(m(0, NCH).rearrange("p (n a) -> p n a", a=1))
            link(dve.tensor_tensor(by_chunk(row(c, MROW)), by_chunk(row(c, KEXP)), before, ALU.max))
            link(dve.tensor_tensor(row(c, MTROW), row(c, BCUM), row(c, MROW), ALU.add))
            link(dve.tensor_tensor(by_chunk(row(c, IEXP)), before, by_chunk(row(c, MROW)), ALU.subtract))
            link(dve.tensor_tensor(by_chunk(row(c, KEXP)), by_chunk(row(c, ACOL)), wide(last(MROW)), ALU.subtract))


def gate_columns(c):
    CO, TMP = A2["COLS"], A2["SMALL"]
    with phase(c, "turned", "copied", "exp", "own") as (s, block):
        @block.tensor
        def _(pe):
            for r in range(5):
                for t in range(4):
                    mm = pe.matmul(c.bank(0, NH2, (r * 4 + t) * NH2), row(c, r, P, t * P), c.ID[0:NH2, 0:NH2], start=True, stop=True)
            mm.then_inc(s["turned"], 1)

        @block.vector
        def _(dve):
            dve.wait_ge(s["turned"], 1)
            dve.tensor_copy(c.a(CO, 80), c.bank(0, 80)).then_inc(s["copied"], 1)
            dve.wait_ge(s["exp"], 3)
            dve.tensor_tensor(c.a(CO + 96, 16), c.a(CO + 80, 16), c.a(CO, 16), ALU.mult).then_inc(s["own"], 1)
            dve.wait_ge(s["own"], 1)

        @block.scalar
        def _(act):
            act.wait_ge(s["copied"], 1)
            act.activation(c.a(CO + 80, 16), c.a(CO + GCUM * 16, 16), ACT.Exp).then_inc(s["exp"], 1)
            act.activation(c.a(CO + GREST * 16, 16), c.a(CO + GREST * 16, 16), ACT.Exp).then_inc(s["exp"], 1)
            act.activation(c.a(CO + KEXP * 16, 16), c.a(CO + KEXP * 16, 16), ACT.Exp).then_inc(s["exp"], 1)


def token_col(c, r, t, h):
    o = A2["COLS"] + r * 16 + t * 4 + h
    return c.a(o, 1)


EXPG, BEXPG = 5, 6


def project_a(c, args):
    CV = A2["CV"]

    def tap(k, i, m):
        j = COL[f"conv{k}"] + 4 * i + m
        return c.VEC[:, ds(j, 1)] if not isinstance(i, int) else c.VEC[:, j:j + 1]

    def out(i, m):
        return c.a(A2["Q"] + (4 * i + m) * NL, NL)

    def scalar(act, i, m, acc, s):
        if isinstance(i, int) and i == 3:
            act.activation(out(i, m), acc, ACT.Silu).then_inc(s["free"][m], 1)
            return
        act.wait_ge(s["cv_free"], 4 * i + m + 1)
        act.activation(c.a(CV + m * NL, NL), acc, ACT.Identity, scale=tap(3, i, m)).then_inc(s["tap3"], 1)
        act.wait_ge(s["free"][m], i + 2)
        act.activation(out(i, m), c.a(CV + m * NL, NL), ACT.Silu).then_inc(s["cv_free"], 1)

    def vector(dve, i, m, acc, s):
        if isinstance(i, int) and i == 3:
            return
        dve.wait_ge(s["tap3"], 4 * i + m + 1)
        for k in (2, 1, 0):
            d = 3 - k
            y = c.a(CV + m * NL + d, NL - d)
            ins = dve.scalar_tensor_tensor(y, acc[:, 0:NL - d], tap(k, i, m), y, ALU.mult, ALU.add)
            if k:
                ins.then_inc(s["taps"], 1)
                dve.wait_ge(s["taps"], 8 * i + 2 * m + 3 - k)
        ins.then_inc(s["free"][m], 1)

    with c.pair(NL) as xp:
        linear(c, args, (c.h, xp), KT, 16, NL, scalar, vector, extra=("tap3", "taps", "cv_free"),
               credit=lambda dve, s: dve.sem_inc(s["cv_free"], 4), peel=1)


def unit_norms(c, tiles_of, scales, eps=EPS, gain=None, times=None):
    n = len(tiles_of)
    with phase(c, "squared", "summed", "mean", "root", "own", "done") as (s, block):
        MEAN = A2["MEANS"]

        @block.scalar
        def _(act):
            for j in range(n):
                if j >= 2:
                    act.wait_ge(s["summed"], j - 1)
                act.activation(c.SQ[:, (j % 2) * W:(j % 2) * W + NL], tiles_of[j], ACT.Square).then_inc(s["squared"], 1)
            for j in range(n):
                act.wait_ge(s["mean"], j + 1)
                act.activation(c.a(MEAN + j * NL, NL), c.a(MEAN + j * NL, NL), ACT.Sqrt).then_inc(s["root"], 1)

        @block.tensor
        def _(pe):
            for j in range(n):
                pe.wait_ge(s["squared"], j + 1)
                pe.matmul(c.bank(j), c.ONES[:], c.SQ[:, (j % 2) * W:(j % 2) * W + NL], start=True, stop=True).then_inc(s["summed"], 1)

        @block.vector
        def _(dve):
            for j in range(n):
                dve.wait_ge(s["summed"], j + 1)
                mul, add = scales[j]
                dve.tensor_scalar(c.a(MEAN + j * NL, NL), c.bank(j), mul, add, ALU.mult, ALU.add).then_inc(s["mean"], 1)
            link = Chain(dve, s["own"])
            for j in range(n):
                dve.wait_ge(s["root"], j + 1)
                r = c.a(MEAN + j * NL, NL)
                link(dve.reciprocal(r, r))
                if gain is None:
                    dve.tensor_tensor(tiles_of[j], tiles_of[j], r, ALU.mult).then_inc(s["done"], 1)
                else:
                    link(dve.scalar_tensor_tensor(tiles_of[j], tiles_of[j], gain(j), r, ALU.mult, ALU.mult))
                    dve.tensor_tensor(tiles_of[j], tiles_of[j], times[j], ALU.mult).then_inc(s["done"], 1)


def delta_inner(c, args):
    o = A2
    sel = lambda h: c.a(o["SEL"] + h * P, P, 0, NH2)
    with phase(c, "dma", "bank_g", "bank_b", "bank_k", "bank_a", "bank_t", "act_done", "dec", "exp", "masked", "lt",
               "turn_k", "turn_v", "kb", "vb", "own", "att", "own_act", "rounds") as (s, block):

        @block.tensor
        def _(pe):
            for h in range(NH2):
                if h:
                    pe.wait_ge(s["rounds"], h)
                    pe.wait_ge(s["act_done"], h)
                pe.matmul(c.bank(0), sel(h), row(c, GCUM), start=True, stop=True).then_inc(s["bank_g"], 1)
                pe.matmul(c.bank(1), sel(h), row(c, BETA), start=True, stop=True).then_inc(s["bank_b"], 1)
                for b, x, sem in ((2, "K", s["bank_k"]), (3, "Q", s["bank_a"])):
                    for t in range(4):
                        mm = pe.matmul(c.bank(b, P, t * P), c.a(o["K"] + h * NL + t * P, P), c.a(o[x] + h * NL + t * P, P),
                                       start=True, stop=True)
                    mm.then_inc(sem, 1)
                for b, x, sem in ((4, "K", s["turn_k"]), (5, "V", s["turn_v"])):
                    for t in range(4):
                        mm = pe.transpose(c.bank(b, P, t * P), c.a(o[x] + h * NL + t * P, P), c.ID[:])
                    mm.then_inc(sem, 1)

        @block.vector
        def _(dve):
            link = Chain(dve, s["own"])
            m4 = lambda ap: ap.rearrange("p (t q) -> p t q", q=P)
            mask = c.a(o["MASK"], P).rearrange("p (a q) -> p a q", a=1).broadcast_to([P, 4, P])
            for h in range(NH2):
                dec, tmp = c.a(o["DEC"], NL), c.a(o["TMP"], NL)
                dve.wait_ge(s["bank_g"], h + 1)
                if h:
                    dve.wait_ge(s["exp"], 2 * h)
                for t in range(4):
                    ins = dve.scalar_tensor_tensor(c.a(o["DEC"] + t * P, P), c.bank(0, P, t * P), token_col(c, GCUM, t, h),
                                                   c.a(o["MASK"], P), ALU.subtract, ALU.mult)
                ins.then_inc(s["dec"], 1)
                dve.wait_ge(s["exp"], 2 * h + 1)
                link(dve.tensor_tensor(m4(dec), m4(dec), mask, ALU.mult))
                dve.wait_ge(s["bank_k"], h + 1)
                lt = c.a(o["LT"] + h * NL, NL)
                link(dve.tensor_tensor(lt, dec, c.bank(2), ALU.mult))
                dve.wait_ge(s["bank_b"], h + 1)
                link(dve.tensor_tensor(lt, lt, c.bank(1), ALU.mult))
                dve.wait_ge(s["bank_a"], h + 1)
                link(dve.tensor_tensor(c.a(o["ATT"] + h * NL, NL), dec, c.bank(3), ALU.mult))
                dve.wait_ge(s["exp"], 2 * h + 2)
                dve.tensor_copy(c.a(o["SMALL"] + 64 + h * NCH, NCH).rearrange("p (n a) -> p n a", a=1),
                                by_chunk(tmp)[:, :, CHUNK - 1:CHUNK])
                q = c.a(o["Q"] + h * NL, NL)
                link(dve.tensor_tensor(q, q, tmp, ALU.mult))
                dve.wait_ge(s["turn_v"], h + 1)
                for t in range(4):
                    ins = dve.tensor_scalar(c.a(o["VB"] + h * NL + t * P, P), c.bank(5, P, t * P), token_col(c, BETA, t, h), None, ALU.mult)
                ins.then_inc(s["rounds"], 1)

        @block.scalar
        def _(act):
            for h in range(NH2):
                act.wait_ge(s["dec"], h + 1)
                act.activation(c.a(o["DEC"], NL), c.a(o["DEC"], NL), ACT.Exp).then_inc(s["exp"], 1)
                if h:
                    act.wait_ge(s["rounds"], h)
                act.activation(c.a(o["TMP"], NL), c.bank(0), ACT.Exp).then_inc(s["exp"], 1)
                act.wait_ge(s["turn_k"], h + 1)
                for t in range(4):
                    act.activation(c.a(o["KB"] + h * NL + t * P, P), c.bank(4, P, t * P), ACT.Copy, scale=token_col(c, BEXPG, t, h))
                    ins = act.activation(c.a(o["KD"] + h * NL + t * P, P), c.bank(4, P, t * P), ACT.Copy,
                                         scale=token_col(c, GREST, t, h))
                ins.then_inc(s["act_done"], 1)

    tt = lambda h: c.a(o["TT"] + h * NL, NL)
    tn = lambda h: c.a(o["T"] + h * NL, NL)
    id4 = c.ID[:].rearrange("p (a q) -> p a q", a=1).broadcast_to([P, 4, P])
    m4 = lambda ap: ap.rearrange("p (t q) -> p t q", q=P)
    for lv in range(6):
        with phase(c, "dma", "bt", "y", "y_out", "z", "zt", "t_new", "tt_new") as (s, block):
            @block.sync
            def _(sp):
                load(sp, s["dma"], (c.a(o["LV"], P), const(args, f"lv{lv}")))

            @block.tensor
            def _(pe):
                def second(h):
                    pe.wait_ge(s["y_out"], h + 1)
                    if h >= 2:
                        pe.wait_ge(s["tt_new"], h - 1)
                        pe.wait_ge(s["t_new"], h - 1)
                    for t in range(4):
                        mm = pe.matmul(c.bank(2 + h % 2, P, t * P), c.a(o["TT"] + h * NL + t * P, P),
                                       c.a(o["Y"] + (h % 2) * NL + t * P, P), start=True, stop=True)
                    mm.then_inc(s["z"], 1)
                    for t in range(4):
                        mm = pe.matmul(c.bank(4 + h % 2, P, t * P), c.a(o["Y"] + (h % 2) * NL + t * P, P),
                                       c.a(o["TT"] + h * NL + t * P, P), start=True, stop=True)
                    mm.then_inc(s["zt"], 1)
                for h in range(NH2):
                    pe.wait_ge(s["bt"], h + 1)
                    for t in range(4):
                        rhs = c.ID[:] if lv == 0 else c.a(o["T"] + h * NL + t * P, P)
                        mm = pe.matmul(c.bank(h % 2, P, t * P), c.a(o["BT"] + (h % 2) * NL + t * P, P), rhs, start=True, stop=True)
                    mm.then_inc(s["y"], 1)
                    if lv and h:
                        second(h - 1)
                if lv:
                    second(NH2 - 1)

            @block.vector
            def _(dve):
                lvm = c.a(o["LV"], P).rearrange("p (a q) -> p a q", a=1).broadcast_to([P, 4, P])
                dve.wait_ge(s["dma"], 16)

                def masked(h):
                    if h >= 2:
                        dve.wait_ge(s["y"], h - 1)
                        dve.wait_ge(s["tt_new"], h - 1)
                    dve.tensor_tensor(m4(c.a(o["BT"] + (h % 2) * NL, NL)), m4(c.a(o["LT"] + h * NL, NL)), lvm, ALU.mult).then_inc(s["bt"], 1)

                masked(0)
                for h in range(NH2):
                    if h + 1 < NH2:
                        masked(h + 1)
                    if lv == 0:
                        dve.wait_ge(s["bt"], h + 1)
                        dve.tensor_tensor(m4(tt(h)), id4, m4(c.a(o["BT"] + (h % 2) * NL, NL)), ALU.subtract).then_inc(s["tt_new"], 1)
                        dve.wait_ge(s["y"], h + 1)
                        dve.tensor_tensor(m4(tn(h)), id4, m4(c.bank(h % 2)), ALU.subtract).then_inc(s["t_new"], 1)
                    else:
                        dve.wait_ge(s["z"], h + 1)
                        dve.wait_ge(s["zt"], h + 1)
                        dve.tensor_tensor(tn(h), tn(h), c.bank(2 + h % 2), ALU.subtract).then_inc(s["t_new"], 1)
                        dve.tensor_tensor(tt(h), tt(h), c.bank(4 + h % 2), ALU.subtract).then_inc(s["tt_new"], 1)

            if lv:
                @block.scalar
                def _(act):
                    for h in range(NH2):
                        act.wait_ge(s["y"], h + 1)
                        if h >= 2:
                            act.wait_ge(s["zt"], h - 1)
                        act.activation(c.a(o["Y"] + (h % 2) * NL, NL), c.bank(h % 2), ACT.Copy).then_inc(s["y_out"], 1)
    with phase(c, "w", "u", "kb", "vb") as (s, block):
        @block.tensor
        def _(pe):
            for h in range(NH2):
                if h >= 2:
                    pe.wait_ge(s["kb"], h - 1)
                    pe.wait_ge(s["vb"], h - 1)
                for b, sem in ((0, s["w"]), (2, s["u"])):
                    for t in range(4):
                        f = h * NL + t * P
                        x, y = (o["KB"], o["TT"]) if b == 0 else (o["TT"], o["VB"])
                        mm = pe.matmul(c.bank(b + h % 2, P, t * P), c.a(x + f, P), c.a(y + f, P), start=True, stop=True)
                    mm.then_inc(sem, 1)

        @block.scalar
        def _(act):
            for h in range(NH2):
                act.wait_ge(s["w"], h + 1)
                act.activation(c.a(o["KB"] + h * NL, NL), c.bank(h % 2), ACT.Copy).then_inc(s["kb"], 1)

        @block.vector
        def _(dve):
            for h in range(NH2):
                dve.wait_ge(s["u"], h + 1)
                dve.tensor_copy(c.a(o["VB"] + h * NL, NL), c.bank(2 + h % 2)).then_inc(s["vb"], 1)


def heads(c, name, lo, n, p0=0, p1=P):
    return c.a(A2[name], TW, p0, p1).rearrange("p (h t) -> p h t", t=NL)[:, :, lo:lo + n]


def delta_scan(c):
    o = A2
    ST, VN = o["STATE"], o["BT"]
    with phase(c, "zero", "ws", "vn", "out", "ds", "oa", "state") as (s, block):

        @block.tensor
        def _(pe):
            pe.wait_ge(s["zero"], 1)
            for n in range(NCH):
                t, r, b = n // 2, 64 * (n % 2), 3 * (n % 2)
                lo = t * P + r
                if n:
                    pe.wait_ge(s["state"], 4 * n)
                if n >= 2:
                    pe.wait_ge(s["oa"], n - 1)
                for h in range(NH2):
                    mm = pe.matmul(c.bank(b, P, h * P, r, r + 64), c.a(o["KB"] + h * NL + lo, 64), c.a(ST + h * P, P), start=True, stop=True)
                mm.then_inc(s["ws"], 1)
                pe.wait_ge(s["vn"], n + 1)
                for h in range(NH2):
                    pe.matmul(c.bank(b + 1, 64, h * 64), c.a(ST + h * P, P), c.a(o["Q"] + h * NL + lo, 64), start=True, stop=False)
                    mm = pe.matmul(c.bank(b + 1, 64, h * 64), c.a(VN + h * P, P, r, r + 64),
                                   c.a(o["ATT"] + h * NL + lo, 64, r, r + 64), start=False, stop=True)
                mm.then_inc(s["out"], 1)
                for h in range(NH2):
                    mm = pe.matmul(c.bank(b + 2, P, h * P), c.a(o["KD"] + h * NL + t * P, P, r, r + 64),
                                   c.a(VN + h * P, P, r, r + 64), start=True, stop=True)
                mm.then_inc(s["ds"], 1)

        @block.scalar
        def _(act):
            for n in range(NCH):
                act.wait_ge(s["out"], n + 1)
                act.activation(heads(c, "OA", n * CHUNK, CHUNK), c.bank(3 * (n % 2) + 1, 256).rearrange("p (h t) -> p h t", t=64),
                               ACT.Copy).then_inc(s["oa"], 1)

        @block.vector
        def _(dve):
            dve.memset(c.a(ST, 4 * P), 0.0).then_inc(s["zero"], 1)
            dve.wait_ge(s["zero"], 1)
            for n in range(NCH):
                t, r, b = n // 2, 64 * (n % 2), 3 * (n % 2)
                dve.wait_ge(s["ws"], n + 1)
                if n:
                    dve.wait_ge(s["ds"], n)
                dve.tensor_tensor(c.a(VN, 4 * P, r, r + 64).rearrange("p (h q) -> p h q", q=P),
                                  heads(c, "VB", t * P, P, r, r + 64),
                                  c.bank(b, 512, 0, r, r + 64).rearrange("p (h q) -> p h q", q=P), ALU.subtract).then_inc(s["vn"], 1)
                dve.wait_ge(s["ds"], n + 1)
                for h in range(NH2):
                    st = c.a(ST + h * P, P)
                    dve.scalar_tensor_tensor(st, st, c.a(o["SMALL"] + 64 + h * NCH + n, 1), c.bank(b + 2, P, h * P),
                                             ALU.mult, ALU.add).then_inc(s["state"], 1)
                dve.wait_ge(s["state"], 4 * n + 4)


def project_b(c, args):
    def scalar(act, i, m, acc, s):
        free = s["free"][m]
        dst = c.a(A2[("Q", "K", "Z", "V")[i]] + m * NL, NL)
        if i == 2:
            act.activation(dst, acc, ACT.Sigmoid).then_inc(free, 1)
        else:
            act.activation(dst, acc, ACT.Copy, scale=SCALE2 if i == 0 else 1.0).then_inc(free, 1)

    with c.pair(NL) as xp:
        linear(c, args, (c.h, xp), KT, 16, NL, scalar, peel=4)
    values_by_token(c, lambda h: A2["V"] + h * NL, NH2, lambda t: A2["V"] + t * NL)


def values_by_token(c, src, n, dst):
    with phase(c, "turned", "out") as (s, block):
        @block.tensor
        def _(pe):
            for t in range(4):
                for h in range(n):
                    mm = pe.transpose(c.bank(t, P, h * P), c.a(src(h) + t * P, P), c.ID[:])
            mm.then_inc(s["turned"], 1)

        @block.vector
        def _(dve):
            dve.wait_ge(s["turned"], 1)
            for t in range(4):
                dve.tensor_copy(c.a(dst(t), n * P), c.bank(t, n * P)).then_inc(s["out"], 1)


def mlstm_inner(c):
    o = A2
    sel = lambda h: c.a(o["SEL"] + h * P, P, 0, NH2)
    with phase(c, "bank_m", "bank_i", "bank_t", "bank_a", "turn_k", "dec", "exp", "own", "rounds", "act_done") as (s, block):

        @block.tensor
        def _(pe):
            for h in range(NH2):
                if h:
                    pe.wait_ge(s["rounds"], h)
                    pe.wait_ge(s["act_done"], h)
                for b, r, sem in ((0, MROW, s["bank_m"]), (1, IEXP, s["bank_i"]), (2, MTROW, s["bank_t"])):
                    pe.matmul(c.bank(b), sel(h), row(c, r), start=True, stop=True).then_inc(sem, 1)
                for t in range(4):
                    mm = pe.matmul(c.bank(3, P, t * P), c.a(o["K"] + h * NL + t * P, P), c.a(o["Q"] + h * NL + t * P, P),
                                   start=True, stop=True)
                mm.then_inc(s["bank_a"], 1)
                for t in range(4):
                    mm = pe.transpose(c.bank(4, P, t * P), c.a(o["K"] + h * NL + t * P, P), c.ID[:])
                mm.then_inc(s["turn_k"], 1)

        @block.vector
        def _(dve):
            link = Chain(dve, s["own"])
            m4 = lambda ap: ap.rearrange("p (t q) -> p t q", q=P)
            mask = c.a(o["MASK"], P).rearrange("p (a q) -> p a q", a=1).broadcast_to([P, 4, P])
            for h in range(NH2):
                dec, tmp = c.a(o["DEC"], NL), c.a(o["TMP"], NL)
                dve.wait_ge(s["bank_m"], h + 1)
                for t in range(4):
                    ins = dve.scalar_tensor_tensor(c.a(o["DEC"] + t * P, P), c.bank(0, P, t * P), token_col(c, ACOL, t, h),
                                                   c.a(o["MASK"], P), ALU.subtract, ALU.mult)
                ins.then_inc(s["dec"], 1)
                dve.wait_ge(s["exp"], 3 * h + 1)
                link(dve.tensor_tensor(m4(dec), m4(dec), mask, ALU.mult))
                dve.wait_ge(s["bank_a"], h + 1)
                link(dve.tensor_tensor(c.a(o["ATT"] + h * NL, NL), dec, c.bank(3), ALU.mult))
                dve.wait_ge(s["exp"], 3 * h + 2)
                dve.tensor_copy(c.a(o["SMALL"] + 64 + h * NCH, NCH).rearrange("p (n a) -> p n a", a=1),
                                by_chunk(tmp)[:, :, CHUNK - 1:CHUNK])
                q = c.a(o["Q"] + h * NL, NL)
                dve.tensor_tensor(q, q, tmp, ALU.mult).then_inc(s["rounds"], 1)

        @block.scalar
        def _(act):
            for h in range(NH2):
                act.wait_ge(s["dec"], h + 1)
                act.activation(c.a(o["DEC"], NL), c.a(o["DEC"], NL), ACT.Exp, scale=-1.0).then_inc(s["exp"], 1)
                if h:
                    act.wait_ge(s["rounds"], h)
                act.wait_ge(s["bank_i"], h + 1)
                act.activation(c.a(o["TMP"], NL), c.bank(1), ACT.Exp).then_inc(s["exp"], 1)
                act.wait_ge(s["bank_t"], h + 1)
                act.activation(c.a(o["FLOOR"] + h * NL, NL), c.bank(2), ACT.Exp, scale=-1.0).then_inc(s["exp"], 1)
                act.wait_ge(s["turn_k"], h + 1)
                for t in range(4):
                    ins = act.activation(c.a(o["KD"] + h * NL + t * P, P), c.bank(4, P, t * P), ACT.Copy,
                                         scale=token_col(c, KEXP, t, h))
                ins.then_inc(s["act_done"], 1)


def mlstm_scan(c):
    o = A2
    ST = o["STATE"]
    with phase(c, "zero", "out", "ds", "ob", "state") as (s, block):

        @block.tensor
        def _(pe):
            pe.wait_ge(s["zero"], 1)
            for n in range(NCH):
                t, r, b = n // 2, 64 * (n % 2), 3 * (n % 2)
                lo = t * P + r
                if n:
                    pe.wait_ge(s["state"], 8 * n)
                if n >= 2:
                    pe.wait_ge(s["ob"], n - 1)
                for h in range(NH2):
                    att = c.a(o["ATT"] + h * NL + lo, 64, r, r + 64)
                    for z in range(2):
                        out = c.bank(b, 64, z * 256 + h * 64)
                        pe.matmul(out, c.a(ST + (z * 4 + h) * P, P), c.a(o["Q"] + h * NL + lo, 64), start=True, stop=False)
                        inner = c.a(o["V"] + t * NL + h * P, P, r, r + 64) if z == 0 else c.ONES[r:r + 64, :]
                        mm = pe.matmul(out, inner, att, start=False, stop=True)
                mm.then_inc(s["out"], 1)
                for h in range(NH2):
                    kw = c.a(o["KD"] + h * NL + t * P, P, r, r + 64)
                    pe.matmul(c.bank(b + 1, P, h * P), kw, c.a(o["V"] + t * NL + h * P, P, r, r + 64), start=True, stop=True)
                    mm = pe.matmul(c.bank(b + 2, P, h * P), kw, c.ONES[r:r + 64, :], start=True, stop=True)
                mm.then_inc(s["ds"], 1)

        @block.scalar
        def _(act):
            for n in range(NCH):
                act.wait_ge(s["out"], n + 1)
                for z, name in ((0, "OB"), (1, "KB")):
                    ins = act.activation(heads(c, name, n * CHUNK, CHUNK),
                                         c.bank(3 * (n % 2), 256, z * 256).rearrange("p (h t) -> p h t", t=64), ACT.Copy)
                ins.then_inc(s["ob"], 1)

        @block.vector
        def _(dve):
            dve.memset(c.a(ST, 8 * P), 0.0).then_inc(s["zero"], 1)
            dve.wait_ge(s["zero"], 1)
            for n in range(NCH):
                b = 3 * (n % 2)
                dve.wait_ge(s["ds"], n + 1)
                for z in range(2):
                    for h in range(NH2):
                        st = c.a(ST + (z * 4 + h) * P, P)
                        dve.scalar_tensor_tensor(st, st, c.a(o["SMALL"] + 64 + h * NCH + n, 1), c.bank(b + 1 + z, P, h * P),
                                                 ALU.mult, ALU.add).then_inc(s["state"], 1)
                dve.wait_ge(s["state"], 8 * n + 8)
    with phase(c, "own") as (s, block):
        @block.vector
        def _(dve):
            link = Chain(dve, s["own"])
            den, num, floor = c.a(o["KB"], TW), c.a(o["OB"], TW), c.a(o["FLOOR"], TW)
            link(dve.scalar_tensor_tensor(den, den, -1.0, den, ALU.mult, ALU.max))
            link(dve.tensor_tensor(den, den, floor, ALU.max))
            link(dve.reciprocal(den, den))
            link(dve.tensor_tensor(num, num, den, ALU.mult))


def after(c, args, x, gain, dst=None, bias=None):
    dst = dst or c.h

    def scalar(act, i, m, acc, s):
        h, free = dst(4 * i + m, 0, NL), s["free"][m]
        if bias is None:
            act.activation(h, acc, ACT.Copy).then_inc(free, 1)
        else:
            act.activation(h, acc, ACT.Identity, bias=c.vec(bias, 4 * i + m)).then_inc(free, 1)
    linear(c, args, x, KT, KT, NL, scalar)
    add_norm(c, gain, dst)


def add_norm(c, gain, dst):
    def add(dve, scaled, own):
        dve.wait_ge(scaled, KT)
        for k in range(KT):
            dve.tensor_tensor(c.x(k), c.x(k), dst(k, 0, NL), ALU.add)
    norm(c, dst, dst, KT, D, NL, lambda k, q: c.vec(gain, k), post=add)


def ffn2(c, args, l):
    plain_norm(c, f"gain{l}2")
    with c.pair(NL) as xp, c.pair(NL) as hidden, c.room(4 * NL) as room, c.room(KT * NL) as total:
        hh, hl, hw = hidden
        re = lambda m: room[:, m * NL:m * NL + NL]
        y = lambda k, lo, n: total[:, k * NL + lo:k * NL + lo + n]

        def place(t, i, m):
            j = (4 * i + m) * hw
            return t[:, j:j + NL] if isinstance(i, int) else t[:, ds(j, NL)]

        def scalar(act, i, m, acc, s):
            act.wait_ge(s["lo"][m], i + 1)
            act.activation(re(m), acc, ACT.Relu).then_inc(s["relu"], 1)

        def vector(dve, i, m, acc, s):
            dve.wait_ge(s["relu"], 4 * i + m + 1)
            dve.tensor_tensor(re(m), acc, re(m), ALU.mult).then_inc(s["free"][m], 1)

        def scalar2(act, i, m, s):
            act.wait_ge(s["free"][m], i + 2)
            act.activation(place(hh, i, m), re(m), ACT.Copy).then_inc(s["hi"], 1)

        def vector2(dve, i, m, s):
            dve.wait_ge(s["hi"], 4 * i + m + 1)
            dve.tensor_tensor(place(hl, i, m), re(m), place(hh, i, m).bitcast(F32), ALU.subtract).then_inc(s["lo"][m], 1)

        def credit(dve, s):
            for m in range(4):
                dve.sem_inc(s["lo"][m], 1)

        x = (c.h, xp)
        for p, m in ffn_parts(32):
            linear(c, args, x, KT, m, NL, scalar, vector, scalar2, vector2, ("relu", "hi"), credit, groups={"lo": 4})
            x = xp

            def take(dve, i, m, acc, s):
                t = y(4 * i + m, 0, NL)
                if p == 0:
                    dve.tensor_copy(t, acc).then_inc(s["free"][m], 1)
                else:
                    dve.tensor_tensor(t, t, acc, ALU.add).then_inc(s["free"][m], 1)
            linear(c, args, hidden, KT, KT, NL, vector=take)
        add_norm(c, f"gain{l}3", y)


def gated_embedding(c, args, l):
    with c.high_room(2 * D + 2 * NL + 4 * NL):
        gated_embedding_in(c, args, l)


def gated_embedding_in(c, args, l):
    WP, PL, SG = 0, 2 * D, 2 * D + 2 * NL
    with phase(c, "dma", "sums", "copied") as (s, block):
        @block.sync
        def _(sp):
            load(sp, s["dma"], (c.a(WP, 2 * D), args["wple"][l]), (c.a(PL, 2 * NL), args["ple"][l]))

        @block.tensor
        def _(pe):
            pe.wait_ge(s["dma"], 32)
            for m in range(KT):
                for k in range(2):
                    mm = pe.matmul(c.bank(m), c.a(WP + k * D + m * P, P), c.a(PL + k * NL, NL), start=(k == 0), stop=(k == 1))
                mm.then_inc(s["sums"], 1)

        @block.vector
        def _(dve):
            for m in range(KT):
                dve.wait_ge(s["sums"], m + 1)
                dve.tensor_copy(c.h(m), c.bank(m)).then_inc(s["copied"], 1)

    def scalar(act, i, m, acc, s):
        act.wait_ge(s["free"][m], i + 1)
        act.activation(c.a(SG + m * NL, NL), acc, ACT.Sigmoid).then_inc(s["sig"], 1)

    def vector(dve, i, m, acc, s):
        h = c.h(4 * i + m)
        dve.wait_ge(s["sig"], 4 * i + m + 1)
        dve.tensor_tensor(h, h, c.a(SG + m * NL, NL), ALU.mult).then_inc(s["prod"], 1)
        dve.wait_ge(s["prod"], 4 * i + m + 1)
        dve.tensor_tensor(h, h, c.x(4 * i + m), ALU.add).then_inc(s["free"][m], 1)
    with c.pair(NL) as xp:
        linear(c, args, (c.x, xp), KT, KT, NL, scalar, vector, extra=("sig", "prod"))
    c.X, c.H = c.H, c.X


A3 = {}
_at = 0
for _name, _n in (("Q", 8 * NL), ("K", 2 * (NL + P)), ("VT", 2 * NL), ("V", 5 * 256), ("HIGH", 0), ("COS", NL), ("SIN", NL), ("SWAP", P), ("MASK", 4 * 2 * WIN),
                  ("S", 2 * 4 * 2 * WIN), ("PT", 2 * 4 * 2 * WIN), ("ST", 64), ("T", 4 * NL)):
    A3[_name] = _at
    _at += _n
A3["END"] = _at


def positions(c, args):
    o = A3
    T = o["T"]
    two_pi = 2 * np.pi
    c1 = 6.28125
    c2 = float(np.float32(np.floor((two_pi - c1) * 2 ** 21) / 2 ** 21))
    c3 = float(two_pi - c1 - c2)
    magic = float(1.5 * 2 ** 23)
    with phase(c, "dma", "own", "sin") as (s, block):
        @block.sync
        def _(sp):
            load(sp, s["dma"], (c.a(o["SWAP"], P), const(args, "swap32")), (c.a(o["MASK"], 1024), const(args, "window")),
                 (c.a(T, NL).bitcast(I32), args["positions"]))

        @block.vector
        def _(dve):
            link = Chain(dve, s["own"])
            ang, k, t = (c.a(T + j * NL, NL) for j in (1, 2, 3))
            dve.wait_ge(s["dma"], 48)
            link(dve.tensor_copy(ang, c.a(T, NL).bitcast(I32)))
            link(dve.tensor_scalar(ang, ang, c.vec("inv_freq"), None, ALU.mult))
            link(dve.tensor_scalar(k, ang, 1.0 / two_pi, magic, ALU.mult, ALU.add))
            link(dve.tensor_scalar(k, k, magic, None, ALU.subtract))
            for part in (c1, c2, c3):
                link(dve.scalar_tensor_tensor(ang, k, -part, ang, ALU.mult, ALU.add))
            link(dve.tensor_scalar(ang, ang, 3.141592, -3.141592, ALU.min, ALU.max))
            link(dve.scalar_tensor_tensor(t, ang, -1.0, ang, ALU.mult, ALU.min))
            link(dve.tensor_scalar(t, t, float(np.pi / 2), None, ALU.add))
            dve.wait_ge(s["sin"], 2)
            link(dve.tensor_scalar(c.a(o["SIN"], NL), c.a(o["SIN"], NL), c.vec("sign"), None, ALU.mult))
            for g in range(2):
                link(dve.memset(c.a(o["K"] + g * (NL + P), P), 0.0))
            link(dve.memset(c.a(o["V"], 256), 0.0))

        @block.scalar
        def _(act):
            act.wait_ge(s["own"], 10)
            act.activation(c.a(o["SIN"], NL), c.a(T + NL, NL), ACT.Sin).then_inc(s["sin"], 1)
            act.activation(c.a(o["COS"], NL), c.a(T + 3 * NL, NL), ACT.Sin).then_inc(s["sin"], 1)


def project_c(c, args):
    place = place_c

    def scalar(act, i, m, acc, s):
        act.activation(c.a(place(4 * i + m), NL), acc, ACT.Identity, bias=c.vec("b_qkv", 4 * i + m)).then_inc(s["free"][m], 1)
    with c.pair(NL) as xp:
        linear(c, args, (c.h, xp), KT, 12, NL, scalar, peel=3)


def place_c(j):
    o = A3
    return o["Q"] + j * NL if j < 8 else o["K"] + (j - 8) * (NL + P) + P if j < 10 else o["VT"] + (j - 10) * NL


def finish_c(c):
    o, place = A3, place_c
    values_by_token(c, lambda h: o["VT"] + h * NL, 2, lambda t: o["V"] + (t + 1) * 256)

    with phase(c, "swapped", "sined", "own", "done") as (s, block):
        @block.tensor
        def _(pe):
            for j in range(10):
                if j >= 8:
                    pe.wait_ge(s["sined"], j - 7)
                pe.matmul(c.bank(j % 8), c.a(o["SWAP"], P), c.a(place(j), NL), start=True, stop=True).then_inc(s["swapped"], 1)

        @block.vector
        def _(dve):
            for j in range(10):
                x, t = c.a(place(j), NL), c.a(o["T"] + (j % 4) * NL, NL)
                dve.wait_ge(s["swapped"], j + 1)
                dve.tensor_tensor(t, c.bank(j % 8), c.a(o["SIN"], NL), ALU.mult).then_inc(s["sined"], 1)
                dve.tensor_tensor(x, x, c.a(o["COS"], NL), ALU.mult).then_inc(s["own"], 1)
                dve.wait_ge(s["sined"], j + 1)
                dve.wait_ge(s["own"], j + 1)
                dve.tensor_tensor(x, x, t, ALU.add).then_inc(s["done"], 1)


def attention2(c):
    o = A3
    scale = float(HD2 ** -0.5)
    NK = 4 * 2 * WIN
    S, PT, ST = o["S"], o["PT"], o["ST"]
    col = lambda r, a: ST + 4 * (2 * r + a % 2)
    MAX, NEG, SUM, SINK, REC = range(5)
    sink_of = [h for g in range(2) for j in range(4) for h in (8 * g + j, 8 * g + 4 + j)]
    with phase(c, "scores", "masked", "neg", "sink", "probs", "normed", "turned", "pt_a", "pt_v", "o", "o_out", "own") as (s, block):

        @block.tensor
        def _(pe):
            def score(a):
                t, r = a // 2, 64 * (a % 2)
                if a >= 2:
                    pe.wait_ge(s["masked"], a - 1)
                for j in range(4):
                    mm = pe.matmul(c.PS[:, (a % 2) * 1024 + j * 256:(a % 2) * 1024 + j * 256 + 256],
                                   c.a(o["Q"] + t * NL + j * P, P, r, r + 64),
                                   c.a(o["K"] + (t // 4) * (NL + P) + j * P, 2 * WIN, r, r + 64), start=True, stop=True)
                mm.then_inc(s["scores"], 1)

            def turn(a):
                pe.wait_ge(s["normed"], a + 1)
                if a:
                    pe.wait_ge(s["pt_a"], a)
                    pe.wait_ge(s["pt_v"], a)
                for j in range(8):
                    mm = pe.transpose(c.PS[:, 2048 + j * P:2048 + j * P + P], c.a(S + (a % 2) * NK + j * P, P), c.ID[:])
                mm.then_inc(s["turned"], 1)

            def values(a):
                t, r = a // 2, 64 * (a % 2)
                pe.wait_ge(s["pt_a"], a + 1)
                pe.wait_ge(s["pt_v"], a + 1)
                if a >= 2:
                    pe.wait_ge(s["o_out"], a - 1)
                kv = 2 * (t // 4) + a % 2
                for j in range(4):
                    for z in range(2):
                        mm = pe.matmul(c.bank(6 + a % 2, P, j * P, r, r + 64), c.a(o["V"] + (j + z) * 256 + kv * 64, 64),
                                       c.a(PT + (a % 2) * NK + (2 * j + z) * P, P), start=(z == 0), stop=(z == 1))
                mm.then_inc(s["o"], 1)

            for a in range(NQH + 2):
                if a < NQH:
                    score(a)
                if 1 <= a <= NQH:
                    turn(a - 1)
                if a >= 2:
                    values(a - 2)

        @block.scalar
        def _(act):
            for a in range(NQH + 3):
                if a < NQH:
                    act.wait_ge(s["neg"], a + 1)
                    act.activation(c.a(col(SINK, a), 4), c.a(col(NEG, a), 4), ACT.Exp, bias=c.vec("sink", sink_of[a])).then_inc(s["sink"], 1)
                    for j in range(4):
                        x = c.a(S + (a % 2) * NK + j * 256, 256)
                        ins = act.activation(x, x, ACT.Exp, bias=c.a(col(NEG, a) + j, 1), accum_out=c.a(col(SUM, a) + j, 1))
                        ins.then_inc(s["probs"], 1)
                if 1 <= a <= NQH:
                    act.wait_ge(s["turned"], a)
                    if a >= 3:
                        act.wait_ge(s["o"], a - 2)
                    act.activation(c.a(PT + ((a - 1) % 2) * NK, 512), c.bank(4), ACT.Copy).then_inc(s["pt_a"], 1)
                if a >= 3:
                    b = a - 3
                    r = 64 * (b % 2)
                    act.wait_ge(s["o"], b + 1)
                    x = c.H[r:r + 64, (b // 2) * W:(b // 2) * W + NL]
                    act.activation(x, c.bank(6 + b % 2, p0=r, p1=r + 64), ACT.Copy).then_inc(s["o_out"], 1)

        @block.vector
        def _(dve):
            link = Chain(dve, s["own"])
            for a in range(NQH + 1):
                if a < NQH:
                    x = c.a(S + (a % 2) * NK, NK)
                    dve.wait_ge(s["scores"], a + 1)
                    if a >= 2:
                        dve.wait_ge(s["turned"], a - 1)
                    dve.scalar_tensor_tensor(x, c.PS[:, (a % 2) * 1024:(a % 2) * 1024 + NK], scale, c.a(o["MASK"], NK),
                                             ALU.mult, ALU.add).then_inc(s["masked"], 1)
                    dve.wait_ge(s["masked"], a + 1)
                    m = c.a(col(MAX, a), 4)
                    link(dve.tensor_reduce(m, x.rearrange("p (j k) -> p j k", j=4), AX, ALU.max))
                    dve.tensor_scalar(c.a(col(NEG, a), 4), m, c.vec("sink", sink_of[a]), -1.0, ALU.max, ALU.mult).then_inc(s["neg"], 1)
                if a:
                    dve.wait_ge(s["turned"], a)
                    if a >= 3:
                        dve.wait_ge(s["o"], a - 2)
                    dve.tensor_copy(c.a(PT + ((a - 1) % 2) * NK + 512, 512), c.bank(5)).then_inc(s["pt_v"], 1)
                if a < NQH:
                    dve.wait_ge(s["probs"], 4 * a + 4)
                    dve.wait_ge(s["sink"], a + 1)
                    den, rec = c.a(col(SUM, a), 4), c.a(col(REC, a), 4)
                    link(dve.tensor_tensor(den, den, c.a(col(SINK, a), 4), ALU.add))
                    link(dve.reciprocal(rec, den))
                    for j in range(4):
                        x = c.a(S + (a % 2) * NK + j * 256, 256)
                        ins = dve.tensor_scalar(x, x, c.a(col(REC, a) + j, 1), None, ALU.mult)
                    ins.then_inc(s["normed"], 1)


def block2(c, args):
    o = A2
    tile = lambda name, h: c.a(o[name] + h * NL, NL)
    heads_of = range(NH2)
    border = o["U"]
    plain_norm(c, "gain00")
    with c.low_room(border):
        with c.high_room(o["END"] - border):
            gate_rows(c, args)
            gate_columns(c)
        project_a(c, args)
        with c.high_room(o["END"] - border):
            unit_norms(c, [tile("Q", h) for h in heads_of] + [tile("K", h) for h in heads_of],
                       [(float(P), float(P) * EPS)] * NH2 + [(1.0, EPS)] * NH2)
            delta_inner(c, args)
            delta_scan(c)
            unit_norms(c, [tile("OA", h) for h in heads_of], [(1.0 / P, EPS)] * NH2, gain=lambda h: c.vec("norm_a"),
                       times=[tile("Z", h) for h in heads_of])
        project_b(c, args)
        with c.high_room(o["END"] - border):
            mlstm_inner(c)
            mlstm_scan(c)
            unit_norms(c, [tile("OB", h) for h in heads_of], [(1.0 / P, EPS)] * NH2, gain=lambda h: c.vec("norm_b", h),
                       times=[tile("Z", h) for h in heads_of])
        with c.pair(NL) as xp:
            after(c, args, (lambda k, lo, n: c.a(o["OA"] + k * NL + lo, n), xp), "gain01")
    ffn2(c, args, 0)
    gated_embedding(c, args, 0)
    plain_norm(c, "gain10")
    o = A3
    with c.low_room(o["HIGH"]):
        project_c(c, args)
        with c.high_room(o["END"] - o["HIGH"]):
            positions(c, args)
            finish_c(c)
            attention2(c)
    with c.pair(NL) as xp, c.room(KT * NL) as y:
        after(c, args, (c.h, xp), "gain11", dst=lambda k, lo, n: y[:, k * NL + lo:k * NL + lo + n], bias="b_o")
    ffn2(c, args, 1)
    gated_embedding(c, args, 1)


def block1(c, args):
    for l in range(DEPTH):
        n = W if l == 0 else NL
        pr = A1["PROJ"]
        cq = lambda k, lo, m: c.a(pr + (2 + k) * W + lo, m)
        ckv = lambda k, lo, m: c.a(pr + 5 * W + lo, m)
        modulated_norm(c, l, f"g_mix{l}", 0, W)
        with c.low_room(7 * W):
            in_proj(c, args, l)
            with c.high_room(A1["END"] - 7 * W):
                load_mixer(c, args, l)
                norm(c, cq, cq, 3, QRANK, n, lambda k, q: c.vec(f"g_q{l}", k))
                norm(c, ckv, ckv, 1, KVRANK, W, lambda k, q: c.vec(f"g_kv{l}"))
                fourier(c, args, l)
                key_rope(c)
                for g in range(3):
                    heads_qk(c, l, g)
                    attention1(c, l, g)
        with c.pair(n) as xp:
            linear(c, args, (c.h, xp), KT, KT, n, vector=residual(c, l, 2, n))
        modulated_norm(c, l, f"g_ffn{l}", 3, n)
        ffn1(c, args, l, n)
    plain_norm(c, "g_final")
    c.X, c.H = c.H, c.X


def store(c, args, name):
    with phase(c, "out") as (s, block):
        @block.sync
        def _(sp):
            sp.dma_start(args[name].rearrange("p (k n) -> p k n", k=KT),
                         c.X[:].rearrange("p (k n) -> p k n", k=KT)[:, :, 0:NL]).then_inc(s["out"], 16)
            sp.wait_ge(s["out"], 16)


def build(nc, args, total_units):
    with ExitStack() as stack:
        c = Core(nc, stack, total_units)
        start(c, args)
        ada(c, args)
        block1(c, args)
        block2(c, args)
        store(c, args, "out_dram")


def lay_out(x, c, ctx, c_ctx, w_ada, b_ada, g_mix, w_in, w_fourier, b_fourier, g_q_a, w_q_b, g_kv_a, w_kv_b, w_out,
            g_ffn, w_up, w_dw, b_dw, w_down, g_final, p_2, positions_2, norm_gains_2, w_in_ab_2, conv_a_2, a_log_2,
            dt_bias_2, norm_a_2, i_bias_b_2, f_bias_b_2, norm_b_2, w_out_ab_2, w_qkv_c_2, b_qkv_c_2, sinks_c_2, w_o_c_2,
            b_o_c_2, w_up_2, w_down_2, w_ple_2, w_ple_gate_2):
    x, ctx = np.asarray(x), np.asarray(ctx)
    x_in = np.concatenate([x[0], ctx[0]], 0).T
    vecs = np.zeros((P, NV), np.float32)

    def put(name, v):
        v = np.asarray(v)
        if v.ndim == 1:
            v = v.reshape(-1, P).T
        vecs[:v.shape[0], COL[name]:COL[name] + v.shape[1]] = v

    cc = np.stack([np.asarray(c)[0], np.asarray(c_ctx)], 1)
    put("c", tiles(cc))
    for l in range(DEPTH):
        for name, v in (("g_mix", g_mix), ("g_ffn", g_ffn), ("b_ada", b_ada), ("b_four", b_fourier), ("g_q", g_q_a),
                        ("g_kv", g_kv_a), ("b_dw", b_dw)):
            put(f"{name}{l}", np.asarray(v)[l])
        for k in range(3):
            put(f"dw{k}_{l}", np.asarray(w_dw)[l, k])
    put("g_final", g_final)
    for l in range(2):
        for i in range(4):
            put(f"gain{l}{i}", np.asarray(norm_gains_2)[l, i])
    for k in range(4):
        put(f"conv{k}", np.asarray(conv_a_2)[0, k])
    put("norm_a", np.asarray(norm_a_2)[0])
    put("norm_b", np.asarray(norm_b_2)[0].reshape(-1))
    heads = [h for g in range(2) for j in range(4) for h in (8 * g + j, 8 * g + 4 + j)]
    q_cols = [(h * HD2, h * HD2 + HD2) for h in heads]
    bq = np.asarray(b_qkv_c_2)[0]
    put("b_qkv", np.concatenate([bq[a:b] for a, b in q_cols] + [bq[1024:1536]]))
    put("b_o", np.asarray(b_o_c_2)[0])
    put("sink", np.broadcast_to(np.asarray(sinks_c_2)[0], (P, NQH)))
    put("inv_freq", np.tile(INV32, 4))
    put("sign", np.where(np.arange(P) % 64 < 32, np.float32(-1), np.float32(1)))
    put("rowb", np.stack([np.asarray(v)[0] for v in (a_log_2, dt_bias_2, i_bias_b_2, f_bias_b_2)], 1))

    w_ada, w_in, w_out, w_up, w_down = (np.asarray(v) for v in (w_ada, w_in, w_out, w_up, w_down))
    ada_units = w_ada.reshape(DEPTH, KT, P, NMOD * D // UN, UN).transpose(0, 3, 1, 2, 4).reshape(-1, P, UN)
    stream = []
    for l in range(DEPTH):
        stream += [units(w_in[l]), np.zeros((1, P, UB * P), np.float32), units(w_out[l])]
        for p, m in ffn_parts(FT1):
            stream += [units(w_up[l], [(o + j * P, o + j * P + P) for j in range(p, p + m) for o in (0, DFF)]),
                       units(w_down[l, p * P:(p + m) * P])]

    def ffn2_units(l):
        up, down = np.asarray(w_up_2)[l], np.asarray(w_down_2)[l]
        return [x for p, m in ffn_parts(32) for x in (units(up[:, p * P:(p + m) * P]), units(down[p * P:(p + m) * P]))]

    wab = np.asarray(w_in_ab_2)[0]
    A0, B0 = 0, 2056
    stream += [units(wab, [(0, 1536), (A0 + 1544, A0 + 2056)]),
               units(wab, [(B0, B0 + 1024), (B0 + 1544, B0 + 2056), (B0 + 1024, B0 + 1536)]), units(np.asarray(w_out_ab_2)[0]),
               *ffn2_units(0), units(np.asarray(w_ple_gate_2)[0])]
    w_o = np.asarray(w_o_c_2)[0]
    stream += [units(np.asarray(w_qkv_c_2)[0], q_cols + [(1024, 1536)]),
               units(np.concatenate([w_o[a:b] for a, b in q_cols], 0)),
               *ffn2_units(1), units(np.asarray(w_ple_gate_2)[1])]
    stream = np.concatenate(stream, 0)
    assert len(stream) == sum(n for _, n in stages())

    wq = np.asarray(w_q_b).reshape(DEPTH, QRANK, NHEAD, 96)
    wq = np.concatenate([wq[..., :64].reshape(DEPTH, QRANK, -1), wq[..., 64:].reshape(DEPTH, QRANK, -1)], -1)
    wkv = np.asarray(w_kv_b).reshape(DEPTH, KVRANK, NHEAD, 128)
    wkv = np.concatenate([wkv[..., :64].reshape(DEPTH, KVRANK, -1), wkv[..., 64:].reshape(DEPTH, KVRANK, -1)], -1)
    gates = np.zeros((D, P), np.float32)
    for i, o in enumerate((A0 + 1536, A0 + 1540, B0 + 1536, B0 + 1540)):
        gates[:, 32 * i:32 * i + 4] = wab[:, o:o + 4]
    return {
        "x_in": tiles(x_in), "vecs": vecs, "stream": stream, "consts": CONST,
        "wq": np.stack([tiles(wq[l]) for l in range(DEPTH)]), "wkv": wkv,
        "wf": np.stack([tiles(np.asarray(w_fourier)[l]) for l in range(DEPTH)]),
        "gates": tiles(gates), "w_ada": ada_units,
        "wple": np.stack([tiles(np.asarray(w_ple_2)[l]) for l in range(2)]),
        "ple": np.stack([tiles(np.asarray(p_2)[l, 0].T) for l in range(2)]),
        "positions": np.ascontiguousarray(np.broadcast_to(np.asarray(positions_2), (P, NL))),
    }


def kernel(**inputs):
    import concourse.bacc as bacc
    from concourse.bass_utils import run_bass_kernel_spmd

    arrays = {f"in_{k}": np.ascontiguousarray(v) for k, v in lay_out(**inputs).items()}
    nc = bacc.Bacc("TRN2", target_bir_lowering=False, num_devices=1)
    args = {k[3:]: nc.dram_tensor(k, a.shape, mybir.dt.from_np(a.dtype), kind="ExternalInput").ap()
            for k, a in arrays.items()}
    args["out_dram"] = nc.dram_tensor("out_dram", (P, KT * NL), F32, kind="ExternalOutput").ap()
    build(nc, args, len(arrays["in_stream"]))
    r = run_bass_kernel_spmd(nc, [arrays], core_ids=[0])
    out = r.results[0]["out_dram"]
    return out.reshape(P, KT, NL).transpose(2, 1, 0).reshape(1, NL, D)
```
